# Optimizing a Trainium2 kernel written in Bass

```python
import math
import jax, jax.numpy as jnp
from jax import lax
import numpy as np

D_MODEL = 1024
BATCH = 1
SEQ = 256
DEPTH = 2

D_MIX = D_MODEL
D_CONV = D_MIX // 4
D_POOL = D_MIX // 4
D_ATTN = D_MIX // 2
N_HEADS = 4
HEAD_DIM = D_ATTN // (2 * N_HEADS)
V_DIM = 2 * HEAD_DIM
CONV_WIDTH = 31
POOL_WINDOWS = (2, 4, 8, 16)
N_POOL_GROUPS = len(POOL_WINDOWS)
POOL_GROUP_DIM = D_POOL // N_POOL_GROUPS
D_FF = 256 * ((8 * D_MODEL // 3 + 255) // 256)
D_IN = 2 * D_CONV + D_POOL + 3 * D_ATTN
Q_BLOCK = 128
NORM_EPS = 1e-6


def rms_norm(x, g):
    xf = x.astype(jnp.float32)
    y = xf * lax.rsqrt(jnp.mean(xf * xf, axis=-1, keepdims=True) + NORM_EPS)
    return (y * g.astype(jnp.float32)).astype(x.dtype)

def layer_norm(x, g, b):
    xf = x.astype(jnp.float32)
    mu = jnp.mean(xf, axis=-1, keepdims=True)
    xc = xf - mu
    y = xc * lax.rsqrt(jnp.mean(xc * xc, axis=-1, keepdims=True) + NORM_EPS)
    return (y * g.astype(jnp.float32) + b.astype(jnp.float32)).astype(x.dtype)

def swiglu_ffn(h, w_gate, w_up, w_down):
    return (jax.nn.silu(h @ w_gate) * (h @ w_up)) @ w_down

def conformer_conv(u, w_dw, b_dw, ln_g, ln_b):
    a, gate = jnp.split(u, 2, axis=-1)
    z = a * jax.nn.sigmoid(gate)
    z = lax.conv_general_dilated(
        z, w_dw[:, None, :], window_strides=(1,),
        padding=((CONV_WIDTH // 2, CONV_WIDTH // 2),),
        dimension_numbers=("NWC", "WIO", "NWC"),
        feature_group_count=D_CONV) + b_dw
    return jax.nn.silu(layer_norm(z, ln_g, ln_b))

def multiscale_pool(u, w_grp, scale):
    B_, S_, _ = u.shape
    uf = u.astype(jnp.float32)
    cs = jnp.concatenate([jnp.zeros((B_, 1, D_POOL), jnp.float32), jnp.cumsum(uf, axis=1)], axis=1)
    t = jnp.arange(S_, dtype=jnp.int32)
    outs = []
    for g, w in enumerate(POOL_WINDOWS):
        sl = slice(g * POOL_GROUP_DIM, (g + 1) * POOL_GROUP_DIM)
        lo = jnp.clip(t - w // 2, 0, S_)
        hi = jnp.clip(t + w // 2, 0, S_)
        csg = cs[..., sl]
        win_sum = jnp.take(csg, hi, axis=1) - jnp.take(csg, lo, axis=1)
        cnt = (hi - lo).astype(jnp.float32)[None, :, None]
        outs.append(win_sum / cnt - uf[..., sl])
    d = jnp.stack(outs, axis=2)
    y = jnp.einsum("bsgc,gcd->bsgd", d, w_grp.astype(jnp.float32)).reshape(B_, S_, D_POOL)
    return (y * scale.astype(jnp.float32)).astype(u.dtype)

def diff_attention(q, k, v, lam, slopes):
    B_, S_ = q.shape[0], q.shape[1]
    n_blk = S_ // Q_BLOCK
    q_blocks = jnp.moveaxis(q.reshape(B_, n_blk, Q_BLOCK, N_HEADS, 2, HEAD_DIM), 1, 0)
    k_pos = jnp.arange(S_, dtype=jnp.int32)

    def block(args):
        q_blk, blk = args
        q_pos = blk * Q_BLOCK + jnp.arange(Q_BLOCK, dtype=jnp.int32)
        dist = jnp.abs(q_pos[:, None] - k_pos[None, :]).astype(jnp.float32)
        s = jnp.einsum("bqhcd,bkhcd->bhcqk", q_blk, k, preferred_element_type=jnp.float32)
        s = s - slopes[None, :, None, None, None] * dist
        p = jax.nn.softmax(s, axis=-1)
        a = p[:, :, 0] - lam * p[:, :, 1]
        return jnp.einsum("bhqk,bkhe->bqhe", a.astype(v.dtype), v)

    o = lax.map(block, (q_blocks, jnp.arange(n_blk, dtype=jnp.int32)))
    return jnp.moveaxis(o, 0, 1).reshape(B_, S_, N_HEADS, V_DIM)

def first_inputs(seed: int = 0) -> dict:
    key = jax.random.key(seed)
    ks = iter(jax.random.split(key, 32))

    def nrm(shape, scale):
        return jax.random.normal(next(ks), shape, jnp.float32) * scale

    def gain(shape):
        return 1.0 + 0.02 * jax.random.normal(next(ks), shape, jnp.float32)

    L = DEPTH
    return {
        "x": nrm((BATCH, SEQ, D_MODEL), 1.0),
        "ffn1_norm": gain((L, D_MODEL)),
        "ffn1_w_gate": nrm((L, D_MODEL, D_FF), D_MODEL ** -0.5),
        "ffn1_w_up": nrm((L, D_MODEL, D_FF), D_MODEL ** -0.5),
        "ffn1_w_down": nrm((L, D_FF, D_MODEL), D_FF ** -0.5),
        "mix_norm": gain((L, D_MODEL)),
        "w_in": nrm((L, D_MODEL, D_IN), D_MODEL ** -0.5),
        "conv_dw": nrm((L, CONV_WIDTH, D_CONV), CONV_WIDTH ** -0.5),
        "conv_dw_bias": nrm((L, D_CONV), 0.02),
        "conv_ln_gain": gain((L, D_CONV)),
        "conv_ln_bias": nrm((L, D_CONV), 0.02),
        "pool_w": nrm((L, N_POOL_GROUPS, POOL_GROUP_DIM, POOL_GROUP_DIM), POOL_GROUP_DIM ** -0.5),
        "pool_scale": 1.0 + 0.1 * jax.random.normal(next(ks), (L, D_POOL), jnp.float32),
        "q_norm": gain((L, HEAD_DIM)),
        "k_norm": gain((L, HEAD_DIM)),
        "lambda_q1": nrm((L, HEAD_DIM), 0.1),
        "lambda_k1": nrm((L, HEAD_DIM), 0.1),
        "lambda_q2": nrm((L, HEAD_DIM), 0.1),
        "lambda_k2": nrm((L, HEAD_DIM), 0.1),
        "attn_subln": gain((L, V_DIM)),
        "w_out": nrm((L, D_MIX, D_MODEL), D_MIX ** -0.5),
        "ffn2_norm": gain((L, D_MODEL)),
        "ffn2_w_gate": nrm((L, D_MODEL, D_FF), D_MODEL ** -0.5),
        "ffn2_w_up": nrm((L, D_MODEL, D_FF), D_MODEL ** -0.5),
        "ffn2_w_down": nrm((L, D_FF, D_MODEL), D_FF ** -0.5),
        "post_norm": gain((L, D_MODEL)),
    }

def first_block(x, ffn1_norm, ffn1_w_gate, ffn1_w_up, ffn1_w_down, mix_norm, w_in,
              conv_dw, conv_dw_bias, conv_ln_gain, conv_ln_bias, pool_w, pool_scale,
              q_norm, k_norm, lambda_q1, lambda_k1, lambda_q2, lambda_k2, attn_subln,
              w_out, ffn2_norm, ffn2_w_gate, ffn2_w_up, ffn2_w_down, post_norm):
    B_, S_ = x.shape[0], x.shape[1]
    slopes = jnp.exp2(-8.0 * jnp.arange(1, N_HEADS + 1, dtype=jnp.float32) / N_HEADS)
    for l in range(DEPTH):
        lambda_init = 0.8 - 0.6 * math.exp(-0.3 * l)
        x = x + 0.5 * swiglu_ffn(rms_norm(x, ffn1_norm[l]), ffn1_w_gate[l], ffn1_w_up[l], ffn1_w_down[l])
        h = rms_norm(x, mix_norm[l])
        u = h @ w_in[l]
        u_conv = u[..., :2 * D_CONV]
        u_pool = u[..., 2 * D_CONV:2 * D_CONV + D_POOL]
        q, k, v = jnp.split(u[..., 2 * D_CONV + D_POOL:], 3, axis=-1)
        y_conv = conformer_conv(u_conv, conv_dw[l], conv_dw_bias[l], conv_ln_gain[l], conv_ln_bias[l])
        y_pool = multiscale_pool(u_pool, pool_w[l], pool_scale[l])
        q = rms_norm(q.reshape(B_, S_, N_HEADS, 2, HEAD_DIM), q_norm[l]) * (HEAD_DIM ** -0.5)
        k = rms_norm(k.reshape(B_, S_, N_HEADS, 2, HEAD_DIM), k_norm[l])
        v = v.reshape(B_, S_, N_HEADS, V_DIM)
        lam = (jnp.exp(jnp.sum(lambda_q1[l].astype(jnp.float32) * lambda_k1[l].astype(jnp.float32)))
               - jnp.exp(jnp.sum(lambda_q2[l].astype(jnp.float32) * lambda_k2[l].astype(jnp.float32)))
               + lambda_init)
        o = diff_attention(q, k, v, lam, slopes)
        y_attn = (rms_norm(o, attn_subln[l]) * (1.0 - lambda_init)).reshape(B_, S_, D_ATTN)
        y = jnp.concatenate([y_conv, y_pool, y_attn.astype(y_conv.dtype)], axis=-1) @ w_out[l]
        x = x + y
        x = x + 0.5 * swiglu_ffn(rms_norm(x, ffn2_norm[l]), ffn2_w_gate[l], ffn2_w_up[l], ffn2_w_down[l])
        x = rms_norm(x, post_norm[l])
    return x


CHUNK = 64
N_MIXERS = 2
N_A_LAYERS = (DEPTH + 1) // 2
N_B_LAYERS = DEPTH // 2
N_VRES = max(N_B_LAYERS - 1, 0)
PLE_DIM = 256
D_FF_2 = 2816
RMS_EPS = 1e-6
GMLP_BLOCK = 128
GMLP_WIDTH = 2 * D_MODEL
GMLP_GROUPS = 8
GMLP_GROUP_DIM = GMLP_WIDTH // GMLP_GROUPS
LN_EPS = 1e-5
RWKV_HEAD_DIM = 64
RWKV_HEADS = D_MODEL // RWKV_HEAD_DIM
DECAY_LORA = 64
AAA_LORA = 64
MV_LORA = 32
GATE_LORA = 160
GN_EPS = 64e-5


def rms_norm_2(x, g):
    xf = x.astype(jnp.float32)
    y = xf * lax.rsqrt(jnp.mean(xf * xf, axis=-1, keepdims=True) + RMS_EPS)
    return (y * g.astype(jnp.float32)).astype(x.dtype)

def swiglu(x, w13, w2):
    gate, up = jnp.split(x @ w13, 2, axis=-1)
    return (jax.nn.silu(gate) * up) @ w2

def gmlp_mixer(h, w_in, b_in, v_gain, w_s, b_s, w_out):
    B, S, _ = h.shape
    z = jax.nn.gelu(h @ w_in + b_in)
    u, v = jnp.split(z, 2, axis=-1)
    vf = v.astype(jnp.float32)
    mean = jnp.mean(vf, axis=-1, keepdims=True)
    var = jnp.mean(jnp.square(vf - mean), axis=-1, keepdims=True)
    v = ((vf - mean) * lax.rsqrt(var + LN_EPS) * v_gain.astype(jnp.float32)).astype(h.dtype)
    nb = S // GMLP_BLOCK
    v = v.reshape(B, nb, GMLP_BLOCK, GMLP_GROUPS, GMLP_GROUP_DIM)
    u = u.reshape(B, nb, GMLP_BLOCK, GMLP_GROUPS, GMLP_GROUP_DIM)
    cidx = jnp.arange(GMLP_BLOCK) // CHUNK
    mask = cidx[None, :] <= cidx[:, None]
    ws = jnp.where(mask[None], w_s, jnp.zeros_like(w_s))
    s = jnp.einsum('gij,bcjgd->bcigd', ws, v) + b_s.T[None, None, :, :, None]
    y = (u * s).reshape(B, S, GMLP_WIDTH)
    return y @ w_out

def wkv7_scan(r, w, k, v, a, b):
    B, S, H, N = r.shape

    def step(state, inp):
        r_t, w_t, k_t, v_t, a_t, b_t = inp
        sa = jnp.einsum('bhij,bhj->bhi', state, a_t)
        state = (state * w_t[:, :, None, :] + sa[..., None] * b_t[:, :, None, :]
                 + v_t[..., None] * k_t[:, :, None, :])
        y_t = jnp.einsum('bhij,bhj->bhi', state, r_t)
        return state, y_t

    xs = tuple(jnp.moveaxis(t, 1, 0) for t in (r, w, k, v, a, b))
    state0 = jnp.zeros((B, H, N, N), jnp.float32)
    _, ys = lax.scan(step, state0, xs)
    return jnp.moveaxis(ys, 0, 1)

def rwkv7_mixer(h, v_first, vres, mu, w_in, w0, w1, w2, a0, a1, a2, g1, g2,
                k_k, k_a, r_k, lnx, w_out):
    B, S, D = h.shape
    H, N = RWKV_HEADS, RWKV_HEAD_DIM
    f32 = jnp.float32
    dx = jnp.pad(h, ((0, 0), (1, 0), (0, 0)))[:, :-1] - h
    x_rkv = h[:, :, None, :] + dx[:, :, None, :] * mu[:3]
    rkv = jnp.einsum('bsnd,nde->bsne', x_rkv, w_in)
    r, k, v = rkv[:, :, 0], rkv[:, :, 1], rkv[:, :, 2]
    xw = h + dx * mu[3]
    xa = h + dx * mu[4]
    xg = h + dx * mu[5]
    zw = (w0 + jnp.tanh(xw @ w1) @ w2).astype(f32)
    decay = jnp.exp(-jnp.exp(-jax.nn.softplus(-zw) - 0.5))
    a = jax.nn.sigmoid(a0 + (xa @ a1) @ a2)
    g = jax.nn.sigmoid(xg @ g1) @ g2

    def heads(t):
        return t.reshape(B, S, H, N).astype(f32)

    kk = heads(k * k_k)
    kk = kk / jnp.maximum(jnp.sqrt(jnp.sum(kk * kk, axis=-1, keepdims=True)), 1e-12)
    k = k * (1.0 + (a - 1.0) * k_a)
    if vres is None:
        v_first = v
    else:
        v0, v1, v2 = vres
        xv = h + dx * mu[2]
        v = v + (v_first - v) * jax.nn.sigmoid(v0 + (xv @ v1) @ v2)
    rh, kh, vh, ah = heads(r), heads(k), heads(v), heads(a)
    y = wkv7_scan(rh, heads(decay), kh, vh, -kk, kk * ah)
    mean = jnp.mean(y, axis=-1, keepdims=True)
    var = jnp.mean(jnp.square(y - mean), axis=-1, keepdims=True)
    yn = ((y - mean) * lax.rsqrt(var + GN_EPS)).reshape(B, S, D)
    yn = yn * lnx[0].astype(f32) + lnx[1].astype(f32)
    bonus = (jnp.sum(rh * kh * r_k.astype(f32), axis=-1, keepdims=True) * vh).reshape(B, S, D)
    out = ((yn + bonus).astype(h.dtype) * g) @ w_out
    return out, v_first

def second_inputs(seed: int = 0) -> dict:
    key = jax.random.key(seed)
    ks = iter(jax.random.split(key, 40))
    f32 = jnp.float32

    def nrm(shape, scale):
        return jax.random.normal(next(ks), shape, f32) * scale

    def gain(shape):
        return 1.0 + nrm(shape, 0.05)

    D, E2, E = D_MODEL, 2 * GMLP_WIDTH, GMLP_WIDTH
    NA, NB = N_A_LAYERS, N_B_LAYERS
    return {
        "x": nrm((BATCH, SEQ, D), 1.0),
        "p": nrm((DEPTH, BATCH, SEQ, PLE_DIM), 1.0),
        "norm_g": gain((DEPTH, 8, D)),
        "ffn_w13": nrm((DEPTH, 2, D, 2 * D_FF_2), D ** -0.5),
        "ffn_w2": nrm((DEPTH, 2, D_FF_2, D), D_FF_2 ** -0.5),
        "ple_w_gate": nrm((DEPTH, D, D), D ** -0.5),
        "ple_w_proj": nrm((DEPTH, PLE_DIM, D), PLE_DIM ** -0.5),
        "a_w_in": nrm((NA, D, E2), D ** -0.5),
        "a_b_in": nrm((NA, E2), 0.02),
        "a_v_gain": gain((NA, E)),
        "a_w_s": nrm((NA, GMLP_GROUPS, GMLP_BLOCK, GMLP_BLOCK), GMLP_BLOCK ** -0.5),
        "a_b_s": gain((NA, GMLP_GROUPS, GMLP_BLOCK)),
        "a_w_out": nrm((NA, E, D), E ** -0.5),
        "b_mu": jax.random.uniform(next(ks), (NB, 6, D), f32),
        "b_w_in": nrm((NB, 3, D, D), D ** -0.5),
        "b_w0": nrm((NB, D), 0.5),
        "b_w1": nrm((NB, D, DECAY_LORA), D ** -0.5),
        "b_w2": nrm((NB, DECAY_LORA, D), DECAY_LORA ** -0.5),
        "b_a0": nrm((NB, D), 0.1),
        "b_a1": nrm((NB, D, AAA_LORA), D ** -0.5),
        "b_a2": nrm((NB, AAA_LORA, D), AAA_LORA ** -0.5),
        "b_g1": nrm((NB, D, GATE_LORA), D ** -0.5),
        "b_g2": nrm((NB, GATE_LORA, D), GATE_LORA ** -0.5),
        "b_k_k": 0.85 + nrm((NB, D), 0.05),
        "b_k_a": gain((NB, D)),
        "b_r_k": nrm((NB, RWKV_HEADS, RWKV_HEAD_DIM), 0.1),
        "b_lnx": jnp.stack([gain((NB, D)), nrm((NB, D), 0.02)], axis=1),
        "b_w_out": nrm((NB, D, D), D ** -0.5),
        "b_v0": nrm((N_VRES, D), 0.1),
        "b_v1": nrm((N_VRES, D, MV_LORA), D ** -0.5),
        "b_v2": nrm((N_VRES, MV_LORA, D), MV_LORA ** -0.5),
    }

def second_block(x, p, norm_g, ffn_w13, ffn_w2, ple_w_gate, ple_w_proj,
              a_w_in, a_b_in, a_v_gain, a_w_s, a_b_s, a_w_out,
              b_mu, b_w_in, b_w0, b_w1, b_w2, b_a0, b_a1, b_a2, b_g1, b_g2,
              b_k_k, b_k_a, b_r_k, b_lnx, b_w_out, b_v0, b_v1, b_v2):
    h = x
    v_first = None
    for i in range(DEPTH):
        g = norm_g[i]
        h = h + 0.5 * rms_norm_2(swiglu(rms_norm_2(h, g[0]), ffn_w13[i, 0], ffn_w2[i, 0]), g[1])
        hn = rms_norm_2(h, g[2])
        j = i // N_MIXERS
        if i % N_MIXERS == 0:
            m = gmlp_mixer(hn, a_w_in[j], a_b_in[j], a_v_gain[j], a_w_s[j], a_b_s[j], a_w_out[j])
        else:
            vres = None if v_first is None else (b_v0[j - 1], b_v1[j - 1], b_v2[j - 1])
            m, v_first = rwkv7_mixer(hn, v_first, vres, b_mu[j], b_w_in[j], b_w0[j], b_w1[j],
                                     b_w2[j], b_a0[j], b_a1[j], b_a2[j], b_g1[j], b_g2[j],
                                     b_k_k[j], b_k_a[j], b_r_k[j], b_lnx[j], b_w_out[j])
        h = h + rms_norm_2(m, g[3])
        h = h + 0.5 * rms_norm_2(swiglu(rms_norm_2(h, g[4]), ffn_w13[i, 1], ffn_w2[i, 1]), g[5])
        gate = jax.nn.sigmoid(rms_norm_2(h, g[6]) @ ple_w_gate[i])
        h = h + rms_norm_2(gate * (p[i] @ ple_w_proj[i]), g[7])
    return h


def setup_inputs(seed=0):
    out = dict(first_inputs(seed))
    for name, value in second_inputs(seed + 1).items():
        if name != "x":
            out[name + "_2"] = value
    return out


def reference(
    x, ffn1_norm, ffn1_w_gate, ffn1_w_up, ffn1_w_down, mix_norm, w_in, conv_dw, conv_dw_bias,
    conv_ln_gain, conv_ln_bias, pool_w, pool_scale, q_norm, k_norm, lambda_q1, lambda_k1,
    lambda_q2, lambda_k2, attn_subln, w_out, ffn2_norm, ffn2_w_gate, ffn2_w_up, ffn2_w_down,
    post_norm, p_2, norm_g_2, ffn_w13_2, ffn_w2_2, ple_w_gate_2, ple_w_proj_2, a_w_in_2,
    a_b_in_2, a_v_gain_2, a_w_s_2, a_b_s_2, a_w_out_2, b_mu_2, b_w_in_2, b_w0_2, b_w1_2, b_w2_2,
    b_a0_2, b_a1_2, b_a2_2, b_g1_2, b_g2_2, b_k_k_2, b_k_a_2, b_r_k_2, b_lnx_2, b_w_out_2,
    b_v0_2, b_v1_2, b_v2_2,
):
    x = first_block(
        x, ffn1_norm, ffn1_w_gate, ffn1_w_up, ffn1_w_down, mix_norm, w_in, conv_dw,
        conv_dw_bias, conv_ln_gain, conv_ln_bias, pool_w, pool_scale, q_norm, k_norm, lambda_q1,
        lambda_k1, lambda_q2, lambda_k2, attn_subln, w_out, ffn2_norm, ffn2_w_gate, ffn2_w_up,
        ffn2_w_down, post_norm,
    )
    return second_block(
        x, p_2, norm_g_2, ffn_w13_2, ffn_w2_2, ple_w_gate_2, ple_w_proj_2, a_w_in_2, a_b_in_2,
        a_v_gain_2, a_w_s_2, a_b_s_2, a_w_out_2, b_mu_2, b_w_in_2, b_w0_2, b_w1_2, b_w2_2,
        b_a0_2, b_a1_2, b_a2_2, b_g1_2, b_g2_2, b_k_k_2, b_k_a_2, b_r_k_2, b_lnx_2, b_w_out_2,
        b_v0_2, b_v1_2, b_v2_2,
    )


_drawn_inputs = setup_inputs


def setup_inputs(seed=0):
    import zlib

    import numpy as np

    out = dict(_drawn_inputs(seed))
    spreads = {}
    factors = {'conv_ln_gain': 4.245,
     'conv_ln_bias': 4.334,
     'q_norm': 3.16,
     'k_norm': 3.124,
     'attn_subln': 3.007,
     'ffn2_norm': 3.793,
     'a_b_in_2': 2.797,
     'b_k_k_2': 64.0,
     'b_a0_2': 2.678}
    for name, (base, spread) in spreads.items():
        noise = np.random.default_rng([zlib.crc32(name.encode()), seed]).standard_normal(out[name].shape)
        drawn = base * np.exp(spread * noise) if base else spread * noise
        out[name] = __import__('jax').numpy.asarray(drawn.astype(out[name].dtype))
    for name, factor in factors.items():
        out[name] = (out[name] * factor).astype(out[name].dtype)
    return out
```

```python
import math
from contextlib import ExitStack

import concourse.bass as bass
from concourse import mybir

F32 = mybir.dt.float32
F32R = mybir.dt.float32r
ALU = mybir.AluOpType
ACT = mybir.ActivationFunctionType
AX = mybir.AxisListType

P = 128
D = 1024
S = 256
NT = S // P
KT = D // P
DFF = 2816
FT = DFF // P
UNIT = 1024
RING = 6
AHEAD = RING - 1
HALF = 512
EPS = 1e-6
DEPTH = 2
HEADS = 16
HD = 64
AH = 4


def stage_units():
    out = []
    for _ in range(DEPTH):
        out += [3 * FT, 18, 8, 3 * FT]
    out += [3 * FT, 32, 16, 3 * FT, 10]
    out += [3 * FT, 24, 8, 3 * FT, 10]
    return out


class Signal:

    def __init__(self, sem):
        self.sem = sem
        self.base = 0

    def at(self, k):
        return self.base + k


class Order:

    def __init__(self, sem):
        self.sem = sem
        self.count = 0

    def link(self, eng, ins):
        self.count += 1
        ins.then_inc(self.sem, 1)
        eng.wait_ge(self.sem, self.count)


class Core:

    def __init__(self, nc, ctx, dram):
        self.nc = nc
        self.dram = dram

        def sb(name, shape, dt=F32):
            return ctx.enter_context(nc.sbuf_tensor(name, shape, dt))

        def sem(name):
            return Signal(ctx.enter_context(nc.semaphore(name)))

        self.x = sb("x", [P, NT, D])
        self.act_hi = sb("act_hi", [P, 2 * KT, S], F32R)
        self.act_lo = sb("act_lo", [P, 2 * KT, S], F32R)
        self.raw = sb("raw", [P, RING, UNIT])
        self.w_hi = sb("w_hi", [P, RING, UNIT], F32R)
        self.w_lo = sb("w_lo", [P, RING, UNIT], F32R)
        self.g_hi = sb("g_hi", [P, 2, S], F32R)
        self.g_lo = sb("g_lo", [P, 2, S], F32R)
        self.work = sb("work", [P, 20, UNIT])
        self.silu = self.work[:, 0, 0:2 * S].rearrange("p (i s) -> p i s", i=2)
        self.gated = self.work[:, 1, 0:2 * S].rearrange("p (i s) -> p i s", i=2)
        self.small = sb("small", [P, 512])
        self.cols = sb("cols", [P, dram["cols"].shape[1]])
        self.const = sb("const", [P, dram["const"].shape[1]])
        self.ident = self.const[:, 0:P]
        self.bank = [ctx.enter_context(nc.psum_tensor(f"bank{i}", [P, HALF], F32)) for i in range(8)]

        self.landed = [sem(f"landed{i}") for i in range(RING)]
        self.hi_ready = sem("hi_ready")
        self.lo_ready = sem("lo_ready")
        self.unit_used = sem("unit_used")
        self.silu_ready = sem("silu_ready")
        self.gated_ready = sem("gated_ready")
        self.prod_made = sem("prod_made")
        self.prod_hi = sem("prod_hi")
        self.const_in = sem("const_in")
        self.row_in = sem("row_in")
        self.stored = sem("stored")
        self.pe_to_act = sem("pe_to_act")
        self.pe_to_dve = sem("pe_to_dve")
        self.act_to_pe = sem("act_to_pe")
        self.act_to_dve = sem("act_to_dve")
        self.act_to_pool = sem("act_to_pool")
        self.dve_to_pe = sem("dve_to_pe")
        self.dve_to_act = sem("dve_to_act")
        self.dve_to_pool = sem("dve_to_pool")
        self.pool_to_dve = sem("pool_to_dve")
        self.pool_to_act = sem("pool_to_act")
        self.dve_order = Order(ctx.enter_context(nc.semaphore("dve_order")))
        self.act_order = Order(ctx.enter_context(nc.semaphore("act_order")))
        self.pool_order = Order(ctx.enter_context(nc.semaphore("pool_order")))
        self.first_unit = 0
        self.units = sum(stage_units())
        self.new_signal = sem
        self.repeated = {}

    def signals(self, prefix, counts):
        for name in counts:
            if prefix + name not in self.repeated:
                self.repeated[prefix + name] = self.new_signal(prefix + name)
        return {name: self.repeated[prefix + name] for name in counts}

    def load_unit(self, sp, n):
        if n >= self.units:
            return
        if n >= RING:
            sp.wait_ge(self.lo_ready.sem, n - RING + 1)
        sp.dma_start(self.raw[:, n % RING, :], self.dram["w"][n, :, :]).then_inc(
            self.landed[n % RING].sem, 16)

    def split_hi(self, act, n):
        if n >= self.units:
            return
        act.wait_ge(self.landed[n % RING].sem, 16 * (n // RING + 1))
        if n >= RING:
            act.wait_ge(self.unit_used.sem, n - RING + 1)
        self.nc.scalar.activation(self.w_hi[:, n % RING, :], self.raw[:, n % RING, :],
                                  ACT.Copy).then_inc(self.hi_ready.sem, 1)

    def split_lo(self, dve, n):
        if n >= self.units:
            return
        dve.wait_ge(self.hi_ready.sem, n + 1)
        self.nc.vector.tensor_tensor(self.w_lo[:, n % RING, :], self.raw[:, n % RING, :],
                                     self.w_hi[:, n % RING, :].bitcast(F32),
                                     ALU.subtract).then_inc(self.lo_ready.sem, 1)

    def stream_stage_loads(self, sp, count):
        for n in range(self.first_unit + RING, self.first_unit + count + RING):
            self.load_unit(sp, n)

    def end_stage(self, count, *signals):
        self.first_unit += count
        for signal, k in signals:
            signal.base += k

    def end_signals(self, signals, counts):
        for name, k in counts.items():
            signals[name].base += k


def three_products(nc, out, stat_hi, stat_lo, mov_hi, mov_lo, first, last):
    nc.tensor.matmul(out, stat_hi, mov_hi, start=first, stop=False)
    nc.tensor.matmul(out, stat_hi, mov_lo, start=False, stop=False)
    return nc.tensor.matmul(out, stat_lo, mov_hi, start=False, stop=last)


def start_stage(c):
    nc = c.nc
    with nc.Block() as block:
        @block.sync
        def _(sp):
            sp.dma_start(c.const[:, :], c.dram["const"][:, :]).then_inc(c.const_in.sem, 16)
            sp.dma_start(c.cols[:, :], c.dram["cols"][:, :]).then_inc(c.const_in.sem, 16)
            sp.dma_start(c.x[:, :, :], c.dram["x"].rearrange("(t p) d -> p t d", p=P)).then_inc(
                c.const_in.sem, 16)
            for n in range(RING):
                c.load_unit(sp, n)
            sp.wait_ge(c.const_in.sem, 48)

        @block.scalar
        def _(act):
            for n in range(AHEAD):
                c.split_hi(act, n)

        @block.vector
        def _(dve):
            for n in range(AHEAD):
                c.split_lo(dve, n)


def norm_stage(c, gain_col, hi=None, plain=None):
    nc = c.nc
    ms = c.small[:, 0:NT]
    rstd = c.small[:, NT:2 * NT]
    half = c.const[:, 128:128 + NT]
    xn = c.work[:, 0:NT, :]
    junk = c.work[:, NT:2 * NT, :]
    with nc.Block() as block:
        @block.scalar
        def _(act):
            for t in range(NT):
                last = nc.scalar.activation(junk[:, t, :], c.x[:, t, :], ACT.Square,
                                            scale=float(D) ** -0.5, accum_out=ms[:, t:t + 1])
            last.then_inc(c.act_to_pool.sem, 1)
            for k in range(KT):
                act.wait_ge(c.pe_to_act.sem, c.pe_to_act.at(k + 1))
                nc.scalar.activation(c.act_hi[:, k, :], c.bank[k][:, 0:S], ACT.Copy,
                                     scale=c.cols[:, gain_col + k:gain_col + k + 1]).then_inc(
                                         c.act_to_dve.sem, 1)

        @block.gpsimd
        def _(pool):
            pool.wait_ge(c.act_to_pool.sem, c.act_to_pool.at(1))
            c.pool_order.link(pool, nc.gpsimd.tensor_scalar(ms, ms, EPS, None, ALU.add))
            nc.gpsimd.tensor_tensor(rstd, ms, half, ALU.pow).then_inc(c.pool_to_dve.sem, 1)

        @block.vector
        def _(dve):
            dve.wait_ge(c.pool_to_dve.sem, c.pool_to_dve.at(1))
            for t in range(NT):
                nc.vector.tensor_scalar(xn[:, t, :], c.x[:, t, :], rstd[:, t:t + 1], None,
                                        ALU.mult).then_inc(c.dve_to_pe.sem, 1)
            for k in range(KT):
                dve.wait_ge(c.act_to_dve.sem, c.act_to_dve.at(k + 1))
                nc.vector.scalar_tensor_tensor(
                    c.act_lo[:, k, :], c.bank[k][:, 0:S], c.cols[:, gain_col + k:gain_col + k + 1],
                    c.act_hi[:, k, :].bitcast(F32), ALU.mult, ALU.subtract)

        @block.tensor
        def _(pe):
            pe.wait_ge(c.dve_to_pe.sem, c.dve_to_pe.at(NT))
            for k in range(KT):
                for t in range(NT):
                    last = nc.tensor.transpose(c.bank[k][:, t * P:(t + 1) * P],
                                               xn[:, t, k * P:(k + 1) * P], c.ident)
                last.then_inc(c.pe_to_act.sem, 1)
    c.end_stage(0, (c.pe_to_act, KT), (c.act_to_pool, 1), (c.act_to_dve, KT), (c.pool_to_dve, 1),
                (c.dve_to_pe, NT))


def ffn_stage(c):
    nc = c.nc
    first = c.first_unit
    down = [c.bank[i] for i in range(4)]
    gate = [c.bank[4], c.bank[5]]
    up = [c.bank[6], c.bank[7]]

    def slot(m):
        return (first + m) % RING

    count = 3 * FT
    LOOPS = (FT - 2) // 2

    with nc.Block() as block:
        @block.sync
        def _(sp):
            with sp.Fori(0, count // RING) as i:
                for j in range(RING):
                    n = first + RING + j
                    sp.wait_ge(c.lo_ready.sem, i * RING + (n - RING + 1))
                    sp.dma_start(c.raw[:, n % RING, :], c.dram["w"][bass.ds(i * RING + n, 1), :, :]
                                 .rearrange("o p n -> p (o n)")).then_inc(
                                     c.landed[n % RING].sem, 16)

        def hi_units(act, i, ms):
            for m in ms:
                n = first + m
                if i is None:
                    c.split_hi(act, n)
                    continue
                act.wait_ge(c.landed[n % RING].sem, i * 16 + 16 * (n // RING + 1))
                act.wait_ge(c.unit_used.sem, i * RING + (n - RING + 1))
                nc.scalar.activation(c.w_hi[:, n % RING, :], c.raw[:, n % RING, :],
                                     ACT.Copy).then_inc(c.hi_ready.sem, 1)

        def lo_units(dve, i, ms):
            for m in ms:
                n = first + m
                if i is None:
                    c.split_lo(dve, n)
                    continue
                dve.wait_ge(c.hi_ready.sem, i * RING + n + 1)
                nc.vector.tensor_tensor(c.w_lo[:, n % RING, :], c.raw[:, n % RING, :],
                                        c.w_hi[:, n % RING, :].bitcast(F32),
                                        ALU.subtract).then_inc(c.lo_ready.sem, 1)

        def step_value(signal, i, k):
            return signal.at(k) if i is None else i * 2 + signal.at(k)

        def gate_unit(t):
            return 3 * t - 1 if t else 0

        def used_value(i, m):
            return first + m + 1 if i is None else i * RING + (first + m + 1)

        def act_step(act, i, t):
            if t >= 1:
                hi_units(act, i, (3 * t + 2, 3 * t + 3, 3 * t + 4))
            act.wait_ge(c.unit_used.sem, used_value(i, gate_unit(t)))
            if t >= 2:
                act.wait_ge(c.gated_ready.sem, step_value(c.gated_ready, i, t - 1))
            nc.scalar.activation(c.silu[:, t % 2, :], gate[t % 2][:, 0:S], ACT.Silu).then_inc(
                c.silu_ready.sem, 1)

        @block.scalar
        def _(act):
            act_step(act, None, 0)
            act_step(act, None, 1)
            with act.Fori(0, LOOPS) as i:
                act_step(act, i, 2)
                act_step(act, i, 3)
            hi_units(act, None, (3 * FT + 2, 3 * FT + 3, 3 * FT + 4))

        def dve_step(dve, i, t):
            if t >= 1:
                lo_units(dve, i, (3 * t + 2, 3 * t + 3, 3 * t + 4))
            dve.wait_ge(c.unit_used.sem, used_value(i, gate_unit(t) + 1))
            dve.wait_ge(c.silu_ready.sem, step_value(c.silu_ready, i, t + 1))
            p = t % 2
            nc.vector.tensor_tensor(c.gated[:, p, :], c.silu[:, p, :], up[p][:, 0:S],
                                    ALU.mult).then_inc(c.prod_made.sem, 1)
            dve.wait_ge(c.prod_made.sem, step_value(c.prod_made, i, t + 1))
            if t >= 2:
                dve.wait_ge(c.unit_used.sem, used_value(i, 3 * (t - 2) + 4))
            nc.vector.tensor_copy(c.g_hi[:, p, :], c.gated[:, p, :]).then_inc(c.prod_hi.sem, 1)
            dve.wait_ge(c.prod_hi.sem, step_value(c.prod_hi, i, t + 1))
            nc.vector.tensor_tensor(c.g_lo[:, p, :], c.gated[:, p, :], c.g_hi[:, p, :].bitcast(F32),
                                    ALU.subtract).then_inc(c.gated_ready.sem, 1)

        @block.vector
        def _(dve):
            dve_step(dve, None, 0)
            dve_step(dve, None, 1)
            with dve.Fori(0, LOOPS) as i:
                dve_step(dve, i, 2)
                dve_step(dve, i, 3)
            lo_units(dve, None, (3 * FT + 2, 3 * FT + 3, 3 * FT + 4))

        def unit_there(pe, i, m):
            n = first + m
            pe.wait_ge(c.lo_ready.sem, n + 1 if i is None else i * RING + n + 1)

        def hidden(pe, i, m, out):
            s = slot(m)
            unit_there(pe, i, m)
            for k in range(KT):
                w = slice(k * P, (k + 1) * P)
                last = three_products(nc, out[:, 0:S], c.w_hi[:, s, w], c.w_lo[:, s, w],
                                      c.act_hi[:, k, :], c.act_lo[:, k, :], k == 0, k == KT - 1)
            last.then_inc(c.unit_used.sem, 1)

        def add_down(pe, i, f, m, begin=False, end=False):
            s = slot(m)
            unit_there(pe, i, m)
            pe.wait_ge(c.gated_ready.sem, step_value(c.gated_ready, i, f + 1))
            for t in range(NT):
                tok = slice(t * P, (t + 1) * P)
                for h in range(2):
                    w = slice(h * HALF, (h + 1) * HALF)
                    last = three_products(nc, down[2 * t + h][:, :], c.g_hi[:, f % 2, tok],
                                          c.g_lo[:, f % 2, tok], c.w_hi[:, s, w], c.w_lo[:, s, w],
                                          begin, end)
            last.then_inc(c.unit_used.sem, 1)

        def pe_step(pe, i, t):
            m = gate_unit(t)
            if t >= 2:
                pe.wait_ge(c.silu_ready.sem, step_value(c.silu_ready, i, t - 1))
            hidden(pe, i, m, gate[t % 2])
            if t >= 2:
                pe.wait_ge(c.prod_made.sem, step_value(c.prod_made, i, t - 1))
            hidden(pe, i, m + 1, up[t % 2])
            if t >= 1:
                add_down(pe, i, t - 1, m + 2, begin=t == 1)

        @block.tensor
        def _(pe):
            pe_step(pe, None, 0)
            pe_step(pe, None, 1)
            with pe.Fori(0, LOOPS) as i:
                pe_step(pe, i, 2)
                pe_step(pe, i, 3)
            add_down(pe, None, FT - 1, count - 1, end=True)
    c.end_stage(count, (c.silu_ready, FT), (c.gated_ready, FT), (c.prod_made, FT), (c.prod_hi, FT))


def finish_stage(c, scale, sources, row=None):
    nc = c.nc
    gain = c.work[:, 18, :]
    parts = c.small[:, 0:2 * NT]
    rstd = c.small[:, 2 * NT:3 * NT]
    half = c.const[:, 128:128 + NT]
    quads = [(t, h) for t in range(NT) for h in range(2)]

    def piece(unit, t, h):
        return c.work[:, unit + t, h * HALF:(h + 1) * HALF]

    def xs(t, h):
        return c.x[:, t, h * HALF:(h + 1) * HALF]

    with nc.Block() as block:
        if row is None:
            @block.vector
            def _(dve):
                for t, h in quads:
                    nc.vector.scalar_tensor_tensor(xs(t, h), sources(t, h), scale, xs(t, h),
                                                   ALU.mult, ALU.add)
        else:
            @block.sync
            def _(sp):
                sp.dma_start(gain, c.dram["rows"][row, :, :]).then_inc(c.row_in.sem, 16)

            @block.scalar
            def _(act):
                for q, (t, h) in enumerate(quads):
                    last = nc.scalar.activation(piece(16, t, h), sources(t, h), ACT.Square,
                                                scale=float(D) ** -0.5 / scale,
                                                accum_out=parts[:, q:q + 1])
                last.then_inc(c.act_to_dve.sem, 1)

            @block.vector
            def _(dve):
                dve.wait_ge(c.act_to_dve.sem, c.act_to_dve.at(1))
                nc.vector.scalar_tensor_tensor(rstd, parts[:, 0:2 * NT:2], EPS / scale ** 2,
                                               parts[:, 1:2 * NT:2], ALU.add, ALU.add).then_inc(
                                                   c.dve_to_pool.sem, 1)
                dve.wait_ge(c.pool_to_dve.sem, c.pool_to_dve.at(1))
                dve.wait_ge(c.row_in.sem, c.row_in.at(16))
                for t, h in quads:
                    last = nc.vector.scalar_tensor_tensor(
                        piece(14, t, h), sources(t, h), rstd[:, t:t + 1],
                        gain[:, h * HALF:(h + 1) * HALF], ALU.mult, ALU.mult)
                c.dve_order.link(dve, last)
                for t, h in quads:
                    nc.vector.tensor_tensor(xs(t, h), xs(t, h), piece(14, t, h), ALU.add)

            @block.gpsimd
            def _(pool):
                pool.wait_ge(c.dve_to_pool.sem, c.dve_to_pool.at(1))
                nc.gpsimd.tensor_tensor(rstd, rstd, half, ALU.pow).then_inc(c.pool_to_dve.sem, 1)
    if row is not None:
        c.end_stage(0, (c.row_in, 16), (c.act_to_dve, 1), (c.dve_to_pool, 1), (c.pool_to_dve, 1))


def store_stage(c, out):
    with c.nc.Block() as block:
        @block.sync
        def _(sp):
            sp.dma_start(out.rearrange("(t p) d -> p t d", p=P), c.x[:, :, :]).then_inc(
                c.stored.sem, 16)
            sp.wait_ge(c.stored.sem, 16)


def banks(c):
    return lambda t, h: c.bank[2 * t + h][:, :]


def product_b(c, pe, m, out):
    n = c.first_unit + m
    pe.wait_ge(c.lo_ready.sem, n + 1)
    for k in range(KT):
        w = slice(k * P, (k + 1) * P)
        last = three_products(c.nc, out[:, 0:S], c.w_hi[:, n % RING, w], c.w_lo[:, n % RING, w],
                              c.act_hi[:, k, :], c.act_lo[:, k, :], k == 0, k == KT - 1)
    last.then_inc(c.unit_used.sem, 1)


def product_a(c, pe, m, k, count, outs, tile0=0):
    n = c.first_unit + m
    pe.wait_ge(c.lo_ready.sem, n + 1)
    for t in range(NT):
        tok = slice(t * P, (t + 1) * P)
        for j in range(2):
            a = tile0 + 2 * k + j
            w = slice(j * HALF, (j + 1) * HALF)
            last = three_products(c.nc, outs[t][:, :], c.act_hi[:, a, tok], c.act_lo[:, a, tok],
                                  c.w_hi[:, n % RING, w], c.w_lo[:, n % RING, w],
                                  k == 0 and j == 0, k == count - 1 and j == 1)
    last.then_inc(c.unit_used.sem, 1)


def unit_done(c, eng, m):
    eng.wait_ge(c.unit_used.sem, c.first_unit + m + 1)


def project_stage(c, tiles, tile0):
    per = tiles // 2
    count = 2 * per
    with c.nc.Block() as block:
        @block.sync
        def _(sp):
            c.stream_stage_loads(sp, count)

        @block.scalar
        def _(act):
            for m in range(count):
                c.split_hi(act, c.first_unit + AHEAD + m)

        @block.vector
        def _(dve):
            for m in range(count):
                c.split_lo(dve, c.first_unit + AHEAD + m)

        @block.tensor
        def _(pe):
            for h in range(2):
                for k in range(per):
                    product_a(c, pe, h * per + k, k, per, [c.bank[h], c.bank[2 + h]], tile0)
    c.end_stage(count)


def ple_stage(c, i):
    nc = c.nc
    count = 10
    pt = c.work[:, 4, 0:2 * S].rearrange("p (k s) -> p k s", k=2)
    counts = {"p_in": 16, "p_hi": 1, "p_lo": 1, "gate": 4}
    s = c.signals("ple_", counts)
    with nc.Block() as block:
        @block.sync
        def _(sp):
            sp.dma_start(pt, c.dram["pt"][i, :, :, :]).then_inc(s["p_in"].sem, 16)
            c.stream_stage_loads(sp, count)

        @block.scalar
        def _(act):
            act.wait_ge(s["p_in"].sem, s["p_in"].at(16))
            nc.scalar.activation(c.act_hi[:, KT:KT + 2, :], pt, ACT.Copy).then_inc(s["p_hi"].sem, 1)
            for m in range(count + 1):
                if m < count:
                    c.split_hi(act, c.first_unit + AHEAD + m)
                if m in (4, 8):
                    h = m // 4 - 1
                    unit_done(c, act, m - 1)
                    for t in range(NT):
                        nc.scalar.activation(c.work[:, t, h * HALF:(h + 1) * HALF],
                                             c.bank[2 * t + h][:, :], ACT.Sigmoid).then_inc(s["gate"].sem, 1)

        @block.vector
        def _(dve):
            dve.wait_ge(s["p_hi"].sem, s["p_hi"].at(1))
            nc.vector.tensor_tensor(c.act_lo[:, KT:KT + 2, :], pt,
                                    c.act_hi[:, KT:KT + 2, :].bitcast(F32),
                                    ALU.subtract).then_inc(s["p_lo"].sem, 1)
            for m in range(count):
                c.split_lo(dve, c.first_unit + AHEAD + m)
            for h in range(2):
                unit_done(c, dve, 8 + h)
                dve.wait_ge(s["gate"].sem, s["gate"].at(2 * (h + 1)))
                for t in range(NT):
                    g = c.work[:, t, h * HALF:(h + 1) * HALF]
                    nc.vector.tensor_tensor(g, g, c.bank[4 + 2 * t + h][:, :], ALU.mult)

        @block.tensor
        def _(pe):
            for h in range(2):
                for k in range(4):
                    product_a(c, pe, h * 4 + k, k, 4, [c.bank[h], c.bank[2 + h]])
            pe.wait_ge(s["p_lo"].sem, s["p_lo"].at(1))
            for h in range(2):
                product_a(c, pe, 8 + h, 0, 1, [c.bank[4 + h], c.bank[6 + h]], KT)
    c.end_stage(count)
    c.end_signals(s, counts)


def gmlp_in_stage(c, rows, bias_col):
    nc = c.nc
    v = c.work[:, 0:4, :].rearrange("p (t a) n -> p t (a n)", t=NT)
    bias = c.work[:, 4:6, :].rearrange("p a n -> p (a n)")
    u = c.work[:, 6:10, :].rearrange("p a (b s) -> p (a b) s", s=S)
    stats = c.small[:, 0:48].rearrange("p (t q s) -> p t q s", t=NT, q=4)
    mv = c.small[:, 48:52].rearrange("p (t s) -> p t s", t=NT)
    ve = c.small[:, 52:54]
    rstd = c.small[:, 54:56]
    half = c.const[:, 128:130]
    b_in, v_biased, v_made, u_made, var_made, rstd_made = (
        c.new_signal("gmlp_" + n) for n in ("b_in", "v_biased", "v_made", "u_made", "var", "rstd"))
    count = 32
    UT = 16

    def chunk(t, n):
        return v[:, t, n * HALF:(n + 1) * HALF]

    with nc.Block() as block:
        @block.sync
        def _(sp):
            for a in range(2):
                sp.dma_start(c.work[:, 4 + a, :], c.dram["rows"][rows + a, :, :]).then_inc(b_in.sem, 16)
            c.stream_stage_loads(sp, count)

        @block.scalar
        def _(act):
            for m in range(count + 1):
                if m < count:
                    c.split_hi(act, c.first_unit + AHEAD + m)
                if m in (4, 8, 12, 16):
                    n = m // 4 - 1
                    act.wait_ge(v_biased.sem, n + 1)
                    for t in range(NT):
                        last = nc.scalar.activation(chunk(t, n), chunk(t, n), ACT.Gelu_apprx_tanh)
                    last.then_inc(v_made.sem, 1)
                if m > 16:
                    i = m - 17
                    unit_done(c, act, m - 1)
                    nc.scalar.activation(u[:, i, :], c.bank[4 + i % 4][:, 0:S], ACT.Gelu_apprx_tanh,
                                         bias=c.cols[:, bias_col + i:bias_col + i + 1]).then_inc(
                                             u_made.sem, 1)

        @block.vector
        def _(dve):
            dve.wait_ge(b_in.sem, 32)
            for m in range(count + 1):
                if m < count:
                    c.split_lo(dve, c.first_unit + AHEAD + m)
                if m in (4, 8, 12, 16):
                    n = m // 4 - 1
                    unit_done(c, dve, m - 1)
                    for t in range(NT):
                        last = nc.vector.tensor_tensor(chunk(t, n), c.bank[2 * t + n % 2][:, :],
                                                       bias[:, n * HALF:(n + 1) * HALF], ALU.add)
                    last.then_inc(v_biased.sem, 1)
                if m in (6, 10, 14, 18):
                    n = (m - 6) // 4
                    dve.wait_ge(v_made.sem, n + 1)
                    for t in range(NT):
                        last = nc.vector.bn_stats(stats[:, t, n, :], chunk(t, n))
                if m == 18:
                    c.dve_order.link(dve, last)
                    for t in range(NT):
                        last = nc.vector.bn_aggr(mv[:, t, :], stats[:, t, :, :])
                    c.dve_order.link(dve, last)
                    nc.vector.tensor_scalar(ve, mv[:, :, 1], 1e-5, None, ALU.add).then_inc(var_made.sem, 1)
                if m == 20:
                    dve.wait_ge(rstd_made.sem, 1)
                    for t in range(NT):
                        nc.vector.tensor_scalar(v[:, t, :], v[:, t, :], mv[:, t, 0:1], rstd[:, t:t + 1],
                                                ALU.subtract, ALU.mult)

        @block.gpsimd
        def _(pool):
            pool.wait_ge(var_made.sem, 1)
            nc.gpsimd.tensor_tensor(rstd, ve, half, ALU.pow).then_inc(rstd_made.sem, 1)

        @block.tensor
        def _(pe):
            for n in range(4):
                if n >= 2:
                    pe.wait_ge(v_biased.sem, n - 1)
                for k in range(4):
                    product_a(c, pe, 4 * n + k, k, 4, [c.bank[n % 2], c.bank[2 + n % 2]])
            for i in range(UT):
                if i >= 4:
                    pe.wait_ge(u_made.sem, i - 3)
                product_b(c, pe, 16 + i, c.bank[4 + i % 4])
    c.end_stage(count)


def gmlp_mix_stage(c, bs_row, gain_col):
    nc = c.nc
    UT = 16
    v = c.work[:, 0:4, :].rearrange("p (t a) n -> p t (a n)", t=NT)
    u = c.work[:, 6:10, :].rearrange("p a (b s) -> p (a b) s", s=S)
    ws = c.work[:, 10, :].rearrange("p (g i) -> p g i", g=8)
    bs = c.work[:, 11, :].rearrange("p (g i) -> p g i", g=8)
    mixed = c.work[:, 12:16, :].rearrange("p a (b s) -> p (a b) s", s=S)
    ws_in, bs_in, masked, product, scaled, y_made, y_hi = (
        c.new_signal("mix_" + n) for n in ("ws_in", "bs_in", "masked", "product", "scaled", "y", "y_hi"))
    with nc.Block() as block:
        @block.sync
        def _(sp):
            sp.dma_start(ws, c.dram["ws"][:, :, :]).then_inc(ws_in.sem, 16)
            sp.dma_start(c.work[:, 11, :], c.dram["rows"][bs_row, :, :]).then_inc(bs_in.sem, 16)

        @block.gpsimd
        def _(pool):
            pool.wait_ge(ws_in.sem, 16)
            nc.gpsimd.memset(ws[64:128, :, 0:64], 0.0).then_inc(masked.sem, 1)

        @block.tensor
        def _(pe):
            pe.wait_ge(masked.sem, 1)
            for q in range(UT):
                if q >= 8:
                    pe.wait_ge(scaled.sem, q - 7)
                for t in range(NT):
                    last = nc.tensor.matmul(c.bank[q % 8][:, t * P:(t + 1) * P],
                                            v[:, t, q * P:(q + 1) * P], ws[:, q // 2, :],
                                            start=True, stop=True)
                last.then_inc(product.sem, 1)

        @block.vector
        def _(dve):
            dve.wait_ge(bs_in.sem, 16)
            for q in range(UT + 2):
                if q < UT:
                    dve.wait_ge(product.sem, q + 1)
                    nc.vector.scalar_tensor_tensor(
                        mixed[:, q, :].rearrange("p (t i) -> p t i", t=NT),
                        c.bank[q % 8][:, 0:S].rearrange("p (t i) -> p t i", t=NT),
                        c.cols[:, gain_col + q:gain_col + q + 1],
                        bs[:, q // 2:q // 2 + 1, :].to_broadcast([P, NT, P]),
                        ALU.mult, ALU.add).then_inc(scaled.sem, 1)
                if 1 <= q <= UT:
                    dve.wait_ge(scaled.sem, q)
                    nc.vector.tensor_tensor(u[:, q - 1, :], u[:, q - 1, :], mixed[:, q - 1, :],
                                            ALU.mult).then_inc(y_made.sem, 1)
                if q >= 2:
                    dve.wait_ge(y_hi.sem, q - 1)
                    nc.vector.tensor_tensor(c.act_lo[:, q - 2, :], u[:, q - 2, :],
                                            c.act_hi[:, q - 2, :].bitcast(F32), ALU.subtract)

        @block.scalar
        def _(act):
            for q in range(UT):
                act.wait_ge(y_made.sem, q + 1)
                nc.scalar.activation(c.act_hi[:, q, :], u[:, q, :], ACT.Copy).then_inc(y_hi.sem, 1)
    c.end_stage(0)


CONV_W = 31
PAD = CONV_W // 2
POOL_PAD = 8
C_IDENT, C_HALF, C_RCNT, C_MEAN = 0, 128, 384, 896


def mixer_buffers(c):
    class Buffers:
        pass

    b = Buffers()
    b.q, b.k, b.v = (c.work[:, i, :].rearrange("p (t n) -> p t n", t=NT) for i in range(3))
    b.zpad = c.work[:, 3, 0:2 * (S + 2 * PAD)].rearrange("p (i s) -> p i s", i=2)
    b.sig = c.work[:, 4, 0:2 * S].rearrange("p (i s) -> p i s", i=2)
    b.conv = c.work[:, 4, 2 * S:4 * S].rearrange("p (i s) -> p i s", i=2)
    b.upad, b.sum2, b.sum4, b.sum8 = (
        c.work[:, i, 0:2 * (S + 2 * POOL_PAD)].rearrange("p (i s) -> p i s", i=2) for i in range(5, 9))
    b.diff = c.work[:, 9, 0:2 * S].rearrange("p (i s) -> p i s", i=2)
    b.poolw = c.work[:, 9, 2 * S:3 * S].rearrange("p (i d) -> p i d", i=2)
    return b


def mixer_in_stage(c, layer, conv_col, conv_bias_col):
    nc = c.nc
    b = mixer_buffers(c)
    count = 18
    counts = {"sig": 2, "z": 2, "conv_step": 2 * CONV_W, "pool": 2, "qkv": 3, "zeroed": 1,
              "zero_z": 1, "poolw": 32}
    s = c.signals("in_", counts)

    with nc.Block() as block:
        @block.sync
        def _(sp):
            sp.dma_start(b.poolw, c.dram["poolw"][layer, :, :, :]).then_inc(s["poolw"].sem, 16)
            sp.dma_start(c.work[:, 19, 0:2 * S], c.dram["dist"][:, :]).then_inc(s["poolw"].sem, 16)
            c.stream_stage_loads(sp, count)
            sp.wait_ge(s["poolw"].sem, s["poolw"].at(32))

        @block.scalar
        def _(act):
            for m in range(count + 1):
                if m < count:
                    c.split_hi(act, c.first_unit + AHEAD + m)
                if m in (2, 4):
                    i = m // 2 - 1
                    unit_done(c, act, m - 1)
                    nc.scalar.activation(b.sig[:, i, :], c.bank[m - 1][:, 0:S], ACT.Sigmoid).then_inc(s["sig"].sem, 1)
                if m in (5, 6):
                    i = m - 5
                    unit_done(c, act, m - 1)
                    act.wait_ge(s["zeroed"].sem, s["zeroed"].at(1))
                    nc.scalar.activation(b.upad[:, i, POOL_PAD:POOL_PAD + S], c.bank[m - 1][:, 0:S],
                                         ACT.Copy).then_inc(s["pool"].sem, 1)
                if m in (10, 14, 18):
                    i = (m - 10) // 4
                    unit_done(c, act, m - 1)
                    for t in range(NT):
                        last = nc.scalar.activation((b.q, b.k, b.v)[i][:, t, :],
                                                    c.bank[(6, 0, 2)[i] + t][:, :], ACT.Copy)
                    last.then_inc(s["qkv"].sem, 1)

        @block.vector
        def _(dve):
            nc.vector.memset(c.work[:, 3, 0:2 * (S + 2 * PAD)], 0.0).then_inc(s["zero_z"].sem, 1)
            steps = [(j, i) for j in range(CONV_W) for i in range(2)]
            done = 0
            for m in range(count):
                c.split_lo(dve, c.first_unit + AHEAD + m)
                if m in (2, 4):
                    i = m // 2 - 1
                    if i == 0:
                        dve.wait_ge(s["zero_z"].sem, s["zero_z"].at(1))
                    unit_done(c, dve, m - 2)
                    dve.wait_ge(s["sig"].sem, s["sig"].at(i + 1))
                    nc.vector.tensor_tensor(b.zpad[:, i, PAD:PAD + S], c.bank[m - 2][:, 0:S],
                                            b.sig[:, i, :], ALU.mult).then_inc(s["z"].sem, 1)
                if m >= 5:
                    for j, i in steps[5 * (m - 5):5 * (m - 4)]:
                        if done == 0:
                            dve.wait_ge(s["z"].sem, s["z"].at(2))
                        if done >= 2:
                            dve.wait_ge(s["conv_step"].sem, s["conv_step"].at(done - 1))
                        tap = c.cols[:, conv_col + 2 * j + i:conv_col + 2 * j + i + 1]
                        if j == 0:
                            ins = nc.vector.tensor_scalar(
                                b.conv[:, i, :], b.zpad[:, i, 0:S], tap,
                                c.cols[:, conv_bias_col + i:conv_bias_col + i + 1], ALU.mult, ALU.add)
                        else:
                            ins = nc.vector.scalar_tensor_tensor(
                                b.conv[:, i, :], b.zpad[:, i, j:j + S], tap, b.conv[:, i, :],
                                ALU.mult, ALU.add)
                        ins.then_inc(s["conv_step"].sem, 1)
                        done += 1
            assert done == 2 * CONV_W

        @block.gpsimd
        def _(pool):
            nc.gpsimd.memset(c.work[:, 5, 0:2 * (S + 2 * POOL_PAD)], 0.0).then_inc(s["zeroed"].sem, 1)
            pool.wait_ge(s["pool"].sem, s["pool"].at(2))
            order = c.pool_order
            for dst, src, lo, hi, shift in ((b.sum2, b.upad, 1, 272, (1, 0)), (b.sum4, b.sum2, 2, 270, (1, 1)),
                                            (b.sum8, b.sum4, 4, 268, (2, 2))):
                order.link(pool, nc.gpsimd.tensor_tensor(
                    dst[:, :, lo:hi], src[:, :, lo - shift[0]:hi - shift[0]],
                    src[:, :, lo + shift[1]:hi + shift[1]], ALU.add))
            w = slice(POOL_PAD, POOL_PAD + S)
            rcnt = c.const[:, C_RCNT:C_RCNT + 2 * S].rearrange("p (i s) -> p i s", i=2)
            for rows, i, src in ((slice(0, 64), 0, b.sum2), (slice(64, 128), 0, b.sum4),
                                 (slice(0, 64), 1, b.sum8)):
                nc.gpsimd.tensor_tensor(b.diff[rows, i, :], src[rows, i, w], rcnt[rows, i, :], ALU.mult)
            order.link(pool, nc.gpsimd.tensor_tensor(
                b.diff[64:128, 1, :], b.sum8[64:128, 1, POOL_PAD - 4:POOL_PAD - 4 + S],
                b.sum8[64:128, 1, POOL_PAD + 4:POOL_PAD + 4 + S], ALU.add))
            order.link(pool, nc.gpsimd.tensor_tensor(b.diff[64:128, 1, :], b.diff[64:128, 1, :],
                                                     rcnt[64:128, 1, :], ALU.mult))
            nc.gpsimd.tensor_tensor(b.diff, b.diff, b.upad[:, :, w], ALU.subtract)

        @block.tensor
        def _(pe):
            for m in range(6):
                product_b(c, pe, m, c.bank[m])
            for i in range(3):
                if i == 1:
                    pe.wait_ge(s["z"].sem, s["z"].at(1))
                if i == 2:
                    pe.wait_ge(s["z"].sem, s["z"].at(2))
                first = (6, 0, 2)[i]
                for k in range(4):
                    product_a(c, pe, 6 + 4 * i + k, k, 4, [c.bank[first], c.bank[first + 1]])
    c.end_stage(count)
    c.end_signals(s, counts)


def attention_stage(c, layer, qn_col, kn_col, sub_col, lam_col, pool_scale_col, ln_col, lambda_init):
    nc = c.nc
    b = mixer_buffers(c)
    counts = {"lam_sum": 1, "lam_exp": 1, "sq_sum": 1, "qk_rstd": 1, "qk_scaled": 2,
              "qkT": 8, "kT_made": 4, "qT_made": 4, "score": 8, "biased": 8,
              "maxed": 8, "probs": 8, "mixed": 4, "aT_bank": 4, "aT_made": 4,
              "out_bank": 1, "o_ms": 1, "o_rstd": 1, "o_scaled": 1, "oT": 4,
              "oT_hi": 4, "pool_bank": 1, "pool_hi": 3, "mean": 1,
              "centred": 2, "squared": 1, "var": 1, "var_eps": 1, "ln_rstd": 1,
              "normed": 1, "conv_y": 2, "conv_hi": 1, "sub_ready": 1}
    s = c.signals("attn_", counts)
    sq = c.work[:, 5:7, :]
    qT = c.work[:, 10, :].rearrange("p (h s) -> p h s", h=AH)
    kT = c.work[:, 11, :].rearrange("p (h s) -> p h s", h=AH)
    sc = c.work[:, 12:16, :].rearrange("p a (b n) -> p (a b) n", b=2)
    aT = c.work[:, 16:18, :].rearrange("p a (b n) -> p (a b) n", b=2)
    o = c.work[:, 18, :].rearrange("p (t n) -> p t n", t=NT)
    osq = c.work[:, 12, :].rearrange("p (t n) -> p t n", t=NT)
    ln = c.work[:, 7, :].rearrange("p (i s) -> p i s", i=4)
    ln2 = c.work[:, 8, :].rearrange("p (i s) -> p i s", i=4)
    dist = c.work[:, 19, 0:2 * S]
    meanw = c.const[:, C_MEAN:C_MEAN + P]
    sm = c.small
    qk_ms, qk_rstd = sm[:, 0:32], sm[:, 32:64]
    nmax, total, recip = sm[:, 64:80], sm[:, 80:96], sm[:, 96:112]
    lam2, lam_e, lam = sm[:, 112:114], sm[:, 114:116], sm[:, 116:117]
    o_ms, o_rstd = sm[:, 120:128], sm[:, 128:136]
    subg = sm[:, 136:137]
    lam_v = sm[:, 256:384]
    half = c.const[:, C_HALF:C_HALF + S]
    order = c.dve_order
    slopes = [2.0 ** (-8.0 * (h + 1) / AH) for h in range(AH)]

    with nc.Block() as block:
        @block.tensor
        def _(pe):
            for i in range(2):
                last = nc.tensor.matmul(c.bank[7][:, i * S:(i + 1) * S], b.poolw[:, i, :], b.diff[:, i, :],
                                        start=True, stop=True)
            last.then_inc(s["pool_bank"].sem, 1)
            for i in range(2):
                last = nc.tensor.matmul(c.bank[6][:, 0:S], meanw, b.conv[:, i, :], start=i == 0, stop=i == 1)
            last.then_inc(s["mean"].sem, 1)
            pe.wait_ge(s["qk_scaled"].sem, s["qk_scaled"].at(1))
            for h in range(AH):
                for t in range(NT):
                    last = nc.tensor.transpose(c.bank[h][:, t * P:(t + 1) * P],
                                               b.q[:, t, h * P:(h + 1) * P], c.ident)
                last.then_inc(s["qkT"].sem, 1)
            pe.wait_ge(s["qk_scaled"].sem, s["qk_scaled"].at(2))
            for h in range(AH):
                if h == 2:
                    pe.wait_ge(s["centred"].sem, s["centred"].at(2))
                if h == 3:
                    pe.wait_ge(s["pool_hi"].sem, s["pool_hi"].at(3))
                for t in range(NT):
                    last = nc.tensor.transpose(c.bank[4 + h][:, t * P:(t + 1) * P],
                                               b.k[:, t, h * P:(h + 1) * P], c.ident)
                last.then_inc(s["qkT"].sem, 1)
            pe.wait_ge(s["qT_made"].sem, s["qT_made"].at(AH))
            pe.wait_ge(s["kT_made"].sem, s["kT_made"].at(AH))
            for u in range(2 * AH):
                h, g = u // 2, u % 2
                rows = slice(g * HD, (g + 1) * HD)
                for t in range(NT):
                    last = nc.tensor.matmul(c.bank[u][:, t * S:(t + 1) * S], qT[rows, h, t * P:(t + 1) * P],
                                            kT[rows, h, :], start=True, stop=True)
                last.then_inc(s["score"].sem, 1)
            pe.wait_ge(s["biased"].sem, s["biased"].at(8))
            pe.wait_ge(s["squared"].sem, s["squared"].at(1))
            for i in range(2):
                last = nc.tensor.matmul(c.bank[7][:, 0:S], meanw, ln[:, 2 + i, :], start=i == 0, stop=i == 1)
            last.then_inc(s["var"].sem, 1)
            for h in range(AH):
                pe.wait_ge(s["mixed"].sem, s["mixed"].at(h + 1))
                for kt in range(NT):
                    for t in range(NT):
                        last = nc.tensor.transpose(c.bank[h][:, kt * S + t * P:kt * S + (t + 1) * P],
                                                   sc[:, 2 * h, t * S + kt * P:t * S + (kt + 1) * P], c.ident)
                last.then_inc(s["aT_bank"].sem, 1)
            for h in range(AH):
                pe.wait_ge(s["aT_made"].sem, s["aT_made"].at(h + 1))
                for t in range(NT):
                    for kt in range(NT):
                        last = nc.tensor.matmul(c.bank[4 + t][:, h * P:(h + 1) * P],
                                                aT[:, h, kt * S + t * P:kt * S + (t + 1) * P],
                                                b.v[:, kt, h * P:(h + 1) * P], start=kt == 0, stop=kt == 1)
            last.then_inc(s["out_bank"].sem, 1)
            pe.wait_ge(s["o_scaled"].sem, s["o_scaled"].at(1))
            for h in range(AH):
                for t in range(NT):
                    last = nc.tensor.transpose(c.bank[h][:, t * P:(t + 1) * P],
                                               o[:, t, h * P:(h + 1) * P], c.ident)
                last.then_inc(s["oT"].sem, 1)

        @block.scalar
        def _(act):
            act.wait_ge(s["pool_bank"].sem, s["pool_bank"].at(1))
            for i in range(2):
                nc.scalar.activation(c.act_hi[:, KT + 2 + i, :], c.bank[7][:, i * S:(i + 1) * S], ACT.Copy,
                                     scale=c.cols[:, pool_scale_col + i:pool_scale_col + i + 1]).then_inc(s["pool_hi"].sem, 1)
            act.wait_ge(s["lam_sum"].sem, s["lam_sum"].at(1))
            nc.scalar.activation(lam_e, lam2, ACT.Exp).then_inc(s["lam_exp"].sem, 1)
            act.wait_ge(s["centred"].sem, s["centred"].at(2))
            nc.scalar.activation(ln[:, 2:4, :], ln[:, 0:2, :], ACT.Square).then_inc(s["squared"].sem, 1)
            for h in range(AH):
                act.wait_ge(s["qkT"].sem, s["qkT"].at(AH + h + 1))
                nc.scalar.activation(kT[:, h, :], c.bank[4 + h][:, 0:S], ACT.Copy,
                                     scale=c.cols[:, kn_col:kn_col + 1]).then_inc(s["kT_made"].sem, 1)
            for u in range(2 * AH):
                act.wait_ge(s["maxed"].sem, s["maxed"].at(u + 1))
                for t in range(NT):
                    part = sc[:, u, t * S:(t + 1) * S]
                    last = nc.scalar.activation(part, part, ACT.Exp, bias=nmax[:, 2 * u + t:2 * u + t + 1],
                                                accum_out=total[:, 2 * u + t:2 * u + t + 1])
                last.then_inc(s["probs"].sem, 1)
            for h in range(AH):
                act.wait_ge(s["aT_bank"].sem, s["aT_bank"].at(h + 1))
                nc.scalar.activation(aT[:, h, :], c.bank[h][:, :], ACT.Copy).then_inc(s["aT_made"].sem, 1)
            act.wait_ge(s["var_eps"].sem, s["var_eps"].at(1))
            nc.scalar.activation(ln2[:, 0, :], ln2[:, 1, :], ACT.Sqrt).then_inc(s["ln_rstd"].sem, 1)
            act.wait_ge(s["normed"].sem, s["normed"].at(1))
            for i in range(2):
                nc.scalar.activation(ln2[:, 2 + i, :], ln[:, i, :], ACT.Silu,
                                     scale=c.cols[:, ln_col + i:ln_col + i + 1],
                                     bias=c.cols[:, ln_col + 2 + i:ln_col + 3 + i]).then_inc(s["conv_y"].sem, 1)
            act.wait_ge(s["conv_y"].sem, s["conv_y"].at(2))
            nc.scalar.activation(c.act_hi[:, KT:KT + 2, :], ln2[:, 2:4, :], ACT.Copy).then_inc(s["conv_hi"].sem, 1)
            act.wait_ge(s["sub_ready"].sem, s["sub_ready"].at(1))
            for h in range(AH):
                act.wait_ge(s["oT"].sem, s["oT"].at(h + 1))
                nc.scalar.activation(c.act_hi[:, KT + 4 + h, :], c.bank[h][:, 0:S], ACT.Copy,
                                     scale=subg).then_inc(s["oT_hi"].sem, 1)

        @block.gpsimd
        def _(pool):
            pool.wait_ge(s["sq_sum"].sem, s["sq_sum"].at(1))
            nc.gpsimd.tensor_tensor(qk_rstd, qk_ms, half[:, 0:32], ALU.pow).then_inc(s["qk_rstd"].sem, 1)
            pool.wait_ge(s["o_ms"].sem, s["o_ms"].at(1))
            nc.gpsimd.tensor_tensor(o_rstd, o_ms, half[:, 0:8], ALU.pow).then_inc(s["o_rstd"].sem, 1)

        @block.vector
        def _(dve):
            for i, x in enumerate((b.q, b.k)):
                last = nc.vector.tensor_tensor(sq[:, i, :], c.work[:, i, :], c.work[:, i, :], ALU.mult)
            order.link(dve, last)
            order.link(dve, nc.vector.tensor_reduce(
                qk_ms, sq.rearrange("p i (g n) -> p (i g) n", n=HD), AX.X, ALU.add))
            nc.vector.tensor_scalar(qk_ms, qk_ms, 1.0 / HD, EPS, ALU.mult, ALU.add).then_inc(s["sq_sum"].sem, 1)
            for i in range(2):
                last = nc.vector.tensor_tensor(
                    lam_v[:, i * HD:(i + 1) * HD], c.cols[:, lam_col + 2 * i * HD:lam_col + (2 * i + 1) * HD],
                    c.cols[:, lam_col + (2 * i + 1) * HD:lam_col + (2 * i + 2) * HD], ALU.mult)
            order.link(dve, last)
            nc.vector.tensor_reduce(lam2, lam_v.rearrange("p (i n) -> p i n", i=2), AX.X,
                                    ALU.add).then_inc(s["lam_sum"].sem, 1)
            nc.vector.tensor_scalar(subg, c.cols[:, sub_col:sub_col + 1], 1.0 - lambda_init, None,
                                    ALU.mult).then_inc(s["sub_ready"].sem, 1)
            dve.wait_ge(s["mean"].sem, s["mean"].at(1))
            for i in range(2):
                nc.vector.tensor_tensor(ln[:, i, :], b.conv[:, i, :], c.bank[6][:, 0:S],
                                        ALU.subtract).then_inc(s["centred"].sem, 1)
            dve.wait_ge(s["pool_hi"].sem, s["pool_hi"].at(2))
            for i in range(2):
                last = nc.vector.scalar_tensor_tensor(
                    c.act_lo[:, KT + 2 + i, :], c.bank[7][:, i * S:(i + 1) * S],
                    c.cols[:, pool_scale_col + i:pool_scale_col + i + 1],
                    c.act_hi[:, KT + 2 + i, :].bitcast(F32), ALU.mult, ALU.subtract)
            last.then_inc(s["pool_hi"].sem, 1)
            dve.wait_ge(s["qk_rstd"].sem, s["qk_rstd"].at(1))
            for i in range(2):
                nc.vector.tensor_tensor(
                    c.work[:, i, :].rearrange("p (g n) -> p g n", n=HD),
                    c.work[:, i, :].rearrange("p (g n) -> p g n", n=HD),
                    qk_rstd[:, 16 * i:16 * (i + 1)].unsqueeze(2).to_broadcast([P, 16, HD]),
                    ALU.mult).then_inc(s["qk_scaled"].sem, 1)
            dve.wait_ge(s["lam_exp"].sem, s["lam_exp"].at(1))
            order.link(dve, nc.vector.tensor_tensor(lam, lam_e[:, 0:1], lam_e[:, 1:2], ALU.subtract))
            order.link(dve, nc.vector.tensor_scalar(lam, lam, lambda_init, None, ALU.add))
            for h in range(AH):
                dve.wait_ge(s["qkT"].sem, s["qkT"].at(h + 1))
                nc.vector.tensor_scalar(qT[:, h, :], c.bank[h][:, 0:S], c.cols[:, qn_col:qn_col + 1],
                                        float(HD) ** -0.5, ALU.mult, ALU.mult).then_inc(s["qT_made"].sem, 1)
            for u in range(2 * AH):
                dve.wait_ge(s["score"].sem, s["score"].at(u + 1))
                nc.vector.scalar_tensor_tensor(sc[:, u, :], dist, -slopes[u // 2], c.bank[u][:, :],
                                               ALU.mult, ALU.add).then_inc(s["biased"].sem, 1)
                dve.wait_ge(s["biased"].sem, s["biased"].at(u + 1))
                nc.vector.tensor_reduce(nmax[:, 2 * u:2 * u + 2],
                                        sc[:, u, :].rearrange("p (t n) -> p t n", t=NT), AX.X, ALU.max,
                                        negate=True).then_inc(s["maxed"].sem, 1)
            dve.wait_ge(s["var"].sem, s["var"].at(1))
            nc.vector.tensor_scalar(ln2[:, 1, :], c.bank[7][:, 0:S], EPS, None, ALU.add).then_inc(s["var_eps"].sem, 1)
            for h in range(AH):
                dve.wait_ge(s["probs"].sem, s["probs"].at(2 * h + 2))
                r = slice(4 * h, 4 * h + 4)
                order.link(dve, nc.vector.reciprocal(recip[:, r], total[:, r]))
                order.link(dve, nc.vector.tensor_scalar(
                    recip[:, 4 * h + 2:4 * h + 4], recip[:, 4 * h + 2:4 * h + 4], lam, None, ALU.mult))
                for t in range(NT):
                    last = nc.vector.tensor_scalar(
                        sc[:, 2 * h + 1, t * S:(t + 1) * S], sc[:, 2 * h + 1, t * S:(t + 1) * S],
                        recip[:, 4 * h + 2 + t:4 * h + 3 + t], None, ALU.mult)
                order.link(dve, last)
                for t in range(NT):
                    last = nc.vector.scalar_tensor_tensor(
                        sc[:, 2 * h, t * S:(t + 1) * S], sc[:, 2 * h, t * S:(t + 1) * S],
                        recip[:, 4 * h + t:4 * h + 1 + t], sc[:, 2 * h + 1, t * S:(t + 1) * S],
                        ALU.mult, ALU.subtract)
                last.then_inc(s["mixed"].sem, 1)
            dve.wait_ge(s["ln_rstd"].sem, s["ln_rstd"].at(1))
            order.link(dve, nc.vector.reciprocal(ln2[:, 0, :], ln2[:, 0, :]))
            for i in range(2):
                last = nc.vector.tensor_tensor(ln[:, i, :], ln[:, i, :], ln2[:, 0, :], ALU.mult)
            last.then_inc(s["normed"].sem, 1)
            dve.wait_ge(s["out_bank"].sem, s["out_bank"].at(1))
            for t in range(NT):
                last = nc.vector.tensor_copy(o[:, t, :], c.bank[4 + t][:, :])
            order.link(dve, last)
            order.link(dve, nc.vector.tensor_tensor(osq, o, o, ALU.mult))
            order.link(dve, nc.vector.tensor_reduce(
                o_ms, c.work[:, 12, :].rearrange("p (g n) -> p g n", n=P), AX.X, ALU.add))
            nc.vector.tensor_scalar(o_ms, o_ms, 1.0 / P, EPS, ALU.mult, ALU.add).then_inc(s["o_ms"].sem, 1)
            dve.wait_ge(s["conv_hi"].sem, s["conv_hi"].at(1))
            nc.vector.tensor_tensor(c.act_lo[:, KT:KT + 2, :], ln2[:, 2:4, :],
                                    c.act_hi[:, KT:KT + 2, :].bitcast(F32), ALU.subtract)
            dve.wait_ge(s["o_rstd"].sem, s["o_rstd"].at(1))
            o8 = c.work[:, 18, :].rearrange("p (g n) -> p g n", n=P)
            nc.vector.tensor_tensor(o8, o8, o_rstd.unsqueeze(2).to_broadcast([P, 8, P]),
                                    ALU.mult).then_inc(s["o_scaled"].sem, 1)
            for h in range(AH):
                dve.wait_ge(s["oT_hi"].sem, s["oT_hi"].at(h + 1))
                nc.vector.scalar_tensor_tensor(c.act_lo[:, KT + 4 + h, :], c.bank[h][:, 0:S], subg,
                                               c.act_hi[:, KT + 4 + h, :].bitcast(F32), ALU.mult,
                                               ALU.subtract)
    c.end_signals(s, counts)


CHUNK = 64
PAIRS = HEADS // 2
R_STRICT, R_INCL, R_UP1, R_LOW1 = 384, 512, 640, 768
EXP_SCALE = -2.718281828459045 ** -0.5


def feature_view(units):
    return units.rearrange("p a (b s) -> p (a b) s", s=S)


def plain_norm_stage(c, gain_col):
    nc = c.nc
    ms = c.small[:, 0:NT]
    rstd = c.small[:, NT:2 * NT]
    half = c.const[:, 128:128 + NT]
    xn = c.work[:, 0:NT, :]
    junk = c.work[:, NT:2 * NT, :]
    hT = feature_view(c.work[:, 4:6, :])
    squares, rms, scaled, turned = (c.new_signal("plain_" + n) for n in ("squares", "rms", "scaled", "turned"))
    with nc.Block() as block:
        @block.scalar
        def _(act):
            for t in range(NT):
                last = nc.scalar.activation(junk[:, t, :], c.x[:, t, :], ACT.Square,
                                            scale=float(D) ** -0.5, accum_out=ms[:, t:t + 1])
            last.then_inc(squares.sem, 1)
            for k in range(0, KT, 2):
                act.wait_ge(turned.sem, k + 1)
                nc.scalar.activation(hT[:, k, :], c.bank[k][:, 0:S], ACT.Copy,
                                     scale=c.cols[:, gain_col + k:gain_col + k + 1])

        @block.gpsimd
        def _(pool):
            pool.wait_ge(squares.sem, 1)
            c.pool_order.link(pool, nc.gpsimd.tensor_scalar(ms, ms, EPS, None, ALU.add))
            nc.gpsimd.tensor_tensor(rstd, ms, half, ALU.pow).then_inc(rms.sem, 1)

        @block.vector
        def _(dve):
            dve.wait_ge(rms.sem, 1)
            for t in range(NT):
                nc.vector.tensor_scalar(xn[:, t, :], c.x[:, t, :], rstd[:, t:t + 1], None,
                                        ALU.mult).then_inc(scaled.sem, 1)
            for k in range(1, KT, 2):
                dve.wait_ge(turned.sem, k + 1)
                nc.vector.tensor_scalar(hT[:, k, :], c.bank[k][:, 0:S],
                                        c.cols[:, gain_col + k:gain_col + k + 1], None, ALU.mult)

        @block.tensor
        def _(pe):
            pe.wait_ge(scaled.sem, NT)
            for k in range(KT):
                for t in range(NT):
                    last = nc.tensor.transpose(c.bank[k][:, t * P:(t + 1) * P],
                                               xn[:, t, k * P:(k + 1) * P], c.ident)
                last.then_inc(turned.sem, 1)


def mix(c, dve_nc, dst, hT, dx, mu_col, n):
    for k in range(KT):
        col = mu_col + n * KT + k
        last = dve_nc.scalar_tensor_tensor(dst[:, k, :], dx[:, k, :], c.cols[:, col:col + 1],
                                           hT[:, k, :], ALU.mult, ALU.add)
    return last


def lora_stage(c, mu_col):
    nc = c.nc
    hT, dx = feature_view(c.work[:, 4:6, :]), feature_view(c.work[:, 6:8, :])
    xa, xb = feature_view(c.work[:, 0:2, :]), feature_view(c.work[:, 2:4, :])
    flat = c.work[:, :, :].rearrange("p a n -> p (a n)")
    first = flat[:, 8 * UNIT:8 * UNIT + 2304]
    w1 = first[:, 0:512].rearrange("p (k n) -> p k n", k=KT)
    a1 = first[:, 512:1024].rearrange("p (k n) -> p k n", k=KT)
    g1 = first[:, 1024:2304].rearrange("p (k n) -> p k n", k=KT)
    second = c.work[:, 11:14, :]
    tT, aT, gT = (c.work[:, 10, i * S:(i + 1) * S] for i in (1, 2, 3))
    names = ("w1_in", "w2_in", "ones", "dx", "mixed", "split_r", "low", "low_act", "wide", "wide_out", "masks_in")
    s = {n: c.new_signal("lora_" + n).sem for n in names}

    with nc.Block() as block:
        @block.sync
        def _(sp):
            sp.dma_start(first, c.dram["lora1"][:, :]).then_inc(s["w1_in"], 16)
            sp.dma_start(second, c.dram["lora2"][:, :, :]).then_inc(s["w2_in"], 16)
            sp.dma_start(c.const[:, R_STRICT:R_STRICT + 4 * P], c.dram["rmask"][:, 0:4 * P]).then_inc(
                s["masks_in"], 16)
            sp.wait_ge(s["masks_in"], 16)

        @block.gpsimd
        def _(pool):
            nc.gpsimd.memset(c.work[64:65, 10, S:3 * S], 1.0).then_inc(s["ones"], 1)

        @block.vector
        def _(dve):
            last = nc.vector.tensor_tensor(dx[:, :, 1:S], hT[:, :, 0:S - 1], hT[:, :, 1:S], ALU.subtract)
            last = nc.vector.tensor_scalar(dx[:, :, 0:1], hT[:, :, 0:1], -1.0, None, ALU.mult)
            c.dve_order.link(dve, last)
            mix(c, nc.vector, xa, hT, dx, mu_col, 3).then_inc(s["mixed"], 1)
            mix(c, nc.vector, xb, hT, dx, mu_col, 4).then_inc(s["mixed"], 1)
            dve.wait_ge(s["low"], 1)
            mix(c, nc.vector, xa, hT, dx, mu_col, 5).then_inc(s["mixed"], 1)
            dve.wait_ge(s["low"], 2)
            mix(c, nc.vector, xb, hT, dx, mu_col, 0).then_inc(s["mixed"], 1)
            dve.wait_ge(s["split_r"], 1)
            nc.vector.tensor_tensor(c.act_lo[:, 0:KT, :], xb, c.act_hi[:, 0:KT, :].bitcast(F32),
                                    ALU.subtract)
            dve.wait_ge(s["wide"], 3)
            for q in range(4):
                nc.vector.tensor_copy(c.work[:, 18 + q // 2, (q % 2) * HALF:(q % 2 + 1) * HALF],
                                      c.bank[4 + q][:, :])

        @block.tensor
        def _(pe):
            pe.wait_ge(s["w1_in"], 16)
            for i, (w, x, n0, rows, bank) in enumerate((
                    (w1, xa, 0, slice(0, 64), c.bank[0]), (a1, xb, 0, slice(0, 64), c.bank[1]),
                    (g1, xa, 0, slice(0, 128), c.bank[2]), (g1, xa, 128, slice(96, 128), c.bank[3]))):
                pe.wait_ge(s["mixed"], min(i, 2) + 1)
                width = rows.stop - rows.start
                for k in range(KT):
                    last = nc.tensor.matmul(bank[rows, 0:S], w[:, k, n0:n0 + width], x[:, k, :],
                                            start=k == 0, stop=k == KT - 1)
                last.then_inc(s["low"], 1)
            pe.wait_ge(s["w2_in"], 16)
            pe.wait_ge(s["ones"], 1)
            for i in range(3):
                pe.wait_ge(s["low_act"], (1, 4, 4)[i])
                if i == 2:
                    pe.wait_ge(s["wide_out"], 1)
                for t in range(NT):
                    tok = slice(t * P, (t + 1) * P)
                    for h in range(2):
                        w = slice(h * HALF, (h + 1) * HALF)
                        bank = c.bank[(4, 0, 4)[i] + 2 * t + h]
                        if i < 2:
                            last = nc.tensor.matmul(bank[:, :], (tT, aT)[i][0:65, tok], second[0:65, i, w],
                                                    start=True, stop=True)
                        else:
                            nc.tensor.matmul(bank[:, :], gT[:, tok], second[:, 2, w], start=True, stop=False)
                            last = nc.tensor.matmul(bank[:, :], tT[96:128, tok], second[96:128, 0, w],
                                                    start=False, stop=True, tile_position=(96, 0))
                last.then_inc(s["wide"], 1)

        @block.scalar
        def _(act):
            for i, (f, dst, rows) in enumerate(((ACT.Tanh, tT, slice(0, 64)), (ACT.Copy, aT, slice(0, 64)),
                                                (ACT.Sigmoid, gT, slice(0, 128)),
                                                (ACT.Sigmoid, tT, slice(96, 128)))):
                act.wait_ge(s["low"], i + 1)
                nc.scalar.activation(dst[rows, :], c.bank[i][rows, 0:S], f).then_inc(s["low_act"], 1)
            act.wait_ge(s["mixed"], 4)
            nc.scalar.activation(c.act_hi[:, 0:KT, :], xb, ACT.Copy).then_inc(s["split_r"], 1)
            for i in range(2):
                act.wait_ge(s["wide"], i + 1)
                for q in range(4):
                    last = nc.scalar.activation(
                        c.work[:, (14, 16)[i] + q // 2, (q % 2) * HALF:(q % 2 + 1) * HALF],
                        c.bank[(4, 0)[i] + q][:, :], ACT.Sigmoid)
                last.then_inc(s["wide_out"], 1)


def rkv_stage(c, mu_col):
    nc = c.nc
    hT, dx = feature_view(c.work[:, 4:6, :]), feature_view(c.work[:, 6:8, :])
    xa, xb = feature_view(c.work[:, 0:2, :]), feature_view(c.work[:, 2:4, :])
    mixed, high, low, read, saved = (c.new_signal("rkv_" + n) for n in ("mixed", "high", "low", "read", "saved"))
    count = 24
    with nc.Block() as block:
        @block.sync
        def _(sp):
            sp.dma_start(c.dram["g_park"][:, :, :], c.work[:, 18:20, :]).then_inc(saved.sem, 16)
            sp.dma_start(c.dram["x_park"][:, :, :], c.x[:, :, :]).then_inc(saved.sem, 16)
            c.stream_stage_loads(sp, count)
            sp.wait_ge(saved.sem, 32)

        @block.scalar
        def _(act):
            act.wait_ge(mixed.sem, 1)
            nc.scalar.activation(c.act_hi[:, KT:2 * KT, :], xa, ACT.Copy).then_inc(high.sem, 1)
            for m in range(count + 1):
                if m < count:
                    c.split_hi(act, c.first_unit + AHEAD + m)
                if m in (4, 8, 12, 16, 20, 24):
                    e = m // 4 - 1
                    i, h = e // 2, e % 2
                    unit_done(c, act, m - 1)
                    for t in range(NT):
                        last = nc.scalar.activation(c.work[:, 8 + 2 * i + t, h * HALF:(h + 1) * HALF],
                                                    c.bank[(0, 4, 0)[i] + 2 * t + h][:, :], ACT.Copy)
                    last.then_inc(read.sem, 1)
                if m == 8:
                    act.wait_ge(mixed.sem, 2)
                    nc.scalar.activation(c.act_hi[:, 0:KT, :], xb, ACT.Copy).then_inc(high.sem, 1)

        @block.vector
        def _(dve):
            mix(c, nc.vector, xa, hT, dx, mu_col, 1).then_inc(mixed.sem, 1)
            mix(c, nc.vector, xb, hT, dx, mu_col, 2).then_inc(mixed.sem, 1)
            dve.wait_ge(high.sem, 1)
            nc.vector.tensor_tensor(c.act_lo[:, KT:2 * KT, :], xa, c.act_hi[:, KT:2 * KT, :].bitcast(F32),
                                    ALU.subtract).then_inc(low.sem, 1)
            for m in range(count):
                c.split_lo(dve, c.first_unit + AHEAD + m)
                if m == 8:
                    dve.wait_ge(high.sem, 2)
                    nc.vector.tensor_tensor(c.act_lo[:, 0:KT, :], xb, c.act_hi[:, 0:KT, :].bitcast(F32),
                                            ALU.subtract).then_inc(low.sem, 1)

        @block.tensor
        def _(pe):
            for i in range(3):
                if i:
                    pe.wait_ge(low.sem, i)
                for h in range(2):
                    if i == 2:
                        pe.wait_ge(read.sem, h + 1)
                    for k in range(4):
                        product_a(c, pe, 8 * i + 4 * h + k, k, 4,
                                  [c.bank[(0, 4, 0)[i] + h], c.bank[(0, 4, 0)[i] + 2 + h]],
                                  (0, KT, 0)[i])
    c.end_stage(count)


def token_stage(c):
    nc = c.nc
    r, k, v, sig, a = (c.work[:, i:i + 2, :] for i in (8, 10, 12, 14, 16))
    kk, tmp, wexc = c.work[:, 3:5, :], c.work[:, 5:7, :], c.work[:, 0:2, :]
    kk_row, ka_row, rk_row = (c.work[:, i:i + 1, :].to_broadcast([P, NT, D]) for i in (0, 1, 2))
    ss, rinv = c.small[:, 0:32], c.small[:, 32:64]
    bonus, wc = c.small[:, 64:96], c.small[:, 96:128]
    incl, strict = c.const[:, R_INCL:R_INCL + P], c.const[:, R_STRICT:R_STRICT + P]
    half = c.const[:, 128:160]
    names = ("rows", "ss", "rinv", "cum", "cum_ex", "wc_bank", "w_incl", "w_exc", "w_inv", "free_tmp", "free_01", "free_inc")
    s = {n: c.new_signal("token_" + n).sem for n in names}
    order = c.dve_order

    def grouped(u):
        return u.rearrange("p t (h n) -> p (t h) n", n=HD)

    def quad(u, q):
        return u[:, q // 2, (q % 2) * HALF:(q % 2 + 1) * HALF]

    with nc.Block() as block:
        @block.sync
        def _(sp):
            for i in range(3):
                sp.dma_start(c.work[:, i, :], c.dram["rrows"][i, :, :]).then_inc(s["rows"], 16)

        @block.tensor
        def _(pe):
            for q in range(4):
                last = nc.tensor.matmul(c.bank[q][:, :], incl, quad(sig, q), start=True, stop=True)
            last.then_inc(s["cum"], 1)
            for q in range(4):
                last = nc.tensor.matmul(c.bank[4 + q][:, :], strict, quad(sig, q), start=True, stop=True)
            last.then_inc(s["cum_ex"], 1)
            pe.wait_ge(s["free_inc"], 1)
            for p in range(PAIRS):
                for t in range(NT):
                    last = nc.tensor.matmul(c.bank[0][:, 4 * p + 2 * t:4 * p + 2 * t + 2],
                                            sig[:, t, p * P:(p + 1) * P], incl[:, CHUNK - 1:P:CHUNK],
                                            start=True, stop=True)
            last.then_inc(s["wc_bank"], 1)

        @block.scalar
        def _(act):
            act.wait_ge(s["free_tmp"], 1)
            act.wait_ge(s["cum"], 1)
            for q in range(4):
                last = nc.scalar.activation(quad(tmp, q), c.bank[q][:, :], ACT.Exp, scale=-EXP_SCALE)
            last.then_inc(s["w_inv"], 1)
            act.wait_ge(s["free_01"], 1)
            act.wait_ge(s["cum_ex"], 1)
            for q in range(4):
                last = nc.scalar.activation(quad(wexc, q), c.bank[4 + q][:, :], ACT.Exp, scale=EXP_SCALE)
            last.then_inc(s["w_exc"], 1)
            act.wait_ge(s["w_exc"], 1)
            for q in range(1, 5):
                b = q % 4
                last = nc.scalar.activation(c.bank[4 + b][:, :], c.bank[b][:, :], ACT.Exp, scale=EXP_SCALE)
            last.then_inc(s["free_inc"], 1)
            act.wait_ge(s["wc_bank"], 1)
            nc.scalar.activation(wc, c.bank[0][:, 0:32], ACT.Exp, scale=EXP_SCALE)

        @block.gpsimd
        def _(pool):
            pool.wait_ge(s["ss"], 1)
            nc.gpsimd.tensor_tensor(rinv, ss, half, ALU.pow).then_inc(s["rinv"], 1)

        @block.vector
        def _(dve):
            dve.wait_ge(s["rows"], 48)
            order.link(dve, nc.vector.tensor_tensor(kk, k, kk_row, ALU.mult))
            order.link(dve, nc.vector.tensor_tensor(tmp, kk, kk, ALU.mult))
            order.link(dve, nc.vector.tensor_reduce(ss, grouped(tmp), AX.X, ALU.add))
            nc.vector.tensor_scalar(ss, ss, 1e-24, None, ALU.max).then_inc(s["ss"], 1)
            order.link(dve, nc.vector.scalar_tensor_tensor(tmp, a, -1.0, ka_row, ALU.add, ALU.mult))
            order.link(dve, nc.vector.scalar_tensor_tensor(k, tmp, 1.0, k, ALU.add, ALU.mult))
            order.link(dve, nc.vector.tensor_tensor(tmp, r, k, ALU.mult))
            order.link(dve, nc.vector.tensor_tensor(tmp, tmp, rk_row, ALU.mult))
            nc.vector.tensor_reduce(bonus, grouped(tmp), AX.X, ALU.add).then_inc(s["free_tmp"], 1)
            dve.wait_ge(s["rinv"], 1)
            order.link(dve, nc.vector.tensor_tensor(grouped(kk), grouped(kk),
                                                    rinv.unsqueeze(2).to_broadcast([P, 32, HD]), ALU.mult))
            ins = nc.vector.tensor_tensor(a, kk, a, ALU.mult)
            ins.then_inc(s["free_01"], 1)
            dve.wait_ge(s["free_01"], 1)
            dve.wait_ge(s["w_inv"], 1)
            nc.vector.tensor_tensor(a, a, tmp, ALU.mult)
            nc.vector.tensor_tensor(k, k, tmp, ALU.mult)
            dve.wait_ge(s["w_exc"], 1)
            nc.vector.scalar_tensor_tensor(kk, kk, -1.0, wexc, ALU.mult, ALU.mult)
            dve.wait_ge(s["free_inc"], 1)
            for q in range(4):
                nc.vector.tensor_tensor(quad(r, q), quad(r, q), c.bank[4 + q][:, :], ALU.mult)


class Recurrence:

    def __init__(self, c, t):
        w = c.work
        self.r, self.a, self.b, self.k, self.v = (w[:, i + t, :] for i in (8, 3, 16, 10, 12))
        self.y = self.r
        self.rT, self.aT, self.bT, self.kT = (
            w[:, i, :].rearrange("p (h s) -> p h s", h=PAIRS) for i in (0, 1, 2, 5))
        self.rb = w[:, 14:16, :].rearrange("p a (g n) -> p (a g) n", g=2)
        self.base = w[:, 6, :]
        self.sa = w[:, 18, :]
        self.levels = w[:, 7, 0:5 * P]
        self.kv = w[:, 7, 5 * P:5 * P + 2 * P]
        self.state = w[:, 19, 0:HALF]
        self.low, self.m, self.t, self.low_part = (
            c.x[:, i // 2, (i % 2) * HALF:(i % 2 + 1) * HALF] for i in range(4))
        self.p1 = w[:, 19, HALF:UNIT]

    def heads(self, unit, e, half):
        return unit.rearrange("p (q e n) -> p q e n", e=2, n=HD)[:, 4 * half:4 * half + 4, e, :]


def turn_stage(c, t):
    nc = c.nc
    R = Recurrence(c, t)
    turned = c.signals("turn_", {"turned": 8})["turned"]
    levels_in = c.new_signal(f"levels_in{t}")
    jobs = [(src, dst, half) for src, dst in ((R.b, R.bT), (R.a, R.aT), (R.k, R.kT), (R.r, R.rT))
            for half in range(2)]

    def evacuate(eng, copy, mine):
        for i, (src, dst, half) in enumerate(jobs):
            if i % 2 == mine:
                eng.wait_ge(turned.sem, turned.at(i + 1))
                copy(dst[:, 4 * half:4 * half + 4, :], c.bank[i][:, :].rearrange("p (h s) -> p h s", h=4))

    with nc.Block() as block:
        @block.sync
        def _(sp):
            if t == 0:
                sp.dma_start(R.levels, c.dram["rmask"][:, 4 * P:9 * P]).then_inc(levels_in.sem, 16)
                sp.wait_ge(levels_in.sem, 16)

        @block.tensor
        def _(pe):
            for i, (src, dst, half) in enumerate(jobs):
                for p in range(4):
                    f = (4 * half + p) * P
                    last = nc.tensor.transpose(c.bank[i][:, p * P:(p + 1) * P], src[:, f:f + P], c.ident)
                last.then_inc(turned.sem, 1)

        @block.scalar
        def _(act):
            evacuate(act, lambda o, i: nc.scalar.activation(o, i, ACT.Copy), 0)

        @block.vector
        def _(dve):
            if t == 0:
                nc.vector.memset(R.state, 0.0)
            evacuate(dve, nc.vector.tensor_copy, 1)
    turned.base += len(jobs)


def solve_stage(c, t):
    nc = c.nc
    R = Recurrence(c, t)
    counts = {"grams": 20, "u_read": 4, "kr_read": 8, "rb_read": 4, "kv_bank": 4,
              "kv_made": 4, "y_read": 4, "lows": 40, "p1_bank": 40,
              "p1_made": 40, "mt_bank": 40, "m_made": 40, "solved": 8,
              "aT_out": 8}
    s = c.signals("solve_", counts)
    order = c.dve_order
    LEVELS = 5
    groups = [(e, half) for e in range(2) for half in range(2)]

    def four(u):
        return u.rearrange("p (h n) -> p h n", h=4)

    def over4(mask):
        return mask.unsqueeze(1).to_broadcast([P, 4, P])

    strict, incl, up1, low1 = (c.const[:, i:i + P] for i in (R_STRICT, R_INCL, R_UP1, R_LOW1))
    ak, rk = R.low_part, R.p1

    with nc.Block() as block:
        @block.tensor
        def _(pe):
            for g, (e, half) in enumerate(groups):
                rows = slice(HD * e, HD * (e + 1))
                if g:
                    pe.wait_ge(s["aT_out"].sem, s["aT_out"].at(2 * g))
                    pe.wait_ge(s["m_made"].sem, s["m_made"].at(2 * LEVELS * g))
                for bank, stat, mov in ((2, R.kT, R.aT), (3, R.kT, R.rT), (4, R.bT, R.rT),
                                        (0, R.bT, R.aT), (1, R.aT, R.bT)):
                    if bank == 4 and g:
                        pe.wait_ge(s["rb_read"].sem, s["rb_read"].at(g))
                    for p in range(4):
                        last = nc.tensor.matmul(c.bank[bank][:, p * P:(p + 1) * P],
                                                stat[rows, 4 * half + p, :], mov[rows, 4 * half + p, :],
                                                start=True, stop=True)
                    last.then_inc(s["grams"].sem, 1)
                if g:
                    pe.wait_ge(s["y_read"].sem, s["y_read"].at(g))
                    pe.wait_ge(s["kv_made"].sem, s["kv_made"].at(g))
                for i, m in enumerate((ak, rk)):
                    pe.wait_ge(s["kr_read"].sem, s["kr_read"].at(2 * g + i + 1))
                    for p in range(4):
                        h = 2 * (4 * half + p) + e
                        last = nc.tensor.matmul(c.bank[5][:, i * S + p * HD:i * S + (p + 1) * HD],
                                                m[:, p * P:(p + 1) * P], R.v[:, h * HD:(h + 1) * HD],
                                                start=True, stop=True)
                last.then_inc(s["kv_bank"].sem, 1)
                for level in range(LEVELS):
                    for sub in range(2):
                        step = 2 * (LEVELS * g + level) + sub
                        pe.wait_ge(s["lows"].sem, s["lows"].at(step + 1))
                        pe.wait_ge(s["m_made"].sem, s["m_made"].at(step - 1)) if level else pe.wait_ge(s["u_read"].sem, s["u_read"].at(g + 1))
                        for p in (2 * sub, 2 * sub + 1):
                            cols = slice(p * P, (p + 1) * P)
                            last = nc.tensor.matmul(c.bank[6 + sub][:, (p % 2) * P:(p % 2 + 1) * P],
                                                    R.low_part[:, cols], R.m[:, cols], start=True, stop=True)
                        last.then_inc(s["p1_bank"].sem, 1)
                    for sub in range(2):
                        step = 2 * (LEVELS * g + level) + sub
                        pe.wait_ge(s["p1_made"].sem, s["p1_made"].at(step + 1))
                        for p in (2 * sub, 2 * sub + 1):
                            cols = slice(p * P, (p + 1) * P)
                            at = (p % 2) * P
                            nc.tensor.matmul(c.bank[sub][:, at:at + P], R.t[:, cols], R.p1[:, cols],
                                             start=True, stop=True)
                            last = nc.tensor.matmul(c.bank[sub][:, S + at:S + at + P], R.p1[:, cols],
                                                    R.t[:, cols], start=True, stop=True)
                        last.then_inc(s["mt_bank"].sem, 1)
                pe.wait_ge(s["m_made"].sem, s["m_made"].at(2 * LEVELS * (g + 1)))
                for p in range(4):
                    h = 2 * (4 * half + p) + e
                    last = nc.tensor.matmul(c.bank[2][rows, p * P:(p + 1) * P], R.a[:, h * HD:(h + 1) * HD],
                                            R.m[:, p * P:(p + 1) * P], start=True, stop=True)
                last.then_inc(s["solved"].sem, 1)
                pe.wait_ge(s["kv_made"].sem, s["kv_made"].at(g + 1))
                for p in range(4):
                    last = nc.tensor.matmul(c.bank[3][:, p * HD:(p + 1) * HD], R.m[:, p * P:(p + 1) * P],
                                            R.kv[:, p * HD:(p + 1) * HD], start=True, stop=True)
                last.then_inc(s["solved"].sem, 1)

        @block.scalar
        def _(act):
            for g, (e, half) in enumerate(groups):
                rows = slice(HD * e, HD * (e + 1))
                act.wait_ge(s["kv_bank"].sem, s["kv_bank"].at(g + 1))
                if g:
                    act.wait_ge(s["solved"].sem, s["solved"].at(2 * g))
                nc.scalar.activation(R.kv, c.bank[5][:, 0:S], ACT.Copy).then_inc(s["kv_made"].sem, 1)
                nc.scalar.activation(R.heads(R.y, e, half),
                                     c.bank[5][:, S:2 * S].rearrange("p (h n) -> p h n", h=4),
                                     ACT.Copy).then_inc(s["y_read"].sem, 1)
                for step in range(2 * LEVELS * g, 2 * LEVELS * (g + 1)):
                    sub = step % 2
                    act.wait_ge(s["p1_bank"].sem, s["p1_bank"].at(step + 1))
                    if step > 2 * LEVELS * g + 1:
                        act.wait_ge(s["mt_bank"].sem, s["mt_bank"].at(step - 1))
                    nc.scalar.activation(R.p1[:, sub * S:(sub + 1) * S], c.bank[6 + sub][:, 0:S],
                                         ACT.Copy).then_inc(s["p1_made"].sem, 1)
                act.wait_ge(s["solved"].sem, s["solved"].at(2 * g + 1))
                nc.scalar.activation(R.aT[rows, 4 * half:4 * half + 4, :],
                                     c.bank[2][rows, :].rearrange("p (h s) -> p h s", h=4),
                                     ACT.Copy).then_inc(s["aT_out"].sem, 1)
                act.wait_ge(s["solved"].sem, s["solved"].at(2 * g + 2))
                nc.scalar.activation(R.heads(R.base, e, half),
                                     c.bank[3][:, 0:S].rearrange("p (h n) -> p h n", h=4),
                                     ACT.Copy).then_inc(s["aT_out"].sem, 1)

        @block.vector
        def _(dve):
            def mask_low(g, level):
                for sub in range(2):
                    step = 2 * (LEVELS * g + level) + sub
                    if level:
                        dve.wait_ge(s["p1_bank"].sem, s["p1_bank"].at(step - 1))
                    cols = slice(sub * S, (sub + 1) * S)
                    mask = R.levels[:, level * P:(level + 1) * P].unsqueeze(1).to_broadcast([P, 2, P])
                    nc.vector.tensor_tensor(R.low_part[:, cols].rearrange("p (h n) -> p h n", h=2),
                                            R.low[:, cols].rearrange("p (h n) -> p h n", h=2), mask,
                                            ALU.mult).then_inc(s["lows"].sem, 1)

            for g, (e, half) in enumerate(groups):
                for i, (buf, mask) in enumerate(((ak, strict), (rk, incl))):
                    dve.wait_ge(s["grams"].sem, s["grams"].at(5 * g + i + 1))
                    if g:
                        dve.wait_ge(s["mt_bank"].sem, s["mt_bank"].at(2 * LEVELS * g))
                    nc.vector.tensor_tensor(four(buf), four(c.bank[2 + i][:, :]), over4(mask),
                                            ALU.mult).then_inc(s["kr_read"].sem, 1)
                dve.wait_ge(s["grams"].sem, s["grams"].at(5 * g + 3))
                nc.vector.tensor_tensor(four(R.rb[:, 2 * e + half, :]), four(c.bank[4][:, :]), over4(incl),
                                        ALU.mult).then_inc(s["rb_read"].sem, 1)
                if g:
                    dve.wait_ge(s["solved"].sem, s["solved"].at(2 * g))
                dve.wait_ge(s["grams"].sem, s["grams"].at(5 * g + 4))
                nc.vector.tensor_tensor(four(R.m), four(c.bank[0][:, :]), over4(up1), ALU.mult)
                dve.wait_ge(s["grams"].sem, s["grams"].at(5 * g + 5))
                nc.vector.tensor_copy(R.low, c.bank[1][:, :])
                order.link(dve, nc.vector.tensor_tensor(four(R.t), four(c.bank[1][:, :]), over4(low1),
                                                        ALU.mult))
                nc.vector.tensor_tensor(four(R.m), four(R.m), over4(c.ident), ALU.add)
                nc.vector.tensor_tensor(four(R.t), four(R.t), over4(c.ident), ALU.add).then_inc(s["u_read"].sem, 1)
                dve.wait_ge(s["u_read"].sem, s["u_read"].at(g + 1))
                dve.wait_ge(s["kv_bank"].sem, s["kv_bank"].at(g + 1))
                mask_low(g, 0)
                for level in range(LEVELS):
                    if level + 1 < LEVELS:
                        mask_low(g, level + 1)
                    for sub in range(2):
                        step = 2 * (LEVELS * g + level) + sub
                        dve.wait_ge(s["mt_bank"].sem, s["mt_bank"].at(step + 1))
                        if level:
                            dve.wait_ge(s["m_made"].sem, s["m_made"].at(step - 1))
                        cols = slice(sub * S, (sub + 1) * S)
                        nc.vector.tensor_tensor(R.m[:, cols], R.m[:, cols], c.bank[sub][:, 0:S], ALU.add)
                        nc.vector.tensor_tensor(R.t[:, cols], R.t[:, cols], c.bank[sub][:, S:2 * S],
                                                ALU.add).then_inc(s["m_made"].sem, 1)
    c.end_signals(s, counts)


def step_stage(c, t):
    nc = c.nc
    R = Recurrence(c, t)
    counts = {"sa_bank": 2, "sa_made": 4, "y_bank": 2, "state_bank": 2, "state_made": 2,
              "rb_bank": 1}
    s = c.signals("step_", counts)
    order = c.dve_order

    def parity(u, e):
        return u.rearrange("p (q e n) -> p q e n", e=2, n=HD)[:, :, e, :]

    def pairs(u):
        return u.rearrange("p (q n) -> p q n", n=HD)

    with nc.Block() as block:
        @block.tensor
        def _(pe):
            for ch in range(2):
                tok = slice(CHUNK * ch, CHUNK * (ch + 1))
                if ch:
                    pe.wait_ge(s["state_made"].sem, s["state_made"].at(1))
                for first, left, done in ((0, R.aT, "sa_bank"), (2, R.rT, "y_bank")):
                    for e in range(2):
                        rows = slice(HD * e, HD * (e + 1))
                        for p in range(PAIRS):
                            last = nc.tensor.matmul(c.bank[first + e][tok, p * HD:(p + 1) * HD],
                                                    left[rows, p, tok], R.state[rows, p * HD:(p + 1) * HD],
                                                    start=True, stop=True)
                    last.then_inc(s[done].sem, 1)
                pe.wait_ge(s["sa_made"].sem, s["sa_made"].at(2 * (ch + 1)))
                for e in range(2):
                    rows = slice(HD * e, HD * (e + 1))
                    for p in range(PAIRS):
                        h = 2 * p + e
                        cols = slice(h * HD, (h + 1) * HD)
                        out = c.bank[4][rows, p * HD:(p + 1) * HD]
                        nc.tensor.matmul(out, R.b[tok, cols], R.sa[tok, cols], start=True, stop=False)
                        last = nc.tensor.matmul(out, R.k[tok, cols], R.v[tok, cols], start=False, stop=True)
                last.then_inc(s["state_bank"].sem, 1)
            for e in range(2):
                for p in range(PAIRS):
                    h = 2 * p + e
                    last = nc.tensor.matmul(c.bank[5 + e][:, p * HD:(p + 1) * HD],
                                            R.rb[:, 2 * e + p // 4, (p % 4) * P:(p % 4 + 1) * P],
                                            R.sa[:, h * HD:(h + 1) * HD], start=True, stop=True)
            last.then_inc(s["rb_bank"].sem, 1)

        @block.vector
        def _(dve):
            for ch in range(2):
                tok = slice(CHUNK * ch, CHUNK * (ch + 1))
                dve.wait_ge(s["sa_bank"].sem, s["sa_bank"].at(ch + 1))
                for e in range(2):
                    nc.vector.tensor_tensor(parity(R.sa, e)[tok], pairs(c.bank[e][:, :])[tok],
                                            parity(R.base, e)[tok], ALU.add).then_inc(s["sa_made"].sem, 1)
                dve.wait_ge(s["y_bank"].sem, s["y_bank"].at(ch + 1))
                for e in range(2):
                    last = nc.vector.tensor_tensor(parity(R.y, e)[tok], pairs(c.bank[2 + e][:, :])[tok],
                                                   parity(R.y, e)[tok], ALU.add)
                order.link(dve, last)
                dve.wait_ge(s["state_bank"].sem, s["state_bank"].at(ch + 1))
                order.link(dve, nc.vector.tensor_tensor(R.state, R.state, c.bank[4][:, :], ALU.add))
                at = 96 + 2 * t + ch
                decay = c.small[:, at:at + 4 * PAIRS - 3:4].unsqueeze(2).to_broadcast([P, PAIRS, HD])
                nc.vector.tensor_tensor(pairs(R.state), pairs(R.state), decay, ALU.mult).then_inc(s["state_made"].sem, 1)
            dve.wait_ge(s["rb_bank"].sem, s["rb_bank"].at(1))
            for e in range(2):
                nc.vector.tensor_tensor(parity(R.y, e), pairs(c.bank[5 + e][:, :]), parity(R.y, e), ALU.add)
    c.end_signals(s, counts)


def head_out_stage(c):
    nc = c.nc
    y, v, sq, vb, gate = (c.work[:, i:i + 2, :] for i in (8, 12, 14, 16, 0))
    ln0, ln1 = (c.work[:, i:i + 1, :].to_broadcast([P, NT, D]) for i in (2, 5))
    total, mean, var, rstd = (c.small[:, i:i + 32] for i in (0, 32, 128, 160))
    bonus = c.small[:, 64:96]
    half = c.const[:, 128:160]
    names = ("back", "var", "rstd", "y", "turned", "high")
    s = {n: c.new_signal("headout_" + n).sem for n in names}
    order = c.dve_order

    def grouped(u):
        return u.rearrange("p t (h n) -> p (t h) n", n=HD)

    def over_head(u):
        return u.unsqueeze(2).to_broadcast([P, NT * HEADS, HD])

    with nc.Block() as block:
        @block.sync
        def _(sp):
            sp.dma_start(gate, c.dram["g_park"][:, :, :]).then_inc(s["back"], 16)
            sp.dma_start(c.x[:, :, :], c.dram["x_park"][:, :, :]).then_inc(s["back"], 16)
            sp.dma_start(c.work[:, 2, :], c.dram["rrows"][3, :, :]).then_inc(s["back"], 16)
            sp.dma_start(c.work[:, 5, :], c.dram["rrows"][4, :, :]).then_inc(s["back"], 16)
            sp.wait_ge(s["back"], 64)

        @block.vector
        def _(dve):
            order.link(dve, nc.vector.tensor_reduce(total, grouped(y), AX.X, ALU.add))
            order.link(dve, nc.vector.tensor_scalar(mean, total, 1.0 / HD, None, ALU.mult))
            order.link(dve, nc.vector.tensor_tensor(grouped(y), grouped(y), over_head(mean), ALU.subtract))
            order.link(dve, nc.vector.tensor_tensor(sq, y, y, ALU.mult))
            order.link(dve, nc.vector.tensor_reduce(var, grouped(sq), AX.X, ALU.add))
            nc.vector.tensor_scalar(var, var, 1.0 / HD, 64e-5, ALU.mult, ALU.add).then_inc(s["var"], 1)
            order.link(dve, nc.vector.tensor_tensor(grouped(vb), grouped(v), over_head(bonus), ALU.mult))
            dve.wait_ge(s["back"], 64)
            nc.vector.tensor_tensor(vb, vb, ln1, ALU.add)
            dve.wait_ge(s["rstd"], 1)
            order.link(dve, nc.vector.tensor_tensor(grouped(y), grouped(y), over_head(rstd), ALU.mult))
            order.link(dve, nc.vector.tensor_tensor(y, y, ln0, ALU.mult))
            order.link(dve, nc.vector.tensor_tensor(y, y, vb, ALU.add))
            nc.vector.tensor_tensor(y, y, gate, ALU.mult).then_inc(s["y"], 1)
            for k in range(KT):
                dve.wait_ge(s["high"], k + 1)
                nc.vector.tensor_tensor(c.act_lo[:, k, :], c.bank[k][:, 0:S],
                                        c.act_hi[:, k, :].bitcast(F32), ALU.subtract)

        @block.gpsimd
        def _(pool):
            pool.wait_ge(s["var"], 1)
            nc.gpsimd.tensor_tensor(rstd, var, half, ALU.pow).then_inc(s["rstd"], 1)

        @block.tensor
        def _(pe):
            pe.wait_ge(s["y"], 1)
            for k in range(KT):
                for t in range(NT):
                    last = nc.tensor.transpose(c.bank[k][:, t * P:(t + 1) * P],
                                               y[:, t, k * P:(k + 1) * P], c.ident)
                last.then_inc(s["turned"], 1)

        @block.scalar
        def _(act):
            for k in range(KT):
                act.wait_ge(s["turned"], k + 1)
                nc.scalar.activation(c.act_hi[:, k, :], c.bank[k][:, 0:S], ACT.Copy).then_inc(s["high"], 1)


def post_norm_stage(c, row):
    nc = c.nc
    ms, rstd = c.small[:, 0:NT], c.small[:, NT:2 * NT]
    half = c.const[:, 128:128 + NT]
    gain = c.work[:, 18, :]
    with nc.Block() as block:
        @block.sync
        def _(sp):
            sp.dma_start(gain, c.dram["rows"][row, :, :]).then_inc(c.row_in.sem, 16)

        @block.scalar
        def _(act):
            for t in range(NT):
                last = nc.scalar.activation(c.work[:, t, :], c.x[:, t, :], ACT.Square,
                                            scale=float(D) ** -0.5, accum_out=ms[:, t:t + 1])
            last.then_inc(c.act_to_pool.sem, 1)

        @block.gpsimd
        def _(pool):
            pool.wait_ge(c.act_to_pool.sem, c.act_to_pool.at(1))
            c.pool_order.link(pool, nc.gpsimd.tensor_scalar(ms, ms, EPS, None, ALU.add))
            nc.gpsimd.tensor_tensor(rstd, ms, half, ALU.pow).then_inc(c.pool_to_dve.sem, 1)

        @block.vector
        def _(dve):
            dve.wait_ge(c.pool_to_dve.sem, c.pool_to_dve.at(1))
            dve.wait_ge(c.row_in.sem, c.row_in.at(16))
            for t in range(NT):
                nc.vector.scalar_tensor_tensor(c.x[:, t, :], c.x[:, t, :], rstd[:, t:t + 1], gain,
                                               ALU.mult, ALU.mult)
    c.end_stage(0, (c.act_to_pool, 1), (c.pool_to_dve, 1), (c.row_in, 16))


def program(nc, dram, out, col, row):
    with ExitStack() as ctx:
        c = Core(nc, ctx, dram)
        start_stage(c)
        for l in range(DEPTH):
            lambda_init = 0.8 - 0.6 * math.exp(-0.3 * l)
            norm_stage(c, col[f"ffn1_norm{l}"])
            ffn_stage(c)
            finish_stage(c, 0.5, banks(c))
            norm_stage(c, col[f"mix_norm{l}"])
            mixer_in_stage(c, l, col[f"conv{l}"], col[f"convb{l}"])
            attention_stage(c, l, col[f"qn{l}"], col[f"kn{l}"], col[f"sub{l}"], col[f"lam{l}"],
                            col[f"ps{l}"], col[f"ln{l}"], lambda_init)
            project_stage(c, KT, KT)
            finish_stage(c, 1.0, banks(c))
            norm_stage(c, col[f"ffn2_norm{l}"])
            ffn_stage(c)
            finish_stage(c, 0.5, banks(c))
            post_norm_stage(c, row[f"post_norm{l}"])
        for i in range(DEPTH):
            norm_stage(c, col[f"g{i}_0"])
            ffn_stage(c)
            finish_stage(c, 0.5, banks(c), row[f"g{i}_1"])
            if i == 0:
                norm_stage(c, col[f"g{i}_2"])
                gmlp_in_stage(c, row["gmlp_bias_v0"], col["gmlp_bias_u"])
                gmlp_mix_stage(c, row["gmlp_bias_s"], col["gmlp_gain"])
                project_stage(c, 2 * KT, 0)
            else:
                plain_norm_stage(c, col[f"g{i}_2"])
                lora_stage(c, col["mu"])
                rkv_stage(c, col["mu"])
                token_stage(c)
                for t in range(NT):
                    turn_stage(c, t)
                    solve_stage(c, t)
                    step_stage(c, t)
                head_out_stage(c)
                project_stage(c, KT, 0)
            finish_stage(c, 1.0, banks(c), row[f"g{i}_3"])
            norm_stage(c, col[f"g{i}_4"])
            ffn_stage(c)
            finish_stage(c, 0.5, banks(c), row[f"g{i}_5"])
            norm_stage(c, col[f"g{i}_6"])
            ple_stage(c, i)
            finish_stage(c, 1.0, lambda t, h: c.work[:, t, h * HALF:(h + 1) * HALF], row[f"g{i}_7"])
        store_stage(c, out)


class Layout:

    def __init__(self):
        self.cols, self.col_at, self.rows, self.row_at = [], {}, [], {}

    def add_cols(self, name, array):
        self.col_at[name] = sum(a.shape[1] for a in self.cols)
        self.cols.append(array)

    def add_row(self, name, array):
        self.row_at[name] = len(self.rows)
        self.rows.append(array)


def unit_b(w, n0):
    import numpy as np
    return np.ascontiguousarray(w[:, n0:n0 + P].reshape(KT, P, P).transpose(1, 0, 2)).reshape(P, UNIT)


def unit_a(w, k, n0):
    import numpy as np
    return np.ascontiguousarray(
        w[2 * k * P:2 * (k + 1) * P, n0:n0 + HALF].reshape(2, P, HALF).transpose(1, 0, 2)).reshape(P, UNIT)


def units_ffn(gate, up, down):
    out = [unit_b(gate, 0), unit_b(up, 0)]
    for t in range(1, FT):
        out += [unit_b(gate, t * P), unit_b(up, t * P), down[(t - 1) * P:t * P, :]]
    return out + [down[(FT - 1) * P:, :]]


def units_a(w):
    return [unit_a(w, k, n0) for n0 in range(0, w.shape[1], HALF) for k in range(w.shape[0] // (2 * P))]


def mixer_vectors(L, a, l):
    import numpy as np
    L.add_cols(f"conv{l}", a["conv_dw"][l].reshape(CONV_W, 2, P).transpose(2, 0, 1).reshape(P, 2 * CONV_W))
    L.add_cols(f"convb{l}", a["conv_dw_bias"][l].reshape(2, P).T)
    L.add_cols(f"ln{l}", np.concatenate([a["conv_ln_gain"][l].reshape(2, P).T,
                                         a["conv_ln_bias"][l].reshape(2, P).T], axis=1))
    L.add_cols(f"qn{l}", np.concatenate([a["q_norm"][l]] * 2)[:, None])
    L.add_cols(f"kn{l}", np.concatenate([a["k_norm"][l]] * 2)[:, None])
    L.add_cols(f"sub{l}", a["attn_subln"][l][:, None])
    L.add_cols(f"ps{l}", a["pool_scale"][l].reshape(2, P).T)
    lam = np.concatenate([a[n][l] for n in ("lambda_q1", "lambda_k1", "lambda_q2", "lambda_k2")])
    L.add_cols(f"lam{l}", np.broadcast_to(lam, (P, 4 * HD)))


def mixer_units(a, l):
    w = a["w_in"][l]
    out = [unit_b(w, n0) for n0 in (0, 256, 128, 384, 512, 640)]
    for n0 in (768, 1280, 1792):
        out += units_a(w[:, n0:n0 + HALF])
    return out + units_a(a["w_out"][l])


def pool_weights(a):
    import numpy as np
    w = a["pool_w"]
    out = np.zeros((DEPTH, P, 2, P), w.dtype)
    for g in range(4):
        r = slice((g % 2) * 64, (g % 2 + 1) * 64)
        out[:, r, g // 2, r] = w[:, g]
    return out


def constants():
    import numpy as np
    const = np.zeros((P, 1024), np.float32)
    const[:, C_IDENT:C_IDENT + P] = np.eye(P)
    const[:, C_HALF:C_HALF + 256] = -0.5
    q = np.arange(S)
    dist = np.abs(q[:, None] - q[None, :]).reshape(NT, P, S).transpose(1, 0, 2)
    for g, w in enumerate((2, 4, 8, 16)):
        lo, hi = np.clip(q - w // 2, 0, S), np.clip(q + w // 2, 0, S)
        at = C_RCNT + (g // 2) * S
        const[(g % 2) * 64:(g % 2 + 1) * 64, at:at + S] = 1.0 / (hi - lo)
    const[:, C_MEAN:C_MEAN + P] = 1.0 / 256
    return const, np.ascontiguousarray(dist.reshape(P, 2 * S).astype(np.float32))



def rwkv_masks():
    import numpy as np
    i = np.arange(P)
    row, col = i[:, None], i[None, :]
    chunk = row // CHUNK == col // CHUNK
    out = [chunk & (row < col), chunk & (row <= col),
           (row // 2 == col // 2) & (row < col), (row // 2 == col // 2) & (row > col)]
    for b in (2, 4, 8, 16, 32):
        out.append((row // (2 * b) == col // (2 * b)) & (row // b > col // b))
    return np.concatenate(out, axis=1).astype(np.float32)


def lora_weights(a):
    import numpy as np

    def tiles(w):
        return w.reshape(KT, P, w.shape[1]).transpose(1, 0, 2).reshape(P, KT * w.shape[1])

    first = np.concatenate([tiles(a[n + "_2"][0]) for n in ("b_w1", "b_a1", "b_g1")], axis=1)
    second = np.zeros((P, 3, D), first.dtype)
    second[0:64, 0], second[64, 0], second[96:128, 0] = a["b_w2_2"][0], a["b_w0_2"][0], a["b_g2_2"][0][P:]
    second[0:64, 1], second[64, 1] = a["b_a2_2"][0], a["b_a0_2"][0]
    second[:, 2] = a["b_g2_2"][0][0:P]
    return np.ascontiguousarray(first), second


def rwkv_rows(a):
    import numpy as np
    rows = [a["b_k_k_2"][0], a["b_k_a_2"][0], a["b_r_k_2"][0].reshape(-1), a["b_lnx_2"][0][0], a["b_lnx_2"][0][1]]
    return np.stack([np.broadcast_to(r, (P, D)) for r in rows])


def rwkv_units(a):
    out = []
    for i in range(3):
        out += units_a(a["b_w_in_2"][0][i])
    return out + units_a(a["b_w_out_2"][0])


def kernel(**inputs):
    import numpy as np
    import concourse.bacc as bacc
    from concourse.bass_utils import run_bass_kernel_spmd as run

    a = {k: np.asarray(v) for k, v in inputs.items()}
    L = Layout()
    gains = a["norm_g_2"]
    for l in range(DEPTH):
        for n in ("ffn1_norm", "mix_norm", "ffn2_norm"):
            L.add_cols(f"{n}{l}", a[n][l].reshape(KT, P).T)
        mixer_vectors(L, a, l)
        L.add_row(f"post_norm{l}", a["post_norm"][l])
        for j in range(8):
            if j % 2:
                L.add_row(f"g{l}_{j}", gains[l, j])
            else:
                L.add_cols(f"g{l}_{j}", gains[l, j].reshape(KT, P).T)
    L.add_cols("gmlp_bias_u", a["a_b_in_2"][0][:2 * D].reshape(2 * KT, P).T)
    L.add_cols("gmlp_gain", a["a_v_gain_2"][0].reshape(2 * KT, P).T)
    L.add_cols("mu", a["b_mu_2"][0].reshape(6 * KT, P).T)
    L.add_row("gmlp_bias_v0", a["a_b_in_2"][0][2 * D:3 * D])
    L.add_row("gmlp_bias_v1", a["a_b_in_2"][0][3 * D:])
    L.add_row("gmlp_bias_s", a["a_b_s_2"][0].reshape(-1))

    def ffn2_units(i, j):
        w13 = a["ffn_w13_2"][i, j]
        return units_ffn(w13[:, :DFF], w13[:, DFF:], a["ffn_w2_2"][i, j])

    units = []
    for l in range(DEPTH):
        units += units_ffn(a["ffn1_w_gate"][l], a["ffn1_w_up"][l], a["ffn1_w_down"][l])
        units += mixer_units(a, l)
        units += units_ffn(a["ffn2_w_gate"][l], a["ffn2_w_up"][l], a["ffn2_w_down"][l])
    w_in = a["a_w_in_2"][0]
    for i in range(DEPTH):
        units += ffn2_units(i, 0)
        if i == 0:
            units += units_a(w_in[:, 2 * D:]) + [unit_b(w_in, n * P) for n in range(2 * KT)]
            units += units_a(a["a_w_out_2"][0])
        else:
            units += rwkv_units(a)
        units += ffn2_units(i, 1)
        units += units_a(a["ple_w_gate_2"][i]) + units_a(a["ple_w_proj_2"][i])

    const, dist = constants()
    lora1, lora2 = lora_weights(a)
    arrays = {
        "w": np.stack(units), "x": np.ascontiguousarray(a["x"][0]),
        "cols": np.ascontiguousarray(np.concatenate(L.cols, axis=1)),
        "rows": np.stack([np.broadcast_to(r, (P, UNIT)) for r in L.rows]),
        "const": const, "dist": dist, "rmask": rwkv_masks(), "poolw": pool_weights(a),
        "pt": np.ascontiguousarray(a["p_2"][:, 0].reshape(DEPTH, S, 2, P).transpose(0, 3, 2, 1)),
        "ws": np.ascontiguousarray(a["a_w_s_2"][0].transpose(2, 0, 1)),
        "lora1": lora1, "lora2": lora2, "rrows": rwkv_rows(a),
    }
    nc = bacc.Bacc("TRN2", target_bir_lowering=False, num_devices=1)
    dram = {k: nc.dram_tensor(k + "_dram", v.shape, F32, kind="ExternalInput").ap()
            for k, v in arrays.items()}
    for n in ("g_park", "x_park"):
        dram[n] = nc.dram_tensor(n, (P, NT, D), F32, kind="Internal").ap()
    out = nc.dram_tensor("out", (S, D), F32, kind="ExternalOutput").ap()
    program(nc, dram, out, L.col_at, L.row_at)
    r = run(nc, [{k + "_dram": v for k, v in arrays.items()}], core_ids=[0])
    return r.results[0]["out"].reshape(1, S, D)
```

```python
import math
from contextlib import ExitStack

import concourse.bass as bass
from concourse import mybir

F32 = mybir.dt.float32
F32R = mybir.dt.float32r
ALU = mybir.AluOpType
ACT = mybir.ActivationFunctionType
AX = mybir.AxisListType

P = 128
D = 1024
S = 256
NT = S // P
KT = D // P
DFF = 2816
FT = DFF // P
UNIT = 1024
RING = 6
AHEAD = RING - 1
HALF = 512
EPS = 1e-6
DEPTH = 2
HEADS = 16
HD = 64
AH = 4


def stage_units():
    out = []
    for _ in range(DEPTH):
        out += [3 * FT, 18, 8, 3 * FT]
    out += [3 * FT, 32, 16, 3 * FT, 10]
    out += [3 * FT, 24, 8, 3 * FT, 10]
    return out


class Signal:

    def __init__(self, sem):
        self.sem = sem
        self.base = 0

    def at(self, k):
        return self.base + k


class Order:

    def __init__(self, sem):
        self.sem = sem
        self.count = 0

    def link(self, eng, ins):
        self.count += 1
        ins.then_inc(self.sem, 1)
        eng.wait_ge(self.sem, self.count)


class Core:

    def __init__(self, nc, ctx, dram):
        self.nc = nc
        self.dram = dram

        def sb(name, shape, dt=F32):
            return ctx.enter_context(nc.sbuf_tensor(name, shape, dt))

        def sem(name):
            return Signal(ctx.enter_context(nc.semaphore(name)))

        self.x = sb("x", [P, NT, D])
        self.act_hi = sb("act_hi", [P, 2 * KT, S], F32R)
        self.act_lo = sb("act_lo", [P, 2 * KT, S], F32R)
        self.raw = sb("raw", [P, RING, UNIT])
        self.w_hi = sb("w_hi", [P, RING, UNIT], F32R)
        self.w_lo = sb("w_lo", [P, RING, UNIT], F32R)
        self.g_hi = sb("g_hi", [P, 2, S], F32R)
        self.g_lo = sb("g_lo", [P, 2, S], F32R)
        self.work = sb("work", [P, 20, UNIT])
        self.silu = self.work[:, 0, 0:2 * S].rearrange("p (i s) -> p i s", i=2)
        self.gated = self.work[:, 1, 0:2 * S].rearrange("p (i s) -> p i s", i=2)
        self.small = sb("small", [P, 512])
        self.cols = sb("cols", [P, dram["cols"].shape[1]])
        self.const = sb("const", [P, dram["const"].shape[1]])
        self.ident = self.const[:, 0:P]
        self.bank = [ctx.enter_context(nc.psum_tensor(f"bank{i}", [P, HALF], F32)) for i in range(8)]

        self.landed = [sem(f"landed{i}") for i in range(RING)]
        self.hi_ready = sem("hi_ready")
        self.lo_ready = sem("lo_ready")
        self.unit_used = sem("unit_used")
        self.silu_ready = sem("silu_ready")
        self.gated_ready = sem("gated_ready")
        self.prod_made = sem("prod_made")
        self.prod_hi = sem("prod_hi")
        self.const_in = sem("const_in")
        self.row_in = sem("row_in")
        self.stored = sem("stored")
        self.act_to_dve = sem("act_to_dve")
        self.act_to_pool = sem("act_to_pool")
        self.dve_to_pool = sem("dve_to_pool")
        self.pool_to_dve = sem("pool_to_dve")
        self.dve_order = Order(ctx.enter_context(nc.semaphore("dve_order")))
        self.act_order = Order(ctx.enter_context(nc.semaphore("act_order")))
        self.pool_order = Order(ctx.enter_context(nc.semaphore("pool_order")))
        self.first_unit = 0
        self.units = sum(stage_units())
        self.gain_loads = 0
        self.gain_row = None
        self.new_signal = sem
        self.repeated = {}

    def signals(self, prefix, counts):
        for name in counts:
            if prefix + name not in self.repeated:
                self.repeated[prefix + name] = self.new_signal(prefix + name)
        return {name: self.repeated[prefix + name] for name in counts}

    def load_gain(self, sp, row):
        if row is not None:
            self.gain_row = self.work[:, 18 + self.gain_loads % 2, :]
            self.gain_loads += 1
            sp.dma_start(self.gain_row, self.dram["rows"][row, :, :]).then_inc(self.row_in.sem, 16)

    def load_unit(self, sp, n):
        if n >= self.units:
            return
        if n >= RING:
            sp.wait_ge(self.lo_ready.sem, n - RING + 1)
        sp.dma_start(self.raw[:, n % RING, :], self.dram["w"][n, :, :]).then_inc(
            self.landed[n % RING].sem, 16)

    def split_hi(self, act, n):
        if n >= self.units:
            return
        act.wait_ge(self.landed[n % RING].sem, 16 * (n // RING + 1))
        if n >= RING:
            act.wait_ge(self.unit_used.sem, n - RING + 1)
        self.nc.scalar.activation(self.w_hi[:, n % RING, :], self.raw[:, n % RING, :],
                                  ACT.Copy).then_inc(self.hi_ready.sem, 1)

    def split_lo(self, dve, n):
        if n >= self.units:
            return
        dve.wait_ge(self.hi_ready.sem, n + 1)
        self.nc.vector.tensor_tensor(self.w_lo[:, n % RING, :], self.raw[:, n % RING, :],
                                     self.w_hi[:, n % RING, :].bitcast(F32),
                                     ALU.subtract).then_inc(self.lo_ready.sem, 1)

    def stream_stage_loads(self, sp, count):
        for n in range(self.first_unit + RING, self.first_unit + count + RING):
            self.load_unit(sp, n)

    def end_stage(self, count, *signals):
        self.first_unit += count
        for signal, k in signals:
            signal.base += k

    def end_signals(self, signals, counts):
        for name, k in counts.items():
            signals[name].base += k


def three_products(nc, out, stat_hi, stat_lo, mov_hi, mov_lo, first, last):
    nc.tensor.matmul(out, stat_hi, mov_hi, start=first, stop=False)
    nc.tensor.matmul(out, stat_hi, mov_lo, start=False, stop=False)
    return nc.tensor.matmul(out, stat_lo, mov_hi, start=False, stop=last)


def start_stage(c):
    nc = c.nc
    with nc.Block() as block:
        @block.sync
        def _(sp):
            sp.dma_start(c.x[:, :, :], c.dram["x"].rearrange("(t p) d -> p t d", p=P)).then_inc(
                c.const_in.sem, 16)
            sp.dma_start(c.const[:, :], c.dram["const"][:, :]).then_inc(c.const_in.sem, 16)
            sp.dma_start(c.cols[:, :], c.dram["cols"][:, :]).then_inc(c.const_in.sem, 16)
            for n in range(RING):
                c.load_unit(sp, n)
            sp.wait_ge(c.const_in.sem, 48)


class Join:

    PLACE = [(0, 0), (1, 0), (2, 0), (3, 0), (5, 0), (7, 0), (0, S), (1, S)]
    TURN_ORDER = [6, 0, 7, 1, 2, 3, 4, 5]
    TURNED_AFTER = [2, 4, 5, 6, 7, 8, 1, 3]

    def __init__(self, c, gain_col, scale=None, sources=None, normed=False, start=False):
        self.c, self.nc = c, c.nc
        self.gain_col, self.scale, self.sources = gain_col, scale, sources
        self.normed, self.start = normed, start
        self.counts = {"x_squares": NT, "rstd": NT, "scaled": NT, "turned": KT, "high": KT, "low": KT}
        if sources:
            self.counts["x_new"] = NT
        if normed:
            self.counts |= {"y_squares": 2 * NT, "y_mean": NT, "y_rstd": NT}
            self.gain, self.gain_loads = c.gain_row, c.gain_loads
        self.s = c.signals("join_", self.counts)
        self.parts, self.y_rstd = c.small[:, 0:2 * NT], c.small[:, 2 * NT:3 * NT]
        self.ms, self.rstd = c.small[:, 3 * NT:4 * NT], c.small[:, 4 * NT:5 * NT]
        self.half = c.const[:, 128:129]
        self.xn = c.work[:, 14:14 + NT, :]
        self.junk = c.work[:, 16:16 + NT, :]

    def turned_tile(self, k):
        bank, at = self.PLACE[k]
        return self.c.bank[bank][:, at:at + S]

    def gained(self, t, h):
        return self.c.work[:, 14 + t, h * HALF:(h + 1) * HALF]

    def scalar(self, act):
        c, nc, s = self.c, self.nc, self.s
        if self.normed:
            for q in range(2 * NT):
                t, h = q // 2, q % 2
                nc.scalar.activation(self.junk[:, t, h * HALF:(h + 1) * HALF], self.sources(t, h),
                                     ACT.Square, scale=float(D) ** -0.5 / self.scale,
                                     accum_out=self.parts[:, q:q + 1]).then_inc(s["y_squares"].sem, 1)
        for t in range(NT):
            if self.sources:
                act.wait_ge(s["x_new"].sem, s["x_new"].at(t + 1))
            nc.scalar.activation(self.junk[:, t, :], c.x[:, t, :], ACT.Square, scale=float(D) ** -0.5,
                                 accum_out=self.ms[:, t:t + 1]).then_inc(s["x_squares"].sem, 1)
        if self.start:
            for n in range(2):
                c.split_hi(act, n)
        for k in range(KT):
            act.wait_ge(s["turned"].sem, s["turned"].at(self.TURNED_AFTER[k]))
            if k >= 6:
                act.wait_ge(s["low"].sem, s["low"].at(k - 5))
            nc.scalar.activation(c.act_hi[:, k, :], self.turned_tile(k), ACT.Copy,
                                 scale=c.cols[:, self.gain_col + k:self.gain_col + k + 1]).then_inc(
                                     s["high"].sem, 1)
        if self.start:
            for n in range(2, AHEAD):
                c.split_hi(act, n)

    def gpsimd(self, pool):
        c, nc, s = self.c, self.nc, self.s
        if self.normed:
            for t in range(NT):
                pool.wait_ge(s["y_mean"].sem, s["y_mean"].at(t + 1))
                nc.gpsimd.tensor_tensor(self.y_rstd[:, t:t + 1], self.y_rstd[:, t:t + 1], self.half,
                                        ALU.pow).then_inc(s["y_rstd"].sem, 1)
        for t in range(NT):
            pool.wait_ge(s["x_squares"].sem, s["x_squares"].at(t + 1))
            m = self.ms[:, t:t + 1]
            c.pool_order.link(pool, nc.gpsimd.tensor_scalar(m, m, EPS, None, ALU.add))
            nc.gpsimd.tensor_tensor(self.rstd[:, t:t + 1], m, self.half, ALU.pow).then_inc(s["rstd"].sem, 1)

    def vector(self, dve):
        c, nc, s = self.c, self.nc, self.s
        if self.normed:
            dve.wait_ge(c.row_in.sem, 16 * self.gain_loads)
            for t in range(NT):
                for h in range(2):
                    dve.wait_ge(s["y_squares"].sem, s["y_squares"].at(2 * t + h + 1))
                    nc.vector.tensor_tensor(self.gained(t, h), self.sources(t, h),
                                            self.gain[:, h * HALF:(h + 1) * HALF], ALU.mult)
                nc.vector.scalar_tensor_tensor(
                    self.y_rstd[:, t:t + 1], self.parts[:, 2 * t:2 * t + 1], EPS / self.scale ** 2,
                    self.parts[:, 2 * t + 1:2 * t + 2], ALU.add, ALU.add).then_inc(s["y_mean"].sem, 1)
            dve.wait_ge(s["y_mean"].sem, s["y_mean"].at(NT))
        if self.sources:
            for t in range(NT):
                if self.normed:
                    dve.wait_ge(s["y_rstd"].sem, s["y_rstd"].at(t + 1))
                for h in range(2):
                    y, by = self.sources(t, h), self.scale
                    if self.normed:
                        y, by = self.gained(t, h), self.y_rstd[:, t:t + 1]
                    xs = c.x[:, t, h * HALF:(h + 1) * HALF]
                    last = nc.vector.scalar_tensor_tensor(xs, y, by, xs, ALU.mult, ALU.add)
                last.then_inc(s["x_new"].sem, 1)
        for t in range(NT):
            dve.wait_ge(s["rstd"].sem, s["rstd"].at(t + 1))
            nc.vector.tensor_scalar(self.xn[:, t, :], c.x[:, t, :], self.rstd[:, t:t + 1], None,
                                    ALU.mult).then_inc(s["scaled"].sem, 1)
        if self.start:
            for n in range(2):
                c.split_lo(dve, n)
        for k in range(KT):
            dve.wait_ge(s["high"].sem, s["high"].at(k + 1))
            nc.vector.scalar_tensor_tensor(
                c.act_lo[:, k, :], self.turned_tile(k), c.cols[:, self.gain_col + k:self.gain_col + k + 1],
                c.act_hi[:, k, :].bitcast(F32), ALU.mult, ALU.subtract).then_inc(s["low"].sem, 1)
        if self.start:
            for n in range(2, AHEAD):
                c.split_lo(dve, n)

    def tensor(self, pe):
        s = self.s
        for t in range(NT):
            pe.wait_ge(s["scaled"].sem, s["scaled"].at(t + 1))
            for k in self.TURN_ORDER:
                last = self.nc.tensor.transpose(self.turned_tile(k)[:, t * P:(t + 1) * P],
                                                self.xn[:, t, k * P:(k + 1) * P], self.c.ident)
                if t == NT - 1:
                    last.then_inc(s["turned"].sem, 1)

    def tile_there(self, pe, k):
        pe.wait_ge(self.s["low"].sem, self.s["low"].at(k + 1))

    def end(self):
        self.c.end_signals(self.s, self.counts)


def ffn_stage(c, join, next_gain=None):
    nc = c.nc
    first = c.first_unit
    down = [c.bank[i] for i in range(4)]
    gate = [c.bank[4], c.bank[5]]
    up = [c.bank[6], c.bank[7]]

    def slot(m):
        return (first + m) % RING

    count = 3 * FT
    LOOPS = (FT - 2) // 2

    with nc.Block() as block:
        @block.sync
        def _(sp):
            c.load_gain(sp, next_gain)
            with sp.Fori(0, count // RING) as i:
                for j in range(RING):
                    n = first + RING + j
                    sp.wait_ge(c.lo_ready.sem, i * RING + (n - RING + 1))
                    sp.dma_start(c.raw[:, n % RING, :], c.dram["w"][bass.ds(i * RING + n, 1), :, :]
                                 .rearrange("o p n -> p (o n)")).then_inc(
                                     c.landed[n % RING].sem, 16)

        def hi_units(act, i, ms):
            for m in ms:
                n = first + m
                if i is None:
                    c.split_hi(act, n)
                    continue
                act.wait_ge(c.landed[n % RING].sem, i * 16 + 16 * (n // RING + 1))
                act.wait_ge(c.unit_used.sem, i * RING + (n - RING + 1))
                nc.scalar.activation(c.w_hi[:, n % RING, :], c.raw[:, n % RING, :],
                                     ACT.Copy).then_inc(c.hi_ready.sem, 1)

        def lo_units(dve, i, ms):
            for m in ms:
                n = first + m
                if i is None:
                    c.split_lo(dve, n)
                    continue
                dve.wait_ge(c.hi_ready.sem, i * RING + n + 1)
                nc.vector.tensor_tensor(c.w_lo[:, n % RING, :], c.raw[:, n % RING, :],
                                        c.w_hi[:, n % RING, :].bitcast(F32),
                                        ALU.subtract).then_inc(c.lo_ready.sem, 1)

        def step_value(signal, i, k):
            return signal.at(k) if i is None else i * 2 + signal.at(k)

        def gate_unit(t):
            return 3 * t - 1 if t else 0

        def used_value(i, m):
            return first + m + 1 if i is None else i * RING + (first + m + 1)

        def act_step(act, i, t):
            if t >= 1:
                hi_units(act, i, (3 * t + 2, 3 * t + 3, 3 * t + 4))
            act.wait_ge(c.unit_used.sem, used_value(i, gate_unit(t)))
            if t >= 2:
                act.wait_ge(c.gated_ready.sem, step_value(c.gated_ready, i, t - 1))
            nc.scalar.activation(c.silu[:, t % 2, :], gate[t % 2][:, 0:S], ACT.Silu).then_inc(
                c.silu_ready.sem, 1)

        @block.scalar
        def _(act):
            join.scalar(act)
            act_step(act, None, 0)
            act_step(act, None, 1)
            with act.Fori(0, LOOPS) as i:
                act_step(act, i, 2)
                act_step(act, i, 3)
            hi_units(act, None, (3 * FT + 2, 3 * FT + 3, 3 * FT + 4))

        def dve_step(dve, i, t):
            if t >= 1:
                lo_units(dve, i, (3 * t + 2, 3 * t + 3, 3 * t + 4))
            dve.wait_ge(c.unit_used.sem, used_value(i, gate_unit(t) + 1))
            dve.wait_ge(c.silu_ready.sem, step_value(c.silu_ready, i, t + 1))
            p = t % 2
            nc.vector.tensor_tensor(c.gated[:, p, :], c.silu[:, p, :], up[p][:, 0:S],
                                    ALU.mult).then_inc(c.prod_made.sem, 1)
            dve.wait_ge(c.prod_made.sem, step_value(c.prod_made, i, t + 1))
            if t >= 2:
                dve.wait_ge(c.unit_used.sem, used_value(i, 3 * (t - 2) + 4))
            nc.vector.tensor_copy(c.g_hi[:, p, :], c.gated[:, p, :]).then_inc(c.prod_hi.sem, 1)
            dve.wait_ge(c.prod_hi.sem, step_value(c.prod_hi, i, t + 1))
            nc.vector.tensor_tensor(c.g_lo[:, p, :], c.gated[:, p, :], c.g_hi[:, p, :].bitcast(F32),
                                    ALU.subtract).then_inc(c.gated_ready.sem, 1)

        @block.vector
        def _(dve):
            join.vector(dve)
            dve_step(dve, None, 0)
            dve_step(dve, None, 1)
            with dve.Fori(0, LOOPS) as i:
                dve_step(dve, i, 2)
                dve_step(dve, i, 3)
            lo_units(dve, None, (3 * FT + 2, 3 * FT + 3, 3 * FT + 4))

        def unit_there(pe, i, m):
            n = first + m
            pe.wait_ge(c.lo_ready.sem, n + 1 if i is None else i * RING + n + 1)

        def hidden(pe, i, m, out):
            s = slot(m)
            unit_there(pe, i, m)
            for k in range(KT):
                if i is None and m == 0:
                    join.tile_there(pe, k)
                w = slice(k * P, (k + 1) * P)
                last = three_products(nc, out[:, 0:S], c.w_hi[:, s, w], c.w_lo[:, s, w],
                                      c.act_hi[:, k, :], c.act_lo[:, k, :], k == 0, k == KT - 1)
            last.then_inc(c.unit_used.sem, 1)

        def add_down(pe, i, f, m, begin=False, end=False):
            s = slot(m)
            unit_there(pe, i, m)
            pe.wait_ge(c.gated_ready.sem, step_value(c.gated_ready, i, f + 1))
            for t in range(NT):
                tok = slice(t * P, (t + 1) * P)
                for h in range(2):
                    w = slice(h * HALF, (h + 1) * HALF)
                    last = three_products(nc, down[2 * t + h][:, :], c.g_hi[:, f % 2, tok],
                                          c.g_lo[:, f % 2, tok], c.w_hi[:, s, w], c.w_lo[:, s, w],
                                          begin, end)
            last.then_inc(c.unit_used.sem, 1)

        def pe_step(pe, i, t):
            m = gate_unit(t)
            if t >= 2:
                pe.wait_ge(c.silu_ready.sem, step_value(c.silu_ready, i, t - 1))
            hidden(pe, i, m, gate[t % 2])
            if t >= 2:
                pe.wait_ge(c.prod_made.sem, step_value(c.prod_made, i, t - 1))
            hidden(pe, i, m + 1, up[t % 2])
            if t >= 1:
                add_down(pe, i, t - 1, m + 2, begin=t == 1)

        @block.tensor
        def _(pe):
            join.tensor(pe)
            pe_step(pe, None, 0)
            pe_step(pe, None, 1)
            with pe.Fori(0, LOOPS) as i:
                pe_step(pe, i, 2)
                pe_step(pe, i, 3)
            add_down(pe, None, FT - 1, count - 1, end=True)

        @block.gpsimd
        def _(pool):
            join.gpsimd(pool)
    join.end()
    c.end_stage(count, (c.silu_ready, FT), (c.gated_ready, FT), (c.prod_made, FT), (c.prod_hi, FT))


def finish_stage(c, scale, sources, normed=False):
    nc = c.nc
    gain = c.gain_row
    parts = c.small[:, 0:2 * NT]
    rstd = c.small[:, 2 * NT:3 * NT]
    half = c.const[:, 128:128 + NT]
    quads = [(t, h) for t in range(NT) for h in range(2)]

    def piece(unit, t, h):
        return c.work[:, unit + t, h * HALF:(h + 1) * HALF]

    def xs(t, h):
        return c.x[:, t, h * HALF:(h + 1) * HALF]

    with nc.Block() as block:
        if not normed:
            @block.vector
            def _(dve):
                for t, h in quads:
                    nc.vector.scalar_tensor_tensor(xs(t, h), sources(t, h), scale, xs(t, h),
                                                   ALU.mult, ALU.add)
        else:
            @block.scalar
            def _(act):
                for q, (t, h) in enumerate(quads):
                    last = nc.scalar.activation(piece(16, t, h), sources(t, h), ACT.Square,
                                                scale=float(D) ** -0.5 / scale,
                                                accum_out=parts[:, q:q + 1])
                last.then_inc(c.act_to_dve.sem, 1)

            @block.vector
            def _(dve):
                dve.wait_ge(c.act_to_dve.sem, c.act_to_dve.at(1))
                nc.vector.scalar_tensor_tensor(rstd, parts[:, 0:2 * NT:2], EPS / scale ** 2,
                                               parts[:, 1:2 * NT:2], ALU.add, ALU.add).then_inc(
                                                   c.dve_to_pool.sem, 1)
                dve.wait_ge(c.pool_to_dve.sem, c.pool_to_dve.at(1))
                dve.wait_ge(c.row_in.sem, 16 * c.gain_loads)
                for t, h in quads:
                    last = nc.vector.scalar_tensor_tensor(
                        piece(14, t, h), sources(t, h), rstd[:, t:t + 1],
                        gain[:, h * HALF:(h + 1) * HALF], ALU.mult, ALU.mult)
                c.dve_order.link(dve, last)
                for t, h in quads:
                    nc.vector.tensor_tensor(xs(t, h), xs(t, h), piece(14, t, h), ALU.add)

            @block.gpsimd
            def _(pool):
                pool.wait_ge(c.dve_to_pool.sem, c.dve_to_pool.at(1))
                nc.gpsimd.tensor_tensor(rstd, rstd, half, ALU.pow).then_inc(c.pool_to_dve.sem, 1)
    if normed:
        c.end_stage(0, (c.act_to_dve, 1), (c.dve_to_pool, 1), (c.pool_to_dve, 1))


def store_stage(c, out):
    with c.nc.Block() as block:
        @block.sync
        def _(sp):
            sp.dma_start(out.rearrange("(t p) d -> p t d", p=P), c.x[:, :, :]).then_inc(
                c.stored.sem, 16)
            sp.wait_ge(c.stored.sem, 16)


def banks(c):
    return lambda t, h: c.bank[2 * t + h][:, :]


def product_b(c, pe, m, out):
    n = c.first_unit + m
    pe.wait_ge(c.lo_ready.sem, n + 1)
    for k in range(KT):
        w = slice(k * P, (k + 1) * P)
        last = three_products(c.nc, out[:, 0:S], c.w_hi[:, n % RING, w], c.w_lo[:, n % RING, w],
                              c.act_hi[:, k, :], c.act_lo[:, k, :], k == 0, k == KT - 1)
    last.then_inc(c.unit_used.sem, 1)


def product_a(c, pe, m, k, count, outs, tile0=0):
    n = c.first_unit + m
    pe.wait_ge(c.lo_ready.sem, n + 1)
    for t in range(NT):
        tok = slice(t * P, (t + 1) * P)
        for j in range(2):
            a = tile0 + 2 * k + j
            w = slice(j * HALF, (j + 1) * HALF)
            last = three_products(c.nc, outs[t][:, :], c.act_hi[:, a, tok], c.act_lo[:, a, tok],
                                  c.w_hi[:, n % RING, w], c.w_lo[:, n % RING, w],
                                  k == 0 and j == 0, k == count - 1 and j == 1)
    last.then_inc(c.unit_used.sem, 1)


def unit_done(c, eng, m):
    eng.wait_ge(c.unit_used.sem, c.first_unit + m + 1)


def project_stage(c, tiles, tile0, next_gain=None):
    per = tiles // 2
    count = 2 * per
    with c.nc.Block() as block:
        @block.sync
        def _(sp):
            c.load_gain(sp, next_gain)
            c.stream_stage_loads(sp, count)

        @block.scalar
        def _(act):
            for m in range(count):
                c.split_hi(act, c.first_unit + AHEAD + m)

        @block.vector
        def _(dve):
            for m in range(count):
                c.split_lo(dve, c.first_unit + AHEAD + m)

        @block.tensor
        def _(pe):
            for h in range(2):
                for k in range(per):
                    product_a(c, pe, h * per + k, k, per, [c.bank[h], c.bank[2 + h]], tile0)
    c.end_stage(count)


def ple_stage(c, join, i, next_gain):
    nc = c.nc
    count = 10
    pt = c.work[:, 4, 0:2 * S].rearrange("p (k s) -> p k s", k=2)
    counts = {"p_in": 16, "p_hi": 1, "p_lo": 1, "gate": 4}
    s = c.signals("ple_", counts)
    with nc.Block() as block:
        @block.sync
        def _(sp):
            c.load_gain(sp, next_gain)
            sp.dma_start(pt, c.dram["pt"][i, :, :, :]).then_inc(s["p_in"].sem, 16)
            c.stream_stage_loads(sp, count)

        @block.scalar
        def _(act):
            join.scalar(act)
            act.wait_ge(s["p_in"].sem, s["p_in"].at(16))
            nc.scalar.activation(c.act_hi[:, KT:KT + 2, :], pt, ACT.Copy).then_inc(s["p_hi"].sem, 1)
            for m in range(count + 1):
                if m < count:
                    c.split_hi(act, c.first_unit + AHEAD + m)
                if m in (4, 8):
                    h = m // 4 - 1
                    unit_done(c, act, m - 1)
                    for t in range(NT):
                        nc.scalar.activation(c.work[:, t, h * HALF:(h + 1) * HALF],
                                             c.bank[2 * t + h][:, :], ACT.Sigmoid).then_inc(s["gate"].sem, 1)

        @block.vector
        def _(dve):
            join.vector(dve)
            dve.wait_ge(s["p_hi"].sem, s["p_hi"].at(1))
            nc.vector.tensor_tensor(c.act_lo[:, KT:KT + 2, :], pt,
                                    c.act_hi[:, KT:KT + 2, :].bitcast(F32),
                                    ALU.subtract).then_inc(s["p_lo"].sem, 1)
            for m in range(count):
                c.split_lo(dve, c.first_unit + AHEAD + m)
            for h in range(2):
                unit_done(c, dve, 8 + h)
                dve.wait_ge(s["gate"].sem, s["gate"].at(2 * (h + 1)))
                for t in range(NT):
                    g = c.work[:, t, h * HALF:(h + 1) * HALF]
                    nc.vector.tensor_tensor(g, g, c.bank[4 + 2 * t + h][:, :], ALU.mult)

        @block.gpsimd
        def _(pool):
            join.gpsimd(pool)

        @block.tensor
        def _(pe):
            join.tensor(pe)
            join.tile_there(pe, KT - 1)
            for h in range(2):
                for k in range(4):
                    product_a(c, pe, h * 4 + k, k, 4, [c.bank[h], c.bank[2 + h]])
            pe.wait_ge(s["p_lo"].sem, s["p_lo"].at(1))
            for h in range(2):
                product_a(c, pe, 8 + h, 0, 1, [c.bank[4 + h], c.bank[6 + h]], KT)
    join.end()
    c.end_stage(count)
    c.end_signals(s, counts)


def gmlp_in_stage(c, join, rows, bias_col):
    nc = c.nc
    v = c.work[:, 0:4, :].rearrange("p (t a) n -> p t (a n)", t=NT)
    bias = c.work[:, 4:6, :].rearrange("p a n -> p (a n)")
    u = c.work[:, 6:10, :].rearrange("p a (b s) -> p (a b) s", s=S)
    stats = c.small[:, 0:48].rearrange("p (t q s) -> p t q s", t=NT, q=4)
    mv = c.small[:, 48:52].rearrange("p (t s) -> p t s", t=NT)
    ve = c.small[:, 52:54]
    rstd = c.small[:, 54:56]
    half = c.const[:, 128:130]
    b_in, v_biased, v_made, u_made, var_made, rstd_made = (
        c.new_signal("gmlp_" + n) for n in ("b_in", "v_biased", "v_made", "u_made", "var", "rstd"))
    count = 32
    UT = 16

    def chunk(t, n):
        return v[:, t, n * HALF:(n + 1) * HALF]

    with nc.Block() as block:
        @block.sync
        def _(sp):
            for a in range(2):
                sp.dma_start(c.work[:, 4 + a, :], c.dram["rows"][rows + a, :, :]).then_inc(b_in.sem, 16)
            c.stream_stage_loads(sp, count)

        @block.scalar
        def _(act):
            join.scalar(act)
            for m in range(count + 1):
                if m < count:
                    c.split_hi(act, c.first_unit + AHEAD + m)
                if m in (4, 8, 12, 16):
                    n = m // 4 - 1
                    act.wait_ge(v_biased.sem, n + 1)
                    for t in range(NT):
                        last = nc.scalar.activation(chunk(t, n), chunk(t, n), ACT.Gelu_apprx_tanh)
                    last.then_inc(v_made.sem, 1)
                if m > 16:
                    i = m - 17
                    unit_done(c, act, m - 1)
                    nc.scalar.activation(u[:, i, :], c.bank[4 + i % 4][:, 0:S], ACT.Gelu_apprx_tanh,
                                         bias=c.cols[:, bias_col + i:bias_col + i + 1]).then_inc(
                                             u_made.sem, 1)

        @block.vector
        def _(dve):
            join.vector(dve)
            dve.wait_ge(b_in.sem, 32)
            for m in range(count + 1):
                if m < count:
                    c.split_lo(dve, c.first_unit + AHEAD + m)
                if m in (4, 8, 12, 16):
                    n = m // 4 - 1
                    unit_done(c, dve, m - 1)
                    for t in range(NT):
                        last = nc.vector.tensor_tensor(chunk(t, n), c.bank[2 * t + n % 2][:, :],
                                                       bias[:, n * HALF:(n + 1) * HALF], ALU.add)
                    last.then_inc(v_biased.sem, 1)
                if m in (6, 10, 14, 18):
                    n = (m - 6) // 4
                    dve.wait_ge(v_made.sem, n + 1)
                    for t in range(NT):
                        last = nc.vector.bn_stats(stats[:, t, n, :], chunk(t, n))
                if m == 18:
                    c.dve_order.link(dve, last)
                    for t in range(NT):
                        last = nc.vector.bn_aggr(mv[:, t, :], stats[:, t, :, :])
                    c.dve_order.link(dve, last)
                    nc.vector.tensor_scalar(ve, mv[:, :, 1], 1e-5, None, ALU.add).then_inc(var_made.sem, 1)
                if m == 20:
                    dve.wait_ge(rstd_made.sem, 1)
                    for t in range(NT):
                        nc.vector.tensor_scalar(v[:, t, :], v[:, t, :], mv[:, t, 0:1], rstd[:, t:t + 1],
                                                ALU.subtract, ALU.mult)

        @block.gpsimd
        def _(pool):
            join.gpsimd(pool)
            pool.wait_ge(var_made.sem, 1)
            nc.gpsimd.tensor_tensor(rstd, ve, half, ALU.pow).then_inc(rstd_made.sem, 1)

        @block.tensor
        def _(pe):
            join.tensor(pe)
            join.tile_there(pe, KT - 1)
            for n in range(4):
                if n >= 2:
                    pe.wait_ge(v_biased.sem, n - 1)
                for k in range(4):
                    product_a(c, pe, 4 * n + k, k, 4, [c.bank[n % 2], c.bank[2 + n % 2]])
            for i in range(UT):
                if i >= 4:
                    pe.wait_ge(u_made.sem, i - 3)
                product_b(c, pe, 16 + i, c.bank[4 + i % 4])
    join.end()
    c.end_stage(count)


def gmlp_mix_stage(c, bs_row, gain_col):
    nc = c.nc
    UT = 16
    v = c.work[:, 0:4, :].rearrange("p (t a) n -> p t (a n)", t=NT)
    u = c.work[:, 6:10, :].rearrange("p a (b s) -> p (a b) s", s=S)
    ws = c.work[:, 10, :].rearrange("p (g i) -> p g i", g=8)
    bs = c.work[:, 11, :].rearrange("p (g i) -> p g i", g=8)
    mixed = c.work[:, 12:16, :].rearrange("p a (b s) -> p (a b) s", s=S)
    ws_in, bs_in, masked, product, scaled, y_made, y_hi = (
        c.new_signal("mix_" + n) for n in ("ws_in", "bs_in", "masked", "product", "scaled", "y", "y_hi"))
    with nc.Block() as block:
        @block.sync
        def _(sp):
            sp.dma_start(ws, c.dram["ws"][:, :, :]).then_inc(ws_in.sem, 16)
            sp.dma_start(c.work[:, 11, :], c.dram["rows"][bs_row, :, :]).then_inc(bs_in.sem, 16)

        @block.gpsimd
        def _(pool):
            pool.wait_ge(ws_in.sem, 16)
            nc.gpsimd.memset(ws[64:128, :, 0:64], 0.0).then_inc(masked.sem, 1)

        @block.tensor
        def _(pe):
            pe.wait_ge(masked.sem, 1)
            for q in range(UT):
                if q >= 8:
                    pe.wait_ge(scaled.sem, q - 7)
                for t in range(NT):
                    last = nc.tensor.matmul(c.bank[q % 8][:, t * P:(t + 1) * P],
                                            v[:, t, q * P:(q + 1) * P], ws[:, q // 2, :],
                                            start=True, stop=True)
                last.then_inc(product.sem, 1)

        @block.vector
        def _(dve):
            dve.wait_ge(bs_in.sem, 16)
            for q in range(UT + 2):
                if q < UT:
                    dve.wait_ge(product.sem, q + 1)
                    nc.vector.scalar_tensor_tensor(
                        mixed[:, q, :].rearrange("p (t i) -> p t i", t=NT),
                        c.bank[q % 8][:, 0:S].rearrange("p (t i) -> p t i", t=NT),
                        c.cols[:, gain_col + q:gain_col + q + 1],
                        bs[:, q // 2:q // 2 + 1, :].to_broadcast([P, NT, P]),
                        ALU.mult, ALU.add).then_inc(scaled.sem, 1)
                if 1 <= q <= UT:
                    dve.wait_ge(scaled.sem, q)
                    nc.vector.tensor_tensor(u[:, q - 1, :], u[:, q - 1, :], mixed[:, q - 1, :],
                                            ALU.mult).then_inc(y_made.sem, 1)
                if q >= 2:
                    dve.wait_ge(y_hi.sem, q - 1)
                    nc.vector.tensor_tensor(c.act_lo[:, q - 2, :], u[:, q - 2, :],
                                            c.act_hi[:, q - 2, :].bitcast(F32), ALU.subtract)

        @block.scalar
        def _(act):
            for q in range(UT):
                act.wait_ge(y_made.sem, q + 1)
                nc.scalar.activation(c.act_hi[:, q, :], u[:, q, :], ACT.Copy).then_inc(y_hi.sem, 1)
    c.end_stage(0)


CONV_W = 31
PAD = CONV_W // 2
POOL_PAD = 8
C_IDENT, C_HALF, C_RCNT, C_MEAN = 0, 128, 384, 896


def mixer_buffers(c):
    class Buffers:
        pass

    b = Buffers()
    b.q, b.k, b.v = (c.work[:, i, :].rearrange("p (t n) -> p t n", t=NT) for i in range(3))
    b.zpad = c.work[:, 3, 0:2 * (S + 2 * PAD)].rearrange("p (i s) -> p i s", i=2)
    b.sig = c.work[:, 4, 0:2 * S].rearrange("p (i s) -> p i s", i=2)
    b.conv = c.work[:, 4, 2 * S:4 * S].rearrange("p (i s) -> p i s", i=2)
    b.upad, b.sum2, b.sum4, b.sum8 = (
        c.work[:, i, 0:2 * (S + 2 * POOL_PAD)].rearrange("p (i s) -> p i s", i=2) for i in range(5, 9))
    b.diff = c.work[:, 9, 0:2 * S].rearrange("p (i s) -> p i s", i=2)
    b.poolw = c.work[:, 9, 2 * S:3 * S].rearrange("p (i d) -> p i d", i=2)
    return b


def mixer_in_stage(c, join, layer, conv_col, conv_bias_col):
    nc = c.nc
    b = mixer_buffers(c)
    count = 18
    counts = {"sig": 2, "z": 2, "conv_step": 2 * CONV_W, "pool": 2, "qkv": 3, "zeroed": 1,
              "zero_z": 1, "poolw": 32}
    s = c.signals("in_", counts)

    with nc.Block() as block:
        @block.sync
        def _(sp):
            sp.dma_start(b.poolw, c.dram["poolw"][layer, :, :, :]).then_inc(s["poolw"].sem, 16)
            sp.dma_start(c.work[:, 19, 0:2 * S], c.dram["dist"][:, :]).then_inc(s["poolw"].sem, 16)
            c.stream_stage_loads(sp, count)
            sp.wait_ge(s["poolw"].sem, s["poolw"].at(32))

        @block.scalar
        def _(act):
            join.scalar(act)
            for m in range(count + 1):
                if m < count:
                    c.split_hi(act, c.first_unit + AHEAD + m)
                if m in (2, 4):
                    i = m // 2 - 1
                    unit_done(c, act, m - 1)
                    nc.scalar.activation(b.sig[:, i, :], c.bank[m - 1][:, 0:S], ACT.Sigmoid).then_inc(s["sig"].sem, 1)
                if m in (5, 6):
                    i = m - 5
                    unit_done(c, act, m - 1)
                    act.wait_ge(s["zeroed"].sem, s["zeroed"].at(1))
                    nc.scalar.activation(b.upad[:, i, POOL_PAD:POOL_PAD + S], c.bank[m - 1][:, 0:S],
                                         ACT.Copy).then_inc(s["pool"].sem, 1)
                if m in (10, 14, 18):
                    i = (m - 10) // 4
                    unit_done(c, act, m - 1)
                    for t in range(NT):
                        last = nc.scalar.activation((b.q, b.k, b.v)[i][:, t, :],
                                                    c.bank[(6, 0, 2)[i] + t][:, :], ACT.Copy)
                    last.then_inc(s["qkv"].sem, 1)

        @block.vector
        def _(dve):
            join.vector(dve)
            nc.vector.memset(c.work[:, 3, 0:2 * (S + 2 * PAD)], 0.0).then_inc(s["zero_z"].sem, 1)
            steps = [(j, i) for j in range(CONV_W) for i in range(2)]
            done = 0
            for m in range(count):
                c.split_lo(dve, c.first_unit + AHEAD + m)
                if m in (2, 4):
                    i = m // 2 - 1
                    if i == 0:
                        dve.wait_ge(s["zero_z"].sem, s["zero_z"].at(1))
                    unit_done(c, dve, m - 2)
                    dve.wait_ge(s["sig"].sem, s["sig"].at(i + 1))
                    nc.vector.tensor_tensor(b.zpad[:, i, PAD:PAD + S], c.bank[m - 2][:, 0:S],
                                            b.sig[:, i, :], ALU.mult).then_inc(s["z"].sem, 1)
                if m >= 5:
                    for j, i in steps[5 * (m - 5):5 * (m - 4)]:
                        if done == 0:
                            dve.wait_ge(s["z"].sem, s["z"].at(2))
                        if done >= 2:
                            dve.wait_ge(s["conv_step"].sem, s["conv_step"].at(done - 1))
                        tap = c.cols[:, conv_col + 2 * j + i:conv_col + 2 * j + i + 1]
                        if j == 0:
                            ins = nc.vector.tensor_scalar(
                                b.conv[:, i, :], b.zpad[:, i, 0:S], tap,
                                c.cols[:, conv_bias_col + i:conv_bias_col + i + 1], ALU.mult, ALU.add)
                        else:
                            ins = nc.vector.scalar_tensor_tensor(
                                b.conv[:, i, :], b.zpad[:, i, j:j + S], tap, b.conv[:, i, :],
                                ALU.mult, ALU.add)
                        ins.then_inc(s["conv_step"].sem, 1)
                        done += 1
            assert done == 2 * CONV_W

        @block.gpsimd
        def _(pool):
            join.gpsimd(pool)
            nc.gpsimd.memset(c.work[:, 5, 0:2 * (S + 2 * POOL_PAD)], 0.0).then_inc(s["zeroed"].sem, 1)
            pool.wait_ge(s["pool"].sem, s["pool"].at(2))
            order = c.pool_order
            for dst, src, lo, hi, shift in ((b.sum2, b.upad, 1, 272, (1, 0)), (b.sum4, b.sum2, 2, 270, (1, 1)),
                                            (b.sum8, b.sum4, 4, 268, (2, 2))):
                order.link(pool, nc.gpsimd.tensor_tensor(
                    dst[:, :, lo:hi], src[:, :, lo - shift[0]:hi - shift[0]],
                    src[:, :, lo + shift[1]:hi + shift[1]], ALU.add))
            w = slice(POOL_PAD, POOL_PAD + S)
            rcnt = c.const[:, C_RCNT:C_RCNT + 2 * S].rearrange("p (i s) -> p i s", i=2)
            for rows, i, src in ((slice(0, 64), 0, b.sum2), (slice(64, 128), 0, b.sum4),
                                 (slice(0, 64), 1, b.sum8)):
                nc.gpsimd.tensor_tensor(b.diff[rows, i, :], src[rows, i, w], rcnt[rows, i, :], ALU.mult)
            order.link(pool, nc.gpsimd.tensor_tensor(
                b.diff[64:128, 1, :], b.sum8[64:128, 1, POOL_PAD - 4:POOL_PAD - 4 + S],
                b.sum8[64:128, 1, POOL_PAD + 4:POOL_PAD + 4 + S], ALU.add))
            order.link(pool, nc.gpsimd.tensor_tensor(b.diff[64:128, 1, :], b.diff[64:128, 1, :],
                                                     rcnt[64:128, 1, :], ALU.mult))
            nc.gpsimd.tensor_tensor(b.diff, b.diff, b.upad[:, :, w], ALU.subtract)

        @block.tensor
        def _(pe):
            join.tensor(pe)
            join.tile_there(pe, KT - 1)
            for m in range(6):
                product_b(c, pe, m, c.bank[m])
            for i in range(3):
                if i == 1:
                    pe.wait_ge(s["z"].sem, s["z"].at(1))
                if i == 2:
                    pe.wait_ge(s["z"].sem, s["z"].at(2))
                first = (6, 0, 2)[i]
                for k in range(4):
                    product_a(c, pe, 6 + 4 * i + k, k, 4, [c.bank[first], c.bank[first + 1]])
    join.end()
    c.end_stage(count)
    c.end_signals(s, counts)


def attention_stage(c, layer, qn_col, kn_col, sub_col, lam_col, pool_scale_col, ln_col, lambda_init):
    nc = c.nc
    b = mixer_buffers(c)
    counts = {"lam_sum": 1, "lam_exp": 1, "sq_sum": 1, "qk_rstd": 2, "qk_scaled": 2,
              "qkT": 8, "kT_made": 4, "qT_made": 4, "score": 8, "biased": 8,
              "maxed": 8, "probs": 8, "mixed": 4, "aT_bank": 4, "aT_made": 4,
              "out_bank": 1, "o_ms": 1, "o_rstd": 1, "o_scaled": 1, "oT": 4,
              "oT_hi": 4, "pool_bank": 1, "pool_hi": 3, "mean": 1,
              "centred": 2, "squared": 1, "var": 1, "var_eps": 1, "ln_rstd": 1,
              "normed": 1, "conv_y": 2, "conv_hi": 1, "sub_ready": 1}
    s = c.signals("attn_", counts)
    sq = c.work[:, 5:7, :]
    qT = c.work[:, 10, :].rearrange("p (h s) -> p h s", h=AH)
    kT = c.work[:, 11, :].rearrange("p (h s) -> p h s", h=AH)
    sc = c.work[:, 12:16, :].rearrange("p a (b n) -> p (a b) n", b=2)
    aT = c.work[:, 16:18, :].rearrange("p a (b n) -> p (a b) n", b=2)
    o = c.work[:, 18, :].rearrange("p (t n) -> p t n", t=NT)
    osq = c.work[:, 12, :].rearrange("p (t n) -> p t n", t=NT)
    ln = c.work[:, 7, :].rearrange("p (i s) -> p i s", i=4)
    ln2 = c.work[:, 8, :].rearrange("p (i s) -> p i s", i=4)
    dist = c.work[:, 19, 0:2 * S]
    meanw = c.const[:, C_MEAN:C_MEAN + P]
    sm = c.small
    qk_ms, qk_rstd = sm[:, 0:32], sm[:, 32:64]
    nmax, total, recip = sm[:, 64:80], sm[:, 80:96], sm[:, 96:112]
    lam2, lam_e, lam = sm[:, 112:114], sm[:, 114:116], sm[:, 116:117]
    o_ms, o_rstd = sm[:, 120:128], sm[:, 128:136]
    subg = sm[:, 136:137]
    lam_v = sm[:, 256:384]
    half = c.const[:, C_HALF:C_HALF + S]
    order = c.dve_order
    slopes = [2.0 ** (-8.0 * (h + 1) / AH) for h in range(AH)]

    with nc.Block() as block:
        @block.tensor
        def _(pe):
            for i in range(2):
                last = nc.tensor.matmul(c.bank[7][:, i * S:(i + 1) * S], b.poolw[:, i, :], b.diff[:, i, :],
                                        start=True, stop=True)
            last.then_inc(s["pool_bank"].sem, 1)
            for i in range(2):
                last = nc.tensor.matmul(c.bank[6][:, 0:S], meanw, b.conv[:, i, :], start=i == 0, stop=i == 1)
            last.then_inc(s["mean"].sem, 1)
            pe.wait_ge(s["qk_scaled"].sem, s["qk_scaled"].at(1))
            for h in range(AH):
                for t in range(NT):
                    last = nc.tensor.transpose(c.bank[h][:, t * P:(t + 1) * P],
                                               b.q[:, t, h * P:(h + 1) * P], c.ident)
                last.then_inc(s["qkT"].sem, 1)
            pe.wait_ge(s["qk_scaled"].sem, s["qk_scaled"].at(2))
            for h in range(AH):
                if h == 2:
                    pe.wait_ge(s["centred"].sem, s["centred"].at(2))
                if h == 3:
                    pe.wait_ge(s["pool_hi"].sem, s["pool_hi"].at(3))
                for t in range(NT):
                    last = nc.tensor.transpose(c.bank[4 + h][:, t * P:(t + 1) * P],
                                               b.k[:, t, h * P:(h + 1) * P], c.ident)
                last.then_inc(s["qkT"].sem, 1)
            pe.wait_ge(s["qT_made"].sem, s["qT_made"].at(AH))
            pe.wait_ge(s["kT_made"].sem, s["kT_made"].at(AH))
            for u in range(2 * AH):
                h, g = u // 2, u % 2
                rows = slice(g * HD, (g + 1) * HD)
                for t in range(NT):
                    last = nc.tensor.matmul(c.bank[u][:, t * S:(t + 1) * S], qT[rows, h, t * P:(t + 1) * P],
                                            kT[rows, h, :], start=True, stop=True)
                last.then_inc(s["score"].sem, 1)
            pe.wait_ge(s["biased"].sem, s["biased"].at(8))
            pe.wait_ge(s["squared"].sem, s["squared"].at(1))
            for i in range(2):
                last = nc.tensor.matmul(c.bank[7][:, 0:S], meanw, ln[:, 2 + i, :], start=i == 0, stop=i == 1)
            last.then_inc(s["var"].sem, 1)
            for h in range(AH):
                pe.wait_ge(s["mixed"].sem, s["mixed"].at(h + 1))
                for kt in range(NT):
                    for t in range(NT):
                        last = nc.tensor.transpose(c.bank[h][:, kt * S + t * P:kt * S + (t + 1) * P],
                                                   sc[:, 2 * h, t * S + kt * P:t * S + (kt + 1) * P], c.ident)
                last.then_inc(s["aT_bank"].sem, 1)
            for h in range(AH):
                pe.wait_ge(s["aT_made"].sem, s["aT_made"].at(h + 1))
                for t in range(NT):
                    for kt in range(NT):
                        last = nc.tensor.matmul(c.bank[4 + t][:, h * P:(h + 1) * P],
                                                aT[:, h, kt * S + t * P:kt * S + (t + 1) * P],
                                                b.v[:, kt, h * P:(h + 1) * P], start=kt == 0, stop=kt == 1)
            last.then_inc(s["out_bank"].sem, 1)
            pe.wait_ge(s["o_scaled"].sem, s["o_scaled"].at(1))
            for h in range(AH):
                for t in range(NT):
                    last = nc.tensor.transpose(c.bank[h][:, t * P:(t + 1) * P],
                                               o[:, t, h * P:(h + 1) * P], c.ident)
                last.then_inc(s["oT"].sem, 1)

        @block.scalar
        def _(act):
            act.wait_ge(s["pool_bank"].sem, s["pool_bank"].at(1))
            for i in range(2):
                nc.scalar.activation(c.act_hi[:, KT + 2 + i, :], c.bank[7][:, i * S:(i + 1) * S], ACT.Copy,
                                     scale=c.cols[:, pool_scale_col + i:pool_scale_col + i + 1]).then_inc(s["pool_hi"].sem, 1)
            act.wait_ge(s["lam_sum"].sem, s["lam_sum"].at(1))
            nc.scalar.activation(lam_e, lam2, ACT.Exp).then_inc(s["lam_exp"].sem, 1)
            act.wait_ge(s["centred"].sem, s["centred"].at(2))
            nc.scalar.activation(ln[:, 2:4, :], ln[:, 0:2, :], ACT.Square).then_inc(s["squared"].sem, 1)
            for h in range(AH):
                act.wait_ge(s["qkT"].sem, s["qkT"].at(AH + h + 1))
                nc.scalar.activation(kT[:, h, :], c.bank[4 + h][:, 0:S], ACT.Copy,
                                     scale=c.cols[:, kn_col:kn_col + 1]).then_inc(s["kT_made"].sem, 1)
            for u in range(2 * AH):
                act.wait_ge(s["maxed"].sem, s["maxed"].at(u + 1))
                for t in range(NT):
                    part = sc[:, u, t * S:(t + 1) * S]
                    last = nc.scalar.activation(part, part, ACT.Exp, bias=nmax[:, 2 * u + t:2 * u + t + 1],
                                                accum_out=total[:, 2 * u + t:2 * u + t + 1])
                last.then_inc(s["probs"].sem, 1)
            for h in range(AH):
                act.wait_ge(s["aT_bank"].sem, s["aT_bank"].at(h + 1))
                nc.scalar.activation(aT[:, h, :], c.bank[h][:, :], ACT.Copy).then_inc(s["aT_made"].sem, 1)
            act.wait_ge(s["var_eps"].sem, s["var_eps"].at(1))
            nc.scalar.activation(ln2[:, 0, :], ln2[:, 1, :], ACT.Sqrt).then_inc(s["ln_rstd"].sem, 1)
            act.wait_ge(s["normed"].sem, s["normed"].at(1))
            for i in range(2):
                nc.scalar.activation(ln2[:, 2 + i, :], ln[:, i, :], ACT.Silu,
                                     scale=c.cols[:, ln_col + i:ln_col + i + 1],
                                     bias=c.cols[:, ln_col + 2 + i:ln_col + 3 + i]).then_inc(s["conv_y"].sem, 1)
            act.wait_ge(s["conv_y"].sem, s["conv_y"].at(2))
            nc.scalar.activation(c.act_hi[:, KT:KT + 2, :], ln2[:, 2:4, :], ACT.Copy).then_inc(s["conv_hi"].sem, 1)
            act.wait_ge(s["sub_ready"].sem, s["sub_ready"].at(1))
            for h in range(AH):
                act.wait_ge(s["oT"].sem, s["oT"].at(h + 1))
                nc.scalar.activation(c.act_hi[:, KT + 4 + h, :], c.bank[h][:, 0:S], ACT.Copy,
                                     scale=subg).then_inc(s["oT_hi"].sem, 1)

        @block.gpsimd
        def _(pool):
            pool.wait_ge(s["sq_sum"].sem, s["sq_sum"].at(1))
            for i in range(2):
                nc.gpsimd.tensor_tensor(qk_rstd[:, 16 * i:16 * (i + 1)], qk_ms[:, 16 * i:16 * (i + 1)],
                                        half[:, 0:16], ALU.pow).then_inc(s["qk_rstd"].sem, 1)
            pool.wait_ge(s["o_ms"].sem, s["o_ms"].at(1))
            nc.gpsimd.tensor_tensor(o_rstd, o_ms, half[:, 0:8], ALU.pow).then_inc(s["o_rstd"].sem, 1)

        def normalise(i):
            u = c.work[:, i, :].rearrange("p (g n) -> p g n", n=HD)
            nc.vector.tensor_tensor(
                u, u, qk_rstd[:, 16 * i:16 * (i + 1)].unsqueeze(2).to_broadcast([P, 16, HD]),
                ALU.mult).then_inc(s["qk_scaled"].sem, 1)

        @block.vector
        def _(dve):
            for i, x in enumerate((b.q, b.k)):
                last = nc.vector.tensor_tensor(sq[:, i, :], c.work[:, i, :], c.work[:, i, :], ALU.mult)
            order.link(dve, last)
            order.link(dve, nc.vector.tensor_reduce(
                qk_ms, sq.rearrange("p i (g n) -> p (i g) n", n=HD), AX.X, ALU.add))
            nc.vector.tensor_scalar(qk_ms, qk_ms, 1.0 / HD, EPS, ALU.mult, ALU.add).then_inc(s["sq_sum"].sem, 1)
            for i in range(2):
                last = nc.vector.tensor_tensor(
                    lam_v[:, i * HD:(i + 1) * HD], c.cols[:, lam_col + 2 * i * HD:lam_col + (2 * i + 1) * HD],
                    c.cols[:, lam_col + (2 * i + 1) * HD:lam_col + (2 * i + 2) * HD], ALU.mult)
            order.link(dve, last)
            nc.vector.tensor_reduce(lam2, lam_v.rearrange("p (i n) -> p i n", i=2), AX.X,
                                    ALU.add).then_inc(s["lam_sum"].sem, 1)
            nc.vector.tensor_scalar(subg, c.cols[:, sub_col:sub_col + 1], 1.0 - lambda_init, None,
                                    ALU.mult).then_inc(s["sub_ready"].sem, 1)
            dve.wait_ge(s["mean"].sem, s["mean"].at(1))
            for i in range(2):
                nc.vector.tensor_tensor(ln[:, i, :], b.conv[:, i, :], c.bank[6][:, 0:S],
                                        ALU.subtract).then_inc(s["centred"].sem, 1)
            dve.wait_ge(s["pool_hi"].sem, s["pool_hi"].at(2))
            for i in range(2):
                last = nc.vector.scalar_tensor_tensor(
                    c.act_lo[:, KT + 2 + i, :], c.bank[7][:, i * S:(i + 1) * S],
                    c.cols[:, pool_scale_col + i:pool_scale_col + i + 1],
                    c.act_hi[:, KT + 2 + i, :].bitcast(F32), ALU.mult, ALU.subtract)
            last.then_inc(s["pool_hi"].sem, 1)
            for i in range(2):
                dve.wait_ge(s["qk_rstd"].sem, s["qk_rstd"].at(i + 1))
                normalise(i)
            dve.wait_ge(s["lam_exp"].sem, s["lam_exp"].at(1))
            order.link(dve, nc.vector.tensor_tensor(lam, lam_e[:, 0:1], lam_e[:, 1:2], ALU.subtract))
            order.link(dve, nc.vector.tensor_scalar(lam, lam, lambda_init, None, ALU.add))
            for h in range(AH):
                dve.wait_ge(s["qkT"].sem, s["qkT"].at(h + 1))
                nc.vector.tensor_scalar(qT[:, h, :], c.bank[h][:, 0:S], c.cols[:, qn_col:qn_col + 1],
                                        float(HD) ** -0.5, ALU.mult, ALU.mult).then_inc(s["qT_made"].sem, 1)
            for u in range(2 * AH + 1):
                if u < 2 * AH:
                    dve.wait_ge(s["score"].sem, s["score"].at(u + 1))
                    nc.vector.scalar_tensor_tensor(sc[:, u, :], dist, -slopes[u // 2], c.bank[u][:, :],
                                                   ALU.mult, ALU.add).then_inc(s["biased"].sem, 1)
                if u:
                    dve.wait_ge(s["biased"].sem, s["biased"].at(u))
                    nc.vector.tensor_reduce(nmax[:, 2 * u - 2:2 * u],
                                            sc[:, u - 1, :].rearrange("p (t n) -> p t n", t=NT), AX.X,
                                            ALU.max, negate=True).then_inc(s["maxed"].sem, 1)
            dve.wait_ge(s["var"].sem, s["var"].at(1))
            nc.vector.tensor_scalar(ln2[:, 1, :], c.bank[7][:, 0:S], EPS, None, ALU.add).then_inc(s["var_eps"].sem, 1)
            for h in range(AH):
                dve.wait_ge(s["probs"].sem, s["probs"].at(2 * h + 2))
                r = slice(4 * h, 4 * h + 4)
                order.link(dve, nc.vector.reciprocal(recip[:, r], total[:, r]))
                order.link(dve, nc.vector.tensor_scalar(
                    recip[:, 4 * h + 2:4 * h + 4], recip[:, 4 * h + 2:4 * h + 4], lam, None, ALU.mult))
                for t in range(NT):
                    last = nc.vector.tensor_scalar(
                        sc[:, 2 * h + 1, t * S:(t + 1) * S], sc[:, 2 * h + 1, t * S:(t + 1) * S],
                        recip[:, 4 * h + 2 + t:4 * h + 3 + t], None, ALU.mult)
                order.link(dve, last)
                for t in range(NT):
                    last = nc.vector.scalar_tensor_tensor(
                        sc[:, 2 * h, t * S:(t + 1) * S], sc[:, 2 * h, t * S:(t + 1) * S],
                        recip[:, 4 * h + t:4 * h + 1 + t], sc[:, 2 * h + 1, t * S:(t + 1) * S],
                        ALU.mult, ALU.subtract)
                last.then_inc(s["mixed"].sem, 1)
            dve.wait_ge(s["ln_rstd"].sem, s["ln_rstd"].at(1))
            order.link(dve, nc.vector.reciprocal(ln2[:, 0, :], ln2[:, 0, :]))
            for i in range(2):
                last = nc.vector.tensor_tensor(ln[:, i, :], ln[:, i, :], ln2[:, 0, :], ALU.mult)
            last.then_inc(s["normed"].sem, 1)
            dve.wait_ge(s["out_bank"].sem, s["out_bank"].at(1))
            for t in range(NT):
                last = nc.vector.tensor_copy(o[:, t, :], c.bank[4 + t][:, :])
            order.link(dve, last)
            order.link(dve, nc.vector.tensor_tensor(osq, o, o, ALU.mult))
            order.link(dve, nc.vector.tensor_reduce(
                o_ms, c.work[:, 12, :].rearrange("p (g n) -> p g n", n=P), AX.X, ALU.add))
            nc.vector.tensor_scalar(o_ms, o_ms, 1.0 / P, EPS, ALU.mult, ALU.add).then_inc(s["o_ms"].sem, 1)
            dve.wait_ge(s["conv_hi"].sem, s["conv_hi"].at(1))
            nc.vector.tensor_tensor(c.act_lo[:, KT:KT + 2, :], ln2[:, 2:4, :],
                                    c.act_hi[:, KT:KT + 2, :].bitcast(F32), ALU.subtract)
            dve.wait_ge(s["o_rstd"].sem, s["o_rstd"].at(1))
            o8 = c.work[:, 18, :].rearrange("p (g n) -> p g n", n=P)
            nc.vector.tensor_tensor(o8, o8, o_rstd.unsqueeze(2).to_broadcast([P, 8, P]),
                                    ALU.mult).then_inc(s["o_scaled"].sem, 1)
            for h in range(AH):
                dve.wait_ge(s["oT_hi"].sem, s["oT_hi"].at(h + 1))
                nc.vector.scalar_tensor_tensor(c.act_lo[:, KT + 4 + h, :], c.bank[h][:, 0:S], subg,
                                               c.act_hi[:, KT + 4 + h, :].bitcast(F32), ALU.mult,
                                               ALU.subtract)
    c.end_signals(s, counts)


CHUNK = 64
PAIRS = HEADS // 2
R_STRICT, R_INCL = 384, 512
EXP_SCALE = -2.718281828459045 ** -0.5


def feature_view(units):
    return units.rearrange("p a (b s) -> p (a b) s", s=S)


def plain_norm_stage(c, gain_col):
    nc = c.nc
    ms = c.small[:, 0:NT]
    rstd = c.small[:, NT:2 * NT]
    half = c.const[:, 128:128 + NT]
    xn = c.work[:, 0:NT, :]
    junk = c.work[:, NT:2 * NT, :]
    hT = feature_view(c.work[:, 4:6, :])
    squares, rms, scaled, turned = (c.new_signal("plain_" + n) for n in ("squares", "rms", "scaled", "turned"))
    with nc.Block() as block:
        @block.scalar
        def _(act):
            for t in range(NT):
                last = nc.scalar.activation(junk[:, t, :], c.x[:, t, :], ACT.Square,
                                            scale=float(D) ** -0.5, accum_out=ms[:, t:t + 1])
            last.then_inc(squares.sem, 1)
            for k in range(0, KT, 2):
                act.wait_ge(turned.sem, k + 1)
                nc.scalar.activation(hT[:, k, :], c.bank[k][:, 0:S], ACT.Copy,
                                     scale=c.cols[:, gain_col + k:gain_col + k + 1])

        @block.gpsimd
        def _(pool):
            pool.wait_ge(squares.sem, 1)
            c.pool_order.link(pool, nc.gpsimd.tensor_scalar(ms, ms, EPS, None, ALU.add))
            nc.gpsimd.tensor_tensor(rstd, ms, half, ALU.pow).then_inc(rms.sem, 1)

        @block.vector
        def _(dve):
            dve.wait_ge(rms.sem, 1)
            for t in range(NT):
                nc.vector.tensor_scalar(xn[:, t, :], c.x[:, t, :], rstd[:, t:t + 1], None,
                                        ALU.mult).then_inc(scaled.sem, 1)
            for k in range(1, KT, 2):
                dve.wait_ge(turned.sem, k + 1)
                nc.vector.tensor_scalar(hT[:, k, :], c.bank[k][:, 0:S],
                                        c.cols[:, gain_col + k:gain_col + k + 1], None, ALU.mult)

        @block.tensor
        def _(pe):
            pe.wait_ge(scaled.sem, NT)
            for k in range(KT):
                for t in range(NT):
                    last = nc.tensor.transpose(c.bank[k][:, t * P:(t + 1) * P],
                                               xn[:, t, k * P:(k + 1) * P], c.ident)
                last.then_inc(turned.sem, 1)


def mix(c, dve_nc, dst, hT, dx, mu_col, n):
    for k in range(KT):
        col = mu_col + n * KT + k
        last = dve_nc.scalar_tensor_tensor(dst[:, k, :], dx[:, k, :], c.cols[:, col:col + 1],
                                           hT[:, k, :], ALU.mult, ALU.add)
    return last


def lora_stage(c, mu_col):
    nc = c.nc
    hT, dx = feature_view(c.work[:, 4:6, :]), feature_view(c.work[:, 6:8, :])
    xa, xb = feature_view(c.work[:, 0:2, :]), feature_view(c.work[:, 2:4, :])
    flat = c.work[:, :, :].rearrange("p a n -> p (a n)")
    first = flat[:, 8 * UNIT:8 * UNIT + 2304]
    w1 = first[:, 0:512].rearrange("p (k n) -> p k n", k=KT)
    a1 = first[:, 512:1024].rearrange("p (k n) -> p k n", k=KT)
    g1 = first[:, 1024:2304].rearrange("p (k n) -> p k n", k=KT)
    second = c.work[:, 11:14, :]
    tT, aT, gT = (c.work[:, 10, i * S:(i + 1) * S] for i in (1, 2, 3))
    names = ("w1_in", "w2_in", "ones", "dx", "mixed", "split_r", "low", "low_act", "wide", "wide_out", "masks_in")
    s = {n: c.new_signal("lora_" + n).sem for n in names}

    with nc.Block() as block:
        @block.sync
        def _(sp):
            sp.dma_start(first, c.dram["lora1"][:, :]).then_inc(s["w1_in"], 16)
            sp.dma_start(second, c.dram["lora2"][:, :, :]).then_inc(s["w2_in"], 16)
            sp.dma_start(c.const[:, R_STRICT:R_STRICT + 2 * P], c.dram["rmask"][:, 0:2 * P]).then_inc(
                s["masks_in"], 16)
            sp.wait_ge(s["masks_in"], 16)

        @block.gpsimd
        def _(pool):
            nc.gpsimd.memset(c.work[64:65, 10, S:3 * S], 1.0).then_inc(s["ones"], 1)

        @block.vector
        def _(dve):
            last = nc.vector.tensor_tensor(dx[:, :, 1:S], hT[:, :, 0:S - 1], hT[:, :, 1:S], ALU.subtract)
            last = nc.vector.tensor_scalar(dx[:, :, 0:1], hT[:, :, 0:1], -1.0, None, ALU.mult)
            c.dve_order.link(dve, last)
            mix(c, nc.vector, xa, hT, dx, mu_col, 3).then_inc(s["mixed"], 1)
            mix(c, nc.vector, xb, hT, dx, mu_col, 4).then_inc(s["mixed"], 1)
            dve.wait_ge(s["low"], 1)
            mix(c, nc.vector, xa, hT, dx, mu_col, 5).then_inc(s["mixed"], 1)
            dve.wait_ge(s["low"], 2)
            mix(c, nc.vector, xb, hT, dx, mu_col, 0).then_inc(s["mixed"], 1)
            dve.wait_ge(s["split_r"], 1)
            nc.vector.tensor_tensor(c.act_lo[:, 0:KT, :], xb, c.act_hi[:, 0:KT, :].bitcast(F32),
                                    ALU.subtract)
            dve.wait_ge(s["wide"], 3)
            for q in range(4):
                nc.vector.tensor_copy(c.work[:, 18 + q // 2, (q % 2) * HALF:(q % 2 + 1) * HALF],
                                      c.bank[4 + q][:, :])

        @block.tensor
        def _(pe):
            pe.wait_ge(s["w1_in"], 16)
            for i, (w, x, n0, rows, bank) in enumerate((
                    (w1, xa, 0, slice(0, 64), c.bank[0]), (a1, xb, 0, slice(0, 64), c.bank[1]),
                    (g1, xa, 0, slice(0, 128), c.bank[2]), (g1, xa, 128, slice(96, 128), c.bank[3]))):
                pe.wait_ge(s["mixed"], min(i, 2) + 1)
                width = rows.stop - rows.start
                for k in range(KT):
                    last = nc.tensor.matmul(bank[rows, 0:S], w[:, k, n0:n0 + width], x[:, k, :],
                                            start=k == 0, stop=k == KT - 1)
                last.then_inc(s["low"], 1)
            pe.wait_ge(s["w2_in"], 16)
            pe.wait_ge(s["ones"], 1)
            for i in range(3):
                pe.wait_ge(s["low_act"], (1, 4, 4)[i])
                if i == 2:
                    pe.wait_ge(s["wide_out"], 1)
                for t in range(NT):
                    tok = slice(t * P, (t + 1) * P)
                    for h in range(2):
                        w = slice(h * HALF, (h + 1) * HALF)
                        bank = c.bank[(4, 0, 4)[i] + 2 * t + h]
                        if i < 2:
                            last = nc.tensor.matmul(bank[:, :], (tT, aT)[i][0:65, tok], second[0:65, i, w],
                                                    start=True, stop=True)
                        else:
                            nc.tensor.matmul(bank[:, :], gT[:, tok], second[:, 2, w], start=True, stop=False)
                            last = nc.tensor.matmul(bank[:, :], tT[96:128, tok], second[96:128, 0, w],
                                                    start=False, stop=True, tile_position=(96, 0))
                last.then_inc(s["wide"], 1)

        @block.scalar
        def _(act):
            for i, (f, dst, rows) in enumerate(((ACT.Tanh, tT, slice(0, 64)), (ACT.Copy, aT, slice(0, 64)),
                                                (ACT.Sigmoid, gT, slice(0, 128)),
                                                (ACT.Sigmoid, tT, slice(96, 128)))):
                act.wait_ge(s["low"], i + 1)
                nc.scalar.activation(dst[rows, :], c.bank[i][rows, 0:S], f).then_inc(s["low_act"], 1)
            act.wait_ge(s["mixed"], 4)
            nc.scalar.activation(c.act_hi[:, 0:KT, :], xb, ACT.Copy).then_inc(s["split_r"], 1)
            for i in range(2):
                act.wait_ge(s["wide"], i + 1)
                for q in range(4):
                    last = nc.scalar.activation(
                        c.work[:, (14, 16)[i] + q // 2, (q % 2) * HALF:(q % 2 + 1) * HALF],
                        c.bank[(4, 0)[i] + q][:, :], ACT.Sigmoid)
                last.then_inc(s["wide_out"], 1)


def rkv_stage(c, mu_col):
    nc = c.nc
    hT, dx = feature_view(c.work[:, 4:6, :]), feature_view(c.work[:, 6:8, :])
    xa, xb = feature_view(c.work[:, 0:2, :]), feature_view(c.work[:, 2:4, :])
    mixed, high, low, read, saved = (c.new_signal("rkv_" + n) for n in ("mixed", "high", "low", "read", "saved"))
    count = 24
    with nc.Block() as block:
        @block.sync
        def _(sp):
            sp.dma_start(c.dram["g_park"][:, :, :], c.work[:, 18:20, :]).then_inc(saved.sem, 16)
            c.stream_stage_loads(sp, count)
            sp.wait_ge(saved.sem, 16)

        @block.scalar
        def _(act):
            act.wait_ge(mixed.sem, 1)
            nc.scalar.activation(c.act_hi[:, KT:2 * KT, :], xa, ACT.Copy).then_inc(high.sem, 1)
            for m in range(count + 1):
                if m < count:
                    c.split_hi(act, c.first_unit + AHEAD + m)
                if m in (4, 8, 12, 16, 20, 24):
                    e = m // 4 - 1
                    i, h = e // 2, e % 2
                    unit_done(c, act, m - 1)
                    for t in range(NT):
                        last = nc.scalar.activation(c.work[:, 8 + 2 * i + t, h * HALF:(h + 1) * HALF],
                                                    c.bank[(0, 4, 0)[i] + 2 * t + h][:, :], ACT.Copy)
                    last.then_inc(read.sem, 1)
                if m == 8:
                    act.wait_ge(mixed.sem, 2)
                    nc.scalar.activation(c.act_hi[:, 0:KT, :], xb, ACT.Copy).then_inc(high.sem, 1)

        @block.vector
        def _(dve):
            mix(c, nc.vector, xa, hT, dx, mu_col, 1).then_inc(mixed.sem, 1)
            mix(c, nc.vector, xb, hT, dx, mu_col, 2).then_inc(mixed.sem, 1)
            dve.wait_ge(high.sem, 1)
            nc.vector.tensor_tensor(c.act_lo[:, KT:2 * KT, :], xa, c.act_hi[:, KT:2 * KT, :].bitcast(F32),
                                    ALU.subtract).then_inc(low.sem, 1)
            for m in range(count):
                c.split_lo(dve, c.first_unit + AHEAD + m)
                if m == 8:
                    dve.wait_ge(high.sem, 2)
                    nc.vector.tensor_tensor(c.act_lo[:, 0:KT, :], xb, c.act_hi[:, 0:KT, :].bitcast(F32),
                                            ALU.subtract).then_inc(low.sem, 1)

        @block.tensor
        def _(pe):
            for i in range(3):
                if i:
                    pe.wait_ge(low.sem, i)
                for h in range(2):
                    if i == 2:
                        pe.wait_ge(read.sem, h + 1)
                    for k in range(4):
                        product_a(c, pe, 8 * i + 4 * h + k, k, 4,
                                  [c.bank[(0, 4, 0)[i] + h], c.bank[(0, 4, 0)[i] + 2 + h]],
                                  (0, KT, 0)[i])
    c.end_stage(count)


def token_stage(c):
    nc = c.nc
    r, k, v, sig, a = (c.work[:, i:i + 2, :] for i in (8, 10, 12, 14, 16))
    kk, tmp, wexc, winv = (c.work[:, i:i + 2, :] for i in (3, 5, 0, 18))
    kk_row, ka_row, rk_row = (c.work[:, i:i + 1, :].to_broadcast([P, NT, D]) for i in (0, 1, 2))
    ss, rinv = c.small[:, 0:32], c.small[:, 32:64]
    bonus, wc = c.small[:, 64:96], c.small[:, 96:128]
    incl, strict = c.const[:, R_INCL:R_INCL + P], c.const[:, R_STRICT:R_STRICT + P]
    half = c.const[:, 128:160]
    names = ("kk_row_in", "rows", "kk_raw", "kk_squared", "ss", "rinv", "cum", "cum_ex", "wc_bank", "w_exc", "w_inv", "free_01", "free_inc")
    s = {n: c.new_signal("token_" + n).sem for n in names}
    order = c.dve_order

    def grouped(u):
        return u.rearrange("p t (h n) -> p (t h) n", n=HD)

    def quad(u, q):
        return u[:, q // 2, (q % 2) * HALF:(q % 2 + 1) * HALF]

    with nc.Block() as block:
        @block.sync
        def _(sp):
            sp.dma_start(c.work[:, 0, :], c.dram["rrows"][0, :, :]).then_inc(s["kk_row_in"], 16)
            for i in range(1, 3):
                sp.dma_start(c.work[:, i, :], c.dram["rrows"][i, :, :]).then_inc(s["rows"], 16)

        @block.tensor
        def _(pe):
            for q in range(4):
                last = nc.tensor.matmul(c.bank[q][:, :], incl, quad(sig, q), start=True, stop=True)
            last.then_inc(s["cum"], 1)
            for q in range(4):
                last = nc.tensor.matmul(c.bank[4 + q][:, :], strict, quad(sig, q), start=True, stop=True)
            last.then_inc(s["cum_ex"], 1)
            pe.wait_ge(s["free_inc"], 1)
            for p in range(PAIRS):
                for t in range(NT):
                    last = nc.tensor.matmul(c.bank[0][:, 4 * p + 2 * t:4 * p + 2 * t + 2],
                                            sig[:, t, p * P:(p + 1) * P], incl[:, CHUNK - 1:P:CHUNK],
                                            start=True, stop=True)
            last.then_inc(s["wc_bank"], 1)

        @block.scalar
        def _(act):
            act.wait_ge(s["kk_raw"], 1)
            nc.scalar.activation(tmp, kk, ACT.Square).then_inc(s["kk_squared"], 1)
            act.wait_ge(s["cum"], 1)
            for q in range(4):
                last = nc.scalar.activation(quad(winv, q), c.bank[q][:, :], ACT.Exp, scale=-EXP_SCALE)
            last.then_inc(s["w_inv"], 1)
            act.wait_ge(s["free_01"], 1)
            act.wait_ge(s["cum_ex"], 1)
            for q in range(4):
                last = nc.scalar.activation(quad(wexc, q), c.bank[4 + q][:, :], ACT.Exp, scale=EXP_SCALE)
            last.then_inc(s["w_exc"], 1)
            act.wait_ge(s["w_exc"], 1)
            for q in range(1, 5):
                b = q % 4
                last = nc.scalar.activation(c.bank[4 + b][:, :], c.bank[b][:, :], ACT.Exp, scale=EXP_SCALE)
            last.then_inc(s["free_inc"], 1)
            act.wait_ge(s["wc_bank"], 1)
            nc.scalar.activation(wc, c.bank[0][:, 0:32], ACT.Exp, scale=EXP_SCALE)

        @block.gpsimd
        def _(pool):
            pool.wait_ge(s["ss"], 1)
            nc.gpsimd.tensor_tensor(rinv, ss, half, ALU.pow).then_inc(s["rinv"], 1)

        @block.vector
        def _(dve):
            dve.wait_ge(s["kk_row_in"], 16)
            nc.vector.tensor_tensor(kk, k, kk_row, ALU.mult).then_inc(s["kk_raw"], 1)
            dve.wait_ge(s["kk_squared"], 1)
            order.link(dve, nc.vector.tensor_reduce(ss, grouped(tmp), AX.X, ALU.add))
            nc.vector.tensor_scalar(ss, ss, 1e-24, None, ALU.max).then_inc(s["ss"], 1)
            dve.wait_ge(s["rows"], 32)
            order.link(dve, nc.vector.scalar_tensor_tensor(tmp, a, -1.0, ka_row, ALU.add, ALU.mult))
            order.link(dve, nc.vector.scalar_tensor_tensor(k, tmp, 1.0, k, ALU.add, ALU.mult))
            order.link(dve, nc.vector.tensor_tensor(tmp, r, k, ALU.mult))
            order.link(dve, nc.vector.tensor_tensor(tmp, tmp, rk_row, ALU.mult))
            nc.vector.tensor_reduce(bonus, grouped(tmp), AX.X, ALU.add)
            dve.wait_ge(s["rinv"], 1)
            order.link(dve, nc.vector.tensor_tensor(grouped(kk), grouped(kk),
                                                    rinv.unsqueeze(2).to_broadcast([P, 32, HD]), ALU.mult))
            ins = nc.vector.tensor_tensor(a, kk, a, ALU.mult)
            ins.then_inc(s["free_01"], 1)
            dve.wait_ge(s["w_inv"], 1)
            nc.vector.tensor_tensor(k, k, winv, ALU.mult)
            dve.wait_ge(s["free_01"], 1)
            nc.vector.tensor_tensor(a, a, winv, ALU.mult)
            dve.wait_ge(s["w_exc"], 1)
            nc.vector.scalar_tensor_tensor(kk, kk, -1.0, wexc, ALU.mult, ALU.mult)
            dve.wait_ge(s["free_inc"], 1)
            for q in range(4):
                nc.vector.tensor_tensor(quad(r, q), quad(r, q), c.bank[4 + q][:, :], ALU.mult)


class Recurrence:

    def __init__(self, c, t):
        w = c.work
        self.r, self.a = (w[:, i + t, :] for i in (8, 3))
        self.y = self.r
        parked = c.act_hi[:, :, :].bitcast(F32).rearrange("p (a b) s -> p a (b s)", b=4)
        self.parked_b, self.parked_k = parked[:, 0:2, :], parked[:, 2:4, :]
        parked = c.act_lo[:, :, :].bitcast(F32).rearrange("p (a b) s -> p a (b s)", b=4)
        self.parked_x, self.parked_v = parked[:, 0:2, :], parked[:, 2:4, :]
        self.b, self.k, self.v = (u[:, t, :] for u in (self.parked_b, self.parked_k, self.parked_v))
        self.rT, self.aT, self.bT, self.kT = (
            w[:, i, :].rearrange("p (h s) -> p h s", h=PAIRS) for i in (0, 1, 2, 5))
        self.rb = w[:, 14, :].rearrange("p (g n) -> p g n", g=4)
        self.base = w[:, 6, :]
        self.sa = w[:, 18, :]
        masks = w[:, 7, 0:10 * CHUNK]
        self.up_low = masks[:, 0:2 * CHUNK]
        self.strict_incl = masks[:, 2 * CHUNK:4 * CHUNK]
        self.ident = masks[:, 4 * CHUNK:5 * CHUNK]
        self.levels = masks[:, 5 * CHUNK:10 * CHUNK]
        self.state = w[:, 19, 0:HALF]
        self.solver = [Solver(u) for u in (w[:, 10:12, :], w[:, 16:18, :], w[:, 12:14, :], c.x)]

    def heads(self, unit, e, half):
        return unit.rearrange("p (q e n) -> p q e n", e=2, n=HD)[:, 4 * half:4 * half + 4, e, :]


class Solver:

    def __init__(self, units):
        def part(unit, i, n=1):
            return units[:, unit, i * S:(i + n) * S]

        self.m, self.t = part(0, 0), part(0, 1)
        self.mt = part(0, 0, 2)
        self.ak, self.rk = part(0, 2), part(0, 3)
        self.akrk = part(0, 2, 2)
        self.low, self.low_part, self.p1, self.kv = (part(1, i) for i in range(4))


def turn_stage(c, t):
    nc = c.nc
    R = Recurrence(c, t)
    turned = c.signals("turn_", {"turned": 8})["turned"]
    masks_in, parked = (c.new_signal("turn_" + n) for n in ("masks_in", "parked")) if t == 0 else (None, None)
    b, k = (c.work[:, 16, :], c.work[:, 10, :]) if t == 0 else (R.b, R.k)
    jobs = [(src, dst, half) for src, dst in ((b, R.bT), (R.a, R.aT), (k, R.kT), (R.r, R.rT))
            for half in range(2)]

    def evacuate(eng, copy, mine):
        for i, (src, dst, half) in enumerate(jobs):
            if i % 2 == mine:
                eng.wait_ge(turned.sem, turned.at(i + 1))
                copy(dst[:, 4 * half:4 * half + 4, :], c.bank[i][:, :].rearrange("p (h s) -> p h s", h=4))

    with nc.Block() as block:
        @block.sync
        def _(sp):
            if t == 0:
                sp.dma_start(c.work[:, 7, 0:10 * CHUNK], c.dram["rmask"][:, 2 * P:7 * P]).then_inc(masks_in.sem, 16)
                sp.dma_start(R.parked_b, c.work[:, 16:18, :]).then_inc(parked.sem, 16)
                sp.dma_start(R.parked_k, c.work[:, 10:12, :]).then_inc(parked.sem, 16)
                sp.dma_start(R.parked_v, c.work[:, 12:14, :]).then_inc(parked.sem, 16)
                sp.dma_start(R.parked_x, c.x[:, :, :]).then_inc(parked.sem, 16)
                sp.wait_ge(masks_in.sem, 16)
                sp.wait_ge(parked.sem, 64)

        @block.tensor
        def _(pe):
            for i, (src, dst, half) in enumerate(jobs):
                for p in range(4):
                    f = (4 * half + p) * P
                    last = nc.tensor.transpose(c.bank[i][:, p * P:(p + 1) * P], src[:, f:f + P], c.ident)
                last.then_inc(turned.sem, 1)

        @block.scalar
        def _(act):
            evacuate(act, lambda o, i: nc.scalar.activation(o, i, ACT.Copy), 0)

        @block.vector
        def _(dve):
            if t == 0:
                nc.vector.memset(R.state, 0.0)
            evacuate(dve, nc.vector.tensor_copy, 1)
    turned.base += len(jobs)


def solve_stage(c, t):
    nc = c.nc
    R = Recurrence(c, t)
    LEVELS = 5
    GROUPS = [(e, half) for half in range(2) for e in range(2)]
    N = len(GROUPS)
    counts = {"ab_bank": 2, "k_bank": 2, "init_masked": N, "init_made": N, "akrk_made": N,
              "low_copied": N, "kv_bank": N, "rb_bank": N, "rb_made": N, "kv_made": N,
              "lows": N * LEVELS, "p1_bank": N * LEVELS, "p1_made": N * LEVELS,
              "mt_bank": N * LEVELS, "mt_made": N * LEVELS, "final": 2}
    s = c.signals("solve_", counts)
    chunks = [slice(CHUNK * ch, CHUNK * (ch + 1)) for ch in range(2)]

    def four(u):
        return u.rearrange("p (h n) -> p h n", n=CHUNK)

    def over4(mask):
        return mask.unsqueeze(1).to_broadcast([P, 4, CHUNK])

    def two_fours(u):
        return u.rearrange("p (m h n) -> p m h n", m=2, n=CHUNK)

    def two_over4(masks):
        return masks.rearrange("p (m n) -> p m n", m=2).unsqueeze(2).to_broadcast([P, 2, 4, CHUNK])

    def col(q, part=0):
        return slice(part * S + q * CHUNK, part * S + (q + 1) * CHUNK)

    def joined(out, part, stat, mov):
        for q in range(4):
            for tok in chunks:
                last = nc.tensor.matmul(out[tok, col(q, part)], stat[tok, col(q)], mov[tok, col(q)],
                                        start=True, stop=True)
        return last

    with nc.Block() as block:
        @block.tensor
        def _(pe):
            def grams(half, bank_of, part, stat, mov):
                for q in range(4):
                    p = 4 * half + q
                    for e in range(2):
                        rows = slice(HD * e, HD * (e + 1))
                        for tok in chunks:
                            last = nc.tensor.matmul(bank_of(2 * half + e)[tok, col(q, part)],
                                                    stat[rows, p, tok], mov[rows, p, tok],
                                                    start=True, stop=True)
                return last

            for half in range(2):
                grams(half, lambda g: c.bank[2 * g], 0, R.bT, R.aT)
                grams(half, lambda g: c.bank[2 * g], 1, R.aT, R.bT).then_inc(s["ab_bank"].sem, 1)
                grams(half, lambda g: c.bank[2 * g + 1], 0, R.kT, R.aT)
                grams(half, lambda g: c.bank[2 * g + 1], 1, R.kT, R.rT).then_inc(s["k_bank"].sem, 1)
            for g, (e, half) in enumerate(GROUPS):
                X = R.solver[g]
                rows = slice(HD * e, HD * (e + 1))
                pe.wait_ge(s["akrk_made"].sem, s["akrk_made"].at(g + 1))
                for part, m in enumerate((X.ak, X.rk)):
                    for q in range(4):
                        h = 2 * (4 * half + q) + e
                        for tok in chunks:
                            last = nc.tensor.matmul(c.bank[2 * g + 1][tok, col(q, part)], m[tok, col(q)],
                                                    R.v[tok, h * HD:(h + 1) * HD], start=True, stop=True)
                last.then_inc(s["kv_bank"].sem, 1)
                pe.wait_ge(s["low_copied"].sem, s["low_copied"].at(g + 1))
                for q in range(4):
                    p = 4 * half + q
                    for tok in chunks:
                        last = nc.tensor.matmul(c.bank[2 * g][tok, col(q)], R.bT[rows, p, tok],
                                                R.rT[rows, p, tok], start=True, stop=True)
                last.then_inc(s["rb_bank"].sem, 1)
            for level in range(LEVELS):
                for g in range(N):
                    step, X = level * N + g, R.solver[g]
                    pe.wait_ge(s["lows"].sem, s["lows"].at(step + 1))
                    if level:
                        pe.wait_ge(s["mt_made"].sem, s["mt_made"].at(step - N + 1))
                    else:
                        pe.wait_ge(s["init_made"].sem, s["init_made"].at(g + 1))
                        pe.wait_ge(s["rb_made"].sem, s["rb_made"].at(g + 1))
                    joined(c.bank[2 * g], 0, X.low_part, X.m).then_inc(s["p1_bank"].sem, 1)
                for g in range(N):
                    step, X = level * N + g, R.solver[g]
                    pe.wait_ge(s["p1_made"].sem, s["p1_made"].at(step + 1))
                    if level == 0:
                        pe.wait_ge(s["kv_made"].sem, s["kv_made"].at(g + 1))
                    last = joined(c.bank[2 * g + 1], 0, X.t, X.p1)
                    if level < LEVELS - 1:
                        last = joined(c.bank[2 * g + 1], 1, X.p1, X.t)
                    last.then_inc(s["mt_bank"].sem, 1)
            for half in range(2):
                pe.wait_ge(s["mt_made"].sem, s["mt_made"].at((LEVELS - 1) * N + 2 * half + 2))
                for q in range(4):
                    for e in range(2):
                        h = 2 * (4 * half + q) + e
                        for ch, tok in enumerate(chunks):
                            nc.tensor.matmul(c.bank[4 * half + 2 * ch][HD * e:HD * (e + 1), col(q)],
                                             R.a[tok, h * HD:(h + 1) * HD],
                                             R.solver[2 * half + e].m[tok, col(q)], start=True, stop=True)
                for e in range(2):
                    X = R.solver[2 * half + e]
                    last = joined(c.bank[4 * half + 2 * e + 1], 0, X.m, X.kv)
                last.then_inc(s["final"].sem, 1)

        @block.scalar
        def _(act):
            for g in range(N):
                act.wait_ge(s["init_masked"].sem, s["init_masked"].at(g + 1))
                nc.scalar.activation(R.solver[g].low, c.bank[2 * g][:, S:2 * S], ACT.Copy).then_inc(
                    s["low_copied"].sem, 1)
            for g, (e, half) in enumerate(GROUPS):
                act.wait_ge(s["kv_bank"].sem, s["kv_bank"].at(g + 1))
                nc.scalar.activation(R.solver[g].kv, c.bank[2 * g + 1][:, 0:S], ACT.Copy)
                nc.scalar.activation(R.heads(R.y, e, half), four(c.bank[2 * g + 1][:, S:2 * S]),
                                     ACT.Copy).then_inc(s["kv_made"].sem, 1)
            for step in range(N * LEVELS):
                g = step % N
                act.wait_ge(s["p1_bank"].sem, s["p1_bank"].at(step + 1))
                if step >= N:
                    act.wait_ge(s["mt_bank"].sem, s["mt_bank"].at(step - N + 1))
                nc.scalar.activation(R.solver[g].p1, c.bank[2 * g][:, 0:S], ACT.Copy).then_inc(
                    s["p1_made"].sem, 1)
            for half in range(2):
                act.wait_ge(s["final"].sem, s["final"].at(half + 1))
                for ch, tok in enumerate(chunks):
                    nc.scalar.activation(R.aT[:, 4 * half:4 * half + 4, tok],
                                         four(c.bank[4 * half + 2 * ch][:, 0:S]), ACT.Copy)
                for e in range(2):
                    nc.scalar.activation(R.heads(R.base, e, half),
                                         four(c.bank[4 * half + 2 * e + 1][:, 0:S]), ACT.Copy)

        @block.gpsimd
        def _(pool):
            for step in range(N * LEVELS):
                level, g = step // N, step % N
                if level:
                    pool.wait_ge(s["p1_bank"].sem, s["p1_bank"].at(step - N + 1))
                else:
                    pool.wait_ge(s["low_copied"].sem, s["low_copied"].at(g + 1))
                nc.gpsimd.tensor_tensor(four(R.solver[g].low_part), four(R.solver[g].low),
                                        over4(R.levels[:, level * CHUNK:(level + 1) * CHUNK]),
                                        ALU.mult).then_inc(s["lows"].sem, 1)

        @block.vector
        def _(dve):
            for half in range(2):
                pair = (2 * half, 2 * half + 1)
                dve.wait_ge(s["ab_bank"].sem, s["ab_bank"].at(half + 1))
                for g in pair:
                    nc.vector.tensor_tensor(two_fours(R.solver[g].mt), two_fours(c.bank[2 * g][:, :]),
                                            two_over4(R.up_low), ALU.mult).then_inc(s["init_masked"].sem, 1)
                dve.wait_ge(s["k_bank"].sem, s["k_bank"].at(half + 1))
                for g in pair:
                    nc.vector.tensor_tensor(two_fours(R.solver[g].akrk), two_fours(c.bank[2 * g + 1][:, :]),
                                            two_over4(R.strict_incl), ALU.mult).then_inc(
                                                s["akrk_made"].sem, 1)
                for g in pair:
                    dve.wait_ge(s["init_masked"].sem, s["init_masked"].at(g + 1))
                    nc.vector.tensor_tensor(four(R.solver[g].mt), four(R.solver[g].mt),
                                            R.ident.unsqueeze(1).to_broadcast([P, 8, CHUNK]),
                                            ALU.add).then_inc(s["init_made"].sem, 1)
            for g in range(N):
                dve.wait_ge(s["rb_bank"].sem, s["rb_bank"].at(g + 1))
                nc.vector.tensor_tensor(four(R.rb[:, g, :]), four(c.bank[2 * g][:, 0:S]),
                                        over4(R.strict_incl[:, CHUNK:2 * CHUNK]), ALU.mult).then_inc(
                                            s["rb_made"].sem, 1)
            for step in range(N * LEVELS):
                X, bank = R.solver[step % N], c.bank[2 * (step % N) + 1]
                dve.wait_ge(s["mt_bank"].sem, s["mt_bank"].at(step + 1))
                new, part = (X.mt, bank[:, :]) if step < N * (LEVELS - 1) else (X.m, bank[:, 0:S])
                nc.vector.tensor_tensor(new, new, part, ALU.add).then_inc(s["mt_made"].sem, 1)
    c.end_signals(s, counts)


def step_stage(c, t):
    nc = c.nc
    R = Recurrence(c, t)
    counts = {"sa_bank": 2, "sa_made": 4, "y_bank": 2, "state_bank": 2, "state_made": 2,
              "rb_bank": 1}
    s = c.signals("step_", counts)
    order = c.dve_order

    def parity(u, e):
        return u.rearrange("p (q e n) -> p q e n", e=2, n=HD)[:, :, e, :]

    def pairs(u):
        return u.rearrange("p (q n) -> p q n", n=HD)

    with nc.Block() as block:
        @block.tensor
        def _(pe):
            for ch in range(2):
                tok = slice(CHUNK * ch, CHUNK * (ch + 1))
                if ch:
                    pe.wait_ge(s["state_made"].sem, s["state_made"].at(1))
                for first, left, done in ((0, R.aT, "sa_bank"), (2, R.rT, "y_bank")):
                    for p in range(PAIRS):
                        for e in range(2):
                            rows = slice(HD * e, HD * (e + 1))
                            last = nc.tensor.matmul(c.bank[first + e][tok, p * HD:(p + 1) * HD],
                                                    left[rows, p, tok], R.state[rows, p * HD:(p + 1) * HD],
                                                    start=True, stop=True)
                    last.then_inc(s[done].sem, 1)
                pe.wait_ge(s["sa_made"].sem, s["sa_made"].at(2 * (ch + 1)))
                for p in range(PAIRS):
                    for e in range(2):
                        rows = slice(HD * e, HD * (e + 1))
                        h = 2 * p + e
                        cols = slice(h * HD, (h + 1) * HD)
                        out = c.bank[4][rows, p * HD:(p + 1) * HD]
                        nc.tensor.matmul(out, R.b[tok, cols], R.sa[tok, cols], start=True, stop=False)
                        last = nc.tensor.matmul(out, R.k[tok, cols], R.v[tok, cols], start=False, stop=True)
                last.then_inc(s["state_bank"].sem, 1)
            for e in range(2):
                for p in range(PAIRS):
                    h = 2 * p + e
                    for ch in range(2):
                        tok = slice(CHUNK * ch, CHUNK * (ch + 1))
                        last = nc.tensor.matmul(c.bank[5 + e][tok, p * HD:(p + 1) * HD],
                                                R.rb[tok, 2 * (p // 4) + e, (p % 4) * HD:(p % 4 + 1) * HD],
                                                R.sa[tok, h * HD:(h + 1) * HD], start=True, stop=True)
            last.then_inc(s["rb_bank"].sem, 1)

        @block.vector
        def _(dve):
            for ch in range(2):
                tok = slice(CHUNK * ch, CHUNK * (ch + 1))
                dve.wait_ge(s["sa_bank"].sem, s["sa_bank"].at(ch + 1))
                for e in range(2):
                    nc.vector.tensor_tensor(parity(R.sa, e)[tok], pairs(c.bank[e][:, :])[tok],
                                            parity(R.base, e)[tok], ALU.add).then_inc(s["sa_made"].sem, 1)
                dve.wait_ge(s["y_bank"].sem, s["y_bank"].at(ch + 1))
                for e in range(2):
                    last = nc.vector.tensor_tensor(parity(R.y, e)[tok], pairs(c.bank[2 + e][:, :])[tok],
                                                   parity(R.y, e)[tok], ALU.add)
                order.link(dve, last)
                dve.wait_ge(s["state_bank"].sem, s["state_bank"].at(ch + 1))
                order.link(dve, nc.vector.tensor_tensor(R.state, R.state, c.bank[4][:, :], ALU.add))
                at = 96 + 2 * t + ch
                decay = c.small[:, at:at + 4 * PAIRS - 3:4].unsqueeze(2).to_broadcast([P, PAIRS, HD])
                nc.vector.tensor_tensor(pairs(R.state), pairs(R.state), decay, ALU.mult).then_inc(s["state_made"].sem, 1)
            dve.wait_ge(s["rb_bank"].sem, s["rb_bank"].at(1))
            for e in range(2):
                nc.vector.tensor_tensor(parity(R.y, e), pairs(c.bank[5 + e][:, :]), parity(R.y, e), ALU.add)
    c.end_signals(s, counts)


def head_out_stage(c):
    nc = c.nc
    y, sq, vb, gate = (c.work[:, i:i + 2, :] for i in (8, 14, 16, 0))
    R = Recurrence(c, 0)
    v = R.parked_v
    ln0, ln1 = (c.work[:, i:i + 1, :].to_broadcast([P, NT, D]) for i in (2, 5))
    total, mean, var, rstd = (c.small[:, i:i + 32] for i in (0, 32, 128, 160))
    bonus = c.small[:, 64:96]
    half = c.const[:, 128:160]
    names = ("back", "centred", "squared", "var", "rstd", "y", "turned", "high")
    s = {n: c.new_signal("headout_" + n).sem for n in names}
    order = c.dve_order

    def grouped(u):
        return u.rearrange("p t (h n) -> p (t h) n", n=HD)

    def over_head(u):
        return u.unsqueeze(2).to_broadcast([P, NT * HEADS, HD])

    with nc.Block() as block:
        @block.sync
        def _(sp):
            sp.dma_start(gate, c.dram["g_park"][:, :, :]).then_inc(s["back"], 16)
            sp.dma_start(c.x[:, :, :], R.parked_x).then_inc(s["back"], 16)
            sp.dma_start(c.work[:, 2, :], c.dram["rrows"][3, :, :]).then_inc(s["back"], 16)
            sp.dma_start(c.work[:, 5, :], c.dram["rrows"][4, :, :]).then_inc(s["back"], 16)
            sp.wait_ge(s["back"], 64)

        @block.vector
        def _(dve):
            order.link(dve, nc.vector.tensor_reduce(total, grouped(y), AX.X, ALU.add))
            order.link(dve, nc.vector.tensor_scalar(mean, total, 1.0 / HD, None, ALU.mult))
            nc.vector.tensor_tensor(grouped(y), grouped(y), over_head(mean), ALU.subtract).then_inc(
                s["centred"], 1)
            order.link(dve, nc.vector.tensor_tensor(grouped(vb), grouped(v), over_head(bonus), ALU.mult))
            dve.wait_ge(s["squared"], 1)
            order.link(dve, nc.vector.tensor_reduce(var, grouped(sq), AX.X, ALU.add))
            nc.vector.tensor_scalar(var, var, 1.0 / HD, 64e-5, ALU.mult, ALU.add).then_inc(s["var"], 1)
            dve.wait_ge(s["back"], 64)
            nc.vector.tensor_tensor(vb, vb, ln1, ALU.add)
            dve.wait_ge(s["rstd"], 1)
            order.link(dve, nc.vector.tensor_tensor(grouped(y), grouped(y), over_head(rstd), ALU.mult))
            order.link(dve, nc.vector.tensor_tensor(y, y, ln0, ALU.mult))
            order.link(dve, nc.vector.tensor_tensor(y, y, vb, ALU.add))
            nc.vector.tensor_tensor(y, y, gate, ALU.mult).then_inc(s["y"], 1)
            for k in range(KT):
                dve.wait_ge(s["high"], k + 1)
                nc.vector.tensor_tensor(c.act_lo[:, k, :], c.bank[k][:, 0:S],
                                        c.act_hi[:, k, :].bitcast(F32), ALU.subtract)

        @block.gpsimd
        def _(pool):
            pool.wait_ge(s["var"], 1)
            nc.gpsimd.tensor_tensor(rstd, var, half, ALU.pow).then_inc(s["rstd"], 1)

        @block.tensor
        def _(pe):
            pe.wait_ge(s["y"], 1)
            for k in range(KT):
                for t in range(NT):
                    last = nc.tensor.transpose(c.bank[k][:, t * P:(t + 1) * P],
                                               y[:, t, k * P:(k + 1) * P], c.ident)
                last.then_inc(s["turned"], 1)

        @block.scalar
        def _(act):
            act.wait_ge(s["centred"], 1)
            nc.scalar.activation(sq, y, ACT.Square).then_inc(s["squared"], 1)
            for k in range(KT):
                act.wait_ge(s["turned"], k + 1)
                nc.scalar.activation(c.act_hi[:, k, :], c.bank[k][:, 0:S], ACT.Copy).then_inc(s["high"], 1)


def post_norm_stage(c):
    nc = c.nc
    ms, rstd = c.small[:, 0:NT], c.small[:, NT:2 * NT]
    half = c.const[:, 128:128 + NT]
    gain = c.gain_row
    with nc.Block() as block:
        @block.scalar
        def _(act):
            for t in range(NT):
                last = nc.scalar.activation(c.work[:, t, :], c.x[:, t, :], ACT.Square,
                                            scale=float(D) ** -0.5, accum_out=ms[:, t:t + 1])
            last.then_inc(c.act_to_pool.sem, 1)

        @block.gpsimd
        def _(pool):
            pool.wait_ge(c.act_to_pool.sem, c.act_to_pool.at(1))
            c.pool_order.link(pool, nc.gpsimd.tensor_scalar(ms, ms, EPS, None, ALU.add))
            nc.gpsimd.tensor_tensor(rstd, ms, half, ALU.pow).then_inc(c.pool_to_dve.sem, 1)

        @block.vector
        def _(dve):
            dve.wait_ge(c.pool_to_dve.sem, c.pool_to_dve.at(1))
            dve.wait_ge(c.row_in.sem, 16 * c.gain_loads)
            for t in range(NT):
                nc.vector.scalar_tensor_tensor(c.x[:, t, :], c.x[:, t, :], rstd[:, t:t + 1], gain,
                                               ALU.mult, ALU.mult)
    c.end_stage(0, (c.act_to_pool, 1), (c.pool_to_dve, 1))


def program(nc, dram, out, col, row):
    with ExitStack() as ctx:
        c = Core(nc, ctx, dram)
        start_stage(c)
        join = Join(c, col["ffn1_norm0"], start=True)
        for l in range(DEPTH):
            lambda_init = 0.8 - 0.6 * math.exp(-0.3 * l)
            ffn_stage(c, join)
            join = Join(c, col[f"mix_norm{l}"], 0.5, banks(c))
            mixer_in_stage(c, join, l, col[f"conv{l}"], col[f"convb{l}"])
            attention_stage(c, l, col[f"qn{l}"], col[f"kn{l}"], col[f"sub{l}"], col[f"lam{l}"],
                            col[f"ps{l}"], col[f"ln{l}"], lambda_init)
            project_stage(c, KT, KT)
            ffn_stage(c, Join(c, col[f"ffn2_norm{l}"], 1.0, banks(c)), row[f"post_norm{l}"])
            finish_stage(c, 0.5, banks(c))
            post_norm_stage(c)
            join = Join(c, col["ffn1_norm1"] if l == 0 else col["g0_0"])
        for i in range(DEPTH):
            ffn_stage(c, join, row[f"g{i}_1"])
            if i == 0:
                join = Join(c, col[f"g{i}_2"], 0.5, banks(c), normed=True)
                gmlp_in_stage(c, join, row["gmlp_bias_v0"], col["gmlp_bias_u"])
                gmlp_mix_stage(c, row["gmlp_bias_s"], col["gmlp_gain"])
                project_stage(c, 2 * KT, 0, row[f"g{i}_3"])
            else:
                finish_stage(c, 0.5, banks(c), normed=True)
                plain_norm_stage(c, col[f"g{i}_2"])
                lora_stage(c, col["mu"])
                rkv_stage(c, col["mu"])
                token_stage(c)
                for t in range(NT):
                    turn_stage(c, t)
                    solve_stage(c, t)
                    step_stage(c, t)
                head_out_stage(c)
                project_stage(c, KT, 0, row[f"g{i}_3"])
            ffn_stage(c, Join(c, col[f"g{i}_4"], 1.0, banks(c), normed=True), row[f"g{i}_5"])
            join = Join(c, col[f"g{i}_6"], 0.5, banks(c), normed=True)
            ple_stage(c, join, i, row[f"g{i}_7"])

            def ple(t, h):
                return c.work[:, t, h * HALF:(h + 1) * HALF]

            if i < DEPTH - 1:
                join = Join(c, col[f"g{i + 1}_0"], 1.0, ple, normed=True)
            else:
                finish_stage(c, 1.0, ple, normed=True)
        store_stage(c, out)


class Layout:

    def __init__(self):
        self.cols, self.col_at, self.rows, self.row_at = [], {}, [], {}

    def add_cols(self, name, array):
        self.col_at[name] = sum(a.shape[1] for a in self.cols)
        self.cols.append(array)

    def add_row(self, name, array):
        self.row_at[name] = len(self.rows)
        self.rows.append(array)


def unit_b(w, n0):
    import numpy as np
    return np.ascontiguousarray(w[:, n0:n0 + P].reshape(KT, P, P).transpose(1, 0, 2)).reshape(P, UNIT)


def unit_a(w, k, n0):
    import numpy as np
    return np.ascontiguousarray(
        w[2 * k * P:2 * (k + 1) * P, n0:n0 + HALF].reshape(2, P, HALF).transpose(1, 0, 2)).reshape(P, UNIT)


def units_ffn(gate, up, down):
    out = [unit_b(gate, 0), unit_b(up, 0)]
    for t in range(1, FT):
        out += [unit_b(gate, t * P), unit_b(up, t * P), down[(t - 1) * P:t * P, :]]
    return out + [down[(FT - 1) * P:, :]]


def units_a(w):
    return [unit_a(w, k, n0) for n0 in range(0, w.shape[1], HALF) for k in range(w.shape[0] // (2 * P))]


def mixer_vectors(L, a, l):
    import numpy as np
    L.add_cols(f"conv{l}", a["conv_dw"][l].reshape(CONV_W, 2, P).transpose(2, 0, 1).reshape(P, 2 * CONV_W))
    L.add_cols(f"convb{l}", a["conv_dw_bias"][l].reshape(2, P).T)
    L.add_cols(f"ln{l}", np.concatenate([a["conv_ln_gain"][l].reshape(2, P).T,
                                         a["conv_ln_bias"][l].reshape(2, P).T], axis=1))
    L.add_cols(f"qn{l}", np.concatenate([a["q_norm"][l]] * 2)[:, None])
    L.add_cols(f"kn{l}", np.concatenate([a["k_norm"][l]] * 2)[:, None])
    L.add_cols(f"sub{l}", a["attn_subln"][l][:, None])
    L.add_cols(f"ps{l}", a["pool_scale"][l].reshape(2, P).T)
    lam = np.concatenate([a[n][l] for n in ("lambda_q1", "lambda_k1", "lambda_q2", "lambda_k2")])
    L.add_cols(f"lam{l}", np.broadcast_to(lam, (P, 4 * HD)))


def mixer_units(a, l):
    w = a["w_in"][l]
    out = [unit_b(w, n0) for n0 in (0, 256, 128, 384, 512, 640)]
    for n0 in (768, 1280, 1792):
        out += units_a(w[:, n0:n0 + HALF])
    return out + units_a(a["w_out"][l])


def pool_weights(a):
    import numpy as np
    w = a["pool_w"]
    out = np.zeros((DEPTH, P, 2, P), w.dtype)
    for g in range(4):
        r = slice((g % 2) * 64, (g % 2 + 1) * 64)
        out[:, r, g // 2, r] = w[:, g]
    return out


def constants():
    import numpy as np
    const = np.zeros((P, 1024), np.float32)
    const[:, C_IDENT:C_IDENT + P] = np.eye(P)
    const[:, C_HALF:C_HALF + 256] = -0.5
    q = np.arange(S)
    dist = np.abs(q[:, None] - q[None, :]).reshape(NT, P, S).transpose(1, 0, 2)
    for g, w in enumerate((2, 4, 8, 16)):
        lo, hi = np.clip(q - w // 2, 0, S), np.clip(q + w // 2, 0, S)
        at = C_RCNT + (g // 2) * S
        const[(g % 2) * 64:(g % 2 + 1) * 64, at:at + S] = 1.0 / (hi - lo)
    const[:, C_MEAN:C_MEAN + P] = 1.0 / 256
    return const, np.ascontiguousarray(dist.reshape(P, 2 * S).astype(np.float32))



def rwkv_masks():
    import numpy as np
    i = np.arange(P)
    row, col = i[:, None], i[None, :]
    chunk = row // CHUNK == col // CHUNK
    own_row, own = row % CHUNK, i[None, :CHUNK]
    pair = own_row // 2 == own // 2
    out = [chunk & (row < col), chunk & (row <= col), pair & (own_row < own), pair & (own_row > own),
           own_row < own, own_row <= own, own_row == own]
    for b in (2, 4, 8, 16, 32):
        out.append((own_row // (2 * b) == own // (2 * b)) & (own_row // b > own // b))
    return np.concatenate(out, axis=1).astype(np.float32)


def lora_weights(a):
    import numpy as np

    def tiles(w):
        return w.reshape(KT, P, w.shape[1]).transpose(1, 0, 2).reshape(P, KT * w.shape[1])

    first = np.concatenate([tiles(a[n + "_2"][0]) for n in ("b_w1", "b_a1", "b_g1")], axis=1)
    second = np.zeros((P, 3, D), first.dtype)
    second[0:64, 0], second[64, 0], second[96:128, 0] = a["b_w2_2"][0], a["b_w0_2"][0], a["b_g2_2"][0][P:]
    second[0:64, 1], second[64, 1] = a["b_a2_2"][0], a["b_a0_2"][0]
    second[:, 2] = a["b_g2_2"][0][0:P]
    return np.ascontiguousarray(first), second


def rwkv_rows(a):
    import numpy as np
    rows = [a["b_k_k_2"][0], a["b_k_a_2"][0], a["b_r_k_2"][0].reshape(-1), a["b_lnx_2"][0][0], a["b_lnx_2"][0][1]]
    return np.stack([np.broadcast_to(r, (P, D)) for r in rows])


def rwkv_units(a):
    out = []
    for i in range(3):
        out += units_a(a["b_w_in_2"][0][i])
    return out + units_a(a["b_w_out_2"][0])


def kernel(**inputs):
    import numpy as np
    import concourse.bacc as bacc
    from concourse.bass_utils import run_bass_kernel_spmd as run

    a = {k: np.asarray(v) for k, v in inputs.items()}
    L = Layout()
    gains = a["norm_g_2"]
    for l in range(DEPTH):
        for n in ("ffn1_norm", "mix_norm", "ffn2_norm"):
            L.add_cols(f"{n}{l}", a[n][l].reshape(KT, P).T)
        mixer_vectors(L, a, l)
        L.add_row(f"post_norm{l}", a["post_norm"][l])
        for j in range(8):
            if j % 2:
                L.add_row(f"g{l}_{j}", gains[l, j])
            else:
                L.add_cols(f"g{l}_{j}", gains[l, j].reshape(KT, P).T)
    L.add_cols("gmlp_bias_u", a["a_b_in_2"][0][:2 * D].reshape(2 * KT, P).T)
    L.add_cols("gmlp_gain", a["a_v_gain_2"][0].reshape(2 * KT, P).T)
    L.add_cols("mu", a["b_mu_2"][0].reshape(6 * KT, P).T)
    L.add_row("gmlp_bias_v0", a["a_b_in_2"][0][2 * D:3 * D])
    L.add_row("gmlp_bias_v1", a["a_b_in_2"][0][3 * D:])
    L.add_row("gmlp_bias_s", a["a_b_s_2"][0].reshape(-1))

    def ffn2_units(i, j):
        w13 = a["ffn_w13_2"][i, j]
        return units_ffn(w13[:, :DFF], w13[:, DFF:], a["ffn_w2_2"][i, j])

    units = []
    for l in range(DEPTH):
        units += units_ffn(a["ffn1_w_gate"][l], a["ffn1_w_up"][l], a["ffn1_w_down"][l])
        units += mixer_units(a, l)
        units += units_ffn(a["ffn2_w_gate"][l], a["ffn2_w_up"][l], a["ffn2_w_down"][l])
    w_in = a["a_w_in_2"][0]
    for i in range(DEPTH):
        units += ffn2_units(i, 0)
        if i == 0:
            units += units_a(w_in[:, 2 * D:]) + [unit_b(w_in, n * P) for n in range(2 * KT)]
            units += units_a(a["a_w_out_2"][0])
        else:
            units += rwkv_units(a)
        units += ffn2_units(i, 1)
        units += units_a(a["ple_w_gate_2"][i]) + units_a(a["ple_w_proj_2"][i])

    const, dist = constants()
    lora1, lora2 = lora_weights(a)
    arrays = {
        "w": np.stack(units), "x": np.ascontiguousarray(a["x"][0]),
        "cols": np.ascontiguousarray(np.concatenate(L.cols, axis=1)),
        "rows": np.stack([np.broadcast_to(r, (P, UNIT)) for r in L.rows]),
        "const": const, "dist": dist, "rmask": rwkv_masks(), "poolw": pool_weights(a),
        "pt": np.ascontiguousarray(a["p_2"][:, 0].reshape(DEPTH, S, 2, P).transpose(0, 3, 2, 1)),
        "ws": np.ascontiguousarray(a["a_w_s_2"][0].transpose(2, 0, 1)),
        "lora1": lora1, "lora2": lora2, "rrows": rwkv_rows(a),
    }
    nc = bacc.Bacc("TRN2", target_bir_lowering=False, num_devices=1)
    dram = {k: nc.dram_tensor(k + "_dram", v.shape, F32, kind="ExternalInput").ap()
            for k, v in arrays.items()}
    for n in ("g_park",):
        dram[n] = nc.dram_tensor(n, (P, NT, D), F32, kind="Internal").ap()
    out = nc.dram_tensor("out", (S, D), F32, kind="ExternalOutput").ap()
    program(nc, dram, out, L.col_at, L.row_at)
    r = run(nc, [{k + "_dram": v for k, v in arrays.items()}], core_ids=[0])
    return r.results[0]["out"].reshape(1, S, D)
```
